# Optimizing a Trainium2 kernel written in Bass

```python
import numpy as np
import jax
import jax.numpy as jnp
from jax import lax

D_MODEL = 1024
BATCH = 1
SEQ = 512
DEPTH = 2

HEAD_DIM = 64
NSA_HEADS = 8
NSA_KV_HEADS = 2
NSA_GROUP = NSA_HEADS // NSA_KV_HEADS
SB_HEADS = 8
CMP_BLOCK = 32
CMP_STRIDE = 16
SLC_BLOCK = 64
SLC_TOPK = 16
WINDOW = 512
WIN_QBLOCK = 128
SLC_QCHUNK = 64
SB_QBLOCK = 128
D_FF = 2816
CONV_WIDTH = 3
ROPE_THETA = 10000.0
RMS_EPS = 1e-6
NEG_INF = -1e30
FORCE_BONUS = 1e4

NSA_WIDTH = NSA_HEADS * HEAD_DIM
KV_WIDTH = NSA_KV_HEADS * HEAD_DIM
SB_WIDTH = SB_HEADS * HEAD_DIM
IN_SPLITS = (NSA_WIDTH, 6 * KV_WIDTH, 3 * NSA_HEADS, 3 * SB_WIDTH, 2 * D_MODEL)
IN_WIDTH = sum(IN_SPLITS)


def rms_norm(x, gain):
    xf = x.astype(jnp.float32)
    y = xf * lax.rsqrt(jnp.mean(xf * xf, axis=-1, keepdims=True) + RMS_EPS)
    return y.astype(x.dtype) * gain

def rope(x, positions):
    half = x.shape[-1] // 2
    inv_freq = ROPE_THETA ** (-jnp.arange(half, dtype=jnp.float32) / half)
    ang = positions.astype(jnp.float32)[:, :, None] * inv_freq
    cos = jnp.cos(ang)[:, :, None, :]
    sin = jnp.sin(ang)[:, :, None, :]
    xf = x.astype(jnp.float32)
    x1, x2 = xf[..., :half], xf[..., half:]
    return jnp.concatenate([x1 * cos - x2 * sin, x2 * cos + x1 * sin], axis=-1).astype(x.dtype)

def compress_blocks(k, pe, w1, b1, w2):
    B, T, Hkv, hd = k.shape
    n_cmp = (T - CMP_BLOCK) // CMP_STRIDE + 1
    idx = np.arange(n_cmp)[:, None] * CMP_STRIDE + np.arange(CMP_BLOCK)[None, :]
    blocks = k[:, idx] + pe[None, None, :, None, :]
    flat = jnp.transpose(blocks, (0, 1, 3, 2, 4)).reshape(B, n_cmp, Hkv, CMP_BLOCK * hd)
    return jax.nn.gelu(flat @ w1 + b1, approximate=True) @ w2

def nsa_attention(q, k_cmp, v_cmp, k_slc, v_slc, k_win, v_win, gate_logits,
                  ck_pe, ck_w1, ck_b1, ck_w2, cv_pe, cv_w1, cv_b1, cv_w2):
    B, T, H, hd = q.shape
    scale = hd ** -0.5
    qg = q.reshape(B, T, NSA_KV_HEADS, NSA_GROUP, hd)
    t_idx = jnp.arange(T)

    kc = compress_blocks(k_cmp, ck_pe, ck_w1, ck_b1, ck_w2)
    vc = compress_blocks(v_cmp, cv_pe, cv_w1, cv_b1, cv_w2)
    n_cmp = kc.shape[1]
    cmp_end = jnp.arange(n_cmp) * CMP_STRIDE + CMP_BLOCK - 1
    cmp_mask = cmp_end[None, :] <= t_idx[:, None]
    s = jnp.einsum('bthgd,bnhd->bhgtn', qg, kc).astype(jnp.float32) * scale
    p_cmp = jax.nn.softmax(jnp.where(cmp_mask, s, NEG_INF), axis=-1) * cmp_mask
    o_cmp = jnp.einsum('bhgtn,bnhd->bthgd', p_cmp.astype(vc.dtype), vc)

    n_slc = T // SLC_BLOCK
    top_n = min(SLC_TOPK, n_slc)
    ci = np.arange(n_cmp)[:, None] * CMP_STRIDE
    sj = np.arange(n_slc)[None, :] * SLC_BLOCK
    overlap = ((ci < sj + SLC_BLOCK) & (sj < ci + CMP_BLOCK)).astype(np.float32)
    p_slc = jnp.einsum('bhtn,nj->bhtj', p_cmp.sum(axis=2), jnp.asarray(overlap))
    blk = jnp.arange(n_slc)
    cur = t_idx // SLC_BLOCK
    blk_valid = blk[None, :] * SLC_BLOCK <= t_idx[:, None]
    forced = (blk[None, :] == 0) | (blk[None, :] == cur[:, None]) | (blk[None, :] == cur[:, None] - 1)
    score = jnp.where(blk_valid, p_slc + jnp.where(forced, FORCE_BONUS, 0.0), -1.0)
    top_score, top_idx = lax.top_k(score, top_n)
    top_valid = top_score >= 0.0

    ks_blk = jnp.transpose(k_slc.reshape(B, n_slc, SLC_BLOCK, NSA_KV_HEADS, hd), (0, 3, 1, 2, 4))
    vs_blk = jnp.transpose(v_slc.reshape(B, n_slc, SLC_BLOCK, NSA_KV_HEADS, hd), (0, 3, 1, 2, 4))
    b_ix = jnp.arange(B)[:, None, None, None]
    h_ix = jnp.arange(NSA_KV_HEADS)[None, :, None, None]
    n_chunk = T // SLC_QCHUNK

    def slc_chunk(args):
        qc, idx_c, ok_c, t_c = args
        kg = ks_blk[b_ix, h_ix, idx_c]
        vg = vs_blk[b_ix, h_ix, idx_c]
        tok = idx_c[..., None] * SLC_BLOCK + jnp.arange(SLC_BLOCK)
        mask = ok_c[..., None] & (tok <= t_c[None, None, :, None, None])
        sc = jnp.einsum('bqhgd,bhqnld->bhgqnl', qc, kg).astype(jnp.float32) * scale
        sc = jnp.where(mask[:, :, None], sc, NEG_INF)
        p = jax.nn.softmax(sc.reshape(*sc.shape[:4], -1), axis=-1).reshape(sc.shape)
        return jnp.einsum('bhgqnl,bhqnld->bqhgd', p.astype(vg.dtype), vg)

    xs = (jnp.swapaxes(qg.reshape(B, n_chunk, SLC_QCHUNK, NSA_KV_HEADS, NSA_GROUP, hd), 0, 1),
          jnp.moveaxis(top_idx.reshape(B, NSA_KV_HEADS, n_chunk, SLC_QCHUNK, top_n), 2, 0),
          jnp.moveaxis(top_valid.reshape(B, NSA_KV_HEADS, n_chunk, SLC_QCHUNK, top_n), 2, 0),
          t_idx.reshape(n_chunk, SLC_QCHUNK))
    o_slc = jnp.swapaxes(lax.map(slc_chunk, xs), 0, 1).reshape(B, T, NSA_KV_HEADS, NSA_GROUP, hd)

    n_wblk = T // WIN_QBLOCK
    span = WINDOW + WIN_QBLOCK
    kw_pad = jnp.pad(k_win, ((0, 0), (WINDOW, 0), (0, 0), (0, 0)))
    vw_pad = jnp.pad(v_win, ((0, 0), (WINDOW, 0), (0, 0), (0, 0)))

    def win_block(i):
        start = i * WIN_QBLOCK
        qb = lax.dynamic_slice_in_dim(qg, start, WIN_QBLOCK, axis=1)
        kb = lax.dynamic_slice_in_dim(kw_pad, start, span, axis=1)
        vb = lax.dynamic_slice_in_dim(vw_pad, start, span, axis=1)
        q_pos = start + jnp.arange(WIN_QBLOCK)
        k_pos = start - WINDOW + jnp.arange(span)
        diff = q_pos[:, None] - k_pos[None, :]
        mask = (diff >= 0) & (diff < WINDOW) & (k_pos[None, :] >= 0)
        sc = jnp.einsum('bqhgd,bkhd->bhgqk', qb, kb).astype(jnp.float32) * scale
        p = jax.nn.softmax(jnp.where(mask, sc, NEG_INF), axis=-1)
        return jnp.einsum('bhgqk,bkhd->bqhgd', p.astype(vb.dtype), vb)

    o_win = jnp.swapaxes(lax.map(win_block, jnp.arange(n_wblk)), 0, 1).reshape(B, T, NSA_KV_HEADS, NSA_GROUP, hd)

    g = jax.nn.sigmoid(gate_logits.reshape(B, T, NSA_KV_HEADS, NSA_GROUP, 3))
    o = g[..., 0:1] * o_cmp + g[..., 1:2] * o_slc + g[..., 2:3] * o_win
    return o.reshape(B, T, H * hd)

def stick_breaking_attention(q, k, v):
    B, T, H, hd = q.shape
    scale = hd ** -0.5
    outs = []
    for i in range(T // SB_QBLOCK):
        q0, q1 = i * SB_QBLOCK, (i + 1) * SB_QBLOCK
        z = jnp.einsum('bqhd,bkhd->bhqk', q[:, q0:q1], k[:, :q1]).astype(jnp.float32) * scale
        q_pos = jnp.arange(q0, q1)
        k_pos = jnp.arange(q1)
        strict = k_pos[None, :] < q_pos[:, None]
        log_1m = jnp.where(strict, -jax.nn.softplus(z), 0.0)
        later = lax.cumsum(log_1m, axis=3, reverse=True) - log_1m
        w = jnp.where(strict, jnp.exp(jax.nn.log_sigmoid(z) + later), 0.0)
        outs.append(jnp.einsum('bhqk,bkhd->bqhd', w.astype(v.dtype), v[:, :q1]))
    return jnp.concatenate(outs, axis=1)

def hybrid_mixer(h, positions, w_in, ck_pe, ck_w1, ck_b1, ck_w2, cv_pe, cv_w1, cv_b1, cv_w2,
                 w_proj_nsa, w_proj_sb, w_out):
    B, T, _ = h.shape
    cuts = np.cumsum(IN_SPLITS)[:-1].tolist()
    q_nsa, kv_nsa, g_nsa, qkv_sb, g_merge = jnp.split(h @ w_in, cuts, axis=-1)
    q_nsa = rope(q_nsa.reshape(B, T, NSA_HEADS, HEAD_DIM), positions)
    kv = kv_nsa.reshape(B, T, 6, NSA_KV_HEADS, HEAD_DIM)
    k_cmp = rope(kv[:, :, 0], positions)
    v_cmp = kv[:, :, 1]
    k_slc = rope(kv[:, :, 2], positions)
    v_slc = kv[:, :, 3]
    k_win = rope(kv[:, :, 4], positions)
    v_win = kv[:, :, 5]
    o_nsa = nsa_attention(q_nsa, k_cmp, v_cmp, k_slc, v_slc, k_win, v_win, g_nsa,
                          ck_pe, ck_w1, ck_b1, ck_w2, cv_pe, cv_w1, cv_b1, cv_w2)
    qkv = qkv_sb.reshape(B, T, 3, SB_HEADS, HEAD_DIM)
    o_sb = stick_breaking_attention(qkv[:, :, 0], qkv[:, :, 1], qkv[:, :, 2]).reshape(B, T, SB_WIDTH)
    g_a, g_b = jnp.split(jax.nn.sigmoid(g_merge), 2, axis=-1)
    y = g_a * (o_nsa @ w_proj_nsa) + g_b * (o_sb @ w_proj_sb)
    return y @ w_out

def conv_ffn(h, w_up, conv_w, conv_b, w_down):
    u = h @ w_up
    c = u.shape[-1]
    u = lax.conv_general_dilated(u, conv_w[:, None, :], window_strides=(1,),
                                 padding=[(CONV_WIDTH - 1, 0)],
                                 dimension_numbers=('NWC', 'WIO', 'NWC'),
                                 feature_group_count=c) + conv_b
    gate, up = jnp.split(u, 2, axis=-1)
    return (jax.nn.gelu(gate, approximate=True) * up) @ w_down

def first_inputs(seed: int = 0) -> dict:
    key = jax.random.key(seed)
    ks = jax.random.split(key, 24)
    f32 = jnp.float32

    def nrm(k, shape, scale):
        return jax.random.normal(k, shape, f32) * scale

    def gain(k):
        return 1.0 + 0.02 * jax.random.normal(k, (DEPTH, D_MODEL), f32)

    cmp_in = CMP_BLOCK * HEAD_DIM
    return {
        'x': nrm(ks[0], (BATCH, SEQ, D_MODEL), 1.0),
        'positions': jnp.broadcast_to(jnp.arange(SEQ, dtype=jnp.int32), (BATCH, SEQ)),
        'g_pre_mix': gain(ks[1]),
        'w_in': nrm(ks[2], (DEPTH, D_MODEL, IN_WIDTH), D_MODEL ** -0.5),
        'ck_pe': nrm(ks[3], (DEPTH, CMP_BLOCK, HEAD_DIM), 0.02),
        'ck_w1': nrm(ks[4], (DEPTH, cmp_in, HEAD_DIM), cmp_in ** -0.5),
        'ck_b1': nrm(ks[5], (DEPTH, HEAD_DIM), 0.01),
        'ck_w2': nrm(ks[6], (DEPTH, HEAD_DIM, HEAD_DIM), HEAD_DIM ** -0.5),
        'cv_pe': nrm(ks[7], (DEPTH, CMP_BLOCK, HEAD_DIM), 0.02),
        'cv_w1': nrm(ks[8], (DEPTH, cmp_in, HEAD_DIM), cmp_in ** -0.5),
        'cv_b1': nrm(ks[9], (DEPTH, HEAD_DIM), 0.01),
        'cv_w2': nrm(ks[10], (DEPTH, HEAD_DIM, HEAD_DIM), HEAD_DIM ** -0.5),
        'w_proj_nsa': nrm(ks[11], (DEPTH, NSA_WIDTH, D_MODEL), NSA_WIDTH ** -0.5),
        'w_proj_sb': nrm(ks[12], (DEPTH, SB_WIDTH, D_MODEL), SB_WIDTH ** -0.5),
        'w_out': nrm(ks[13], (DEPTH, D_MODEL, D_MODEL), D_MODEL ** -0.5),
        'g_post_mix': gain(ks[14]),
        'g_pre_ffn': gain(ks[15]),
        'w_up': nrm(ks[16], (DEPTH, D_MODEL, 2 * D_FF), D_MODEL ** -0.5),
        'conv_w': nrm(ks[17], (DEPTH, CONV_WIDTH, 2 * D_FF), CONV_WIDTH ** -0.5),
        'conv_b': nrm(ks[18], (DEPTH, 2 * D_FF), 0.01),
        'w_down': nrm(ks[19], (DEPTH, D_FF, D_MODEL), D_FF ** -0.5),
        'g_post_ffn': gain(ks[20]),
    }

def first_block(x, positions, g_pre_mix, w_in, ck_pe, ck_w1, ck_b1, ck_w2, cv_pe, cv_w1, cv_b1, cv_w2,
              w_proj_nsa, w_proj_sb, w_out, g_post_mix, g_pre_ffn, w_up, conv_w, conv_b, w_down, g_post_ffn):
    for l in range(DEPTH):
        h = rms_norm(x, g_pre_mix[l])
        m = hybrid_mixer(h, positions, w_in[l], ck_pe[l], ck_w1[l], ck_b1[l], ck_w2[l],
                         cv_pe[l], cv_w1[l], cv_b1[l], cv_w2[l], w_proj_nsa[l], w_proj_sb[l], w_out[l])
        x = x + rms_norm(m, g_post_mix[l])
        h = rms_norm(x, g_pre_ffn[l])
        f = conv_ffn(h, w_up[l], conv_w[l], conv_b[l], w_down[l])
        x = x + rms_norm(f, g_post_ffn[l])
    return x


DEPTH_2 = 1

NA_HEADS = 8
NA_WIDTH = NA_HEADS * HEAD_DIM
NA_ROWS = 8
NA_COLS = 16
GRID_W = 64
DIL_PAIRS = ((128, 1), (512, 4), (2048, 16))
NB_GROUPS = len(DIL_PAIRS)
NB_HEADS_PER_GROUP = 4
NB_HEADS = NB_GROUPS * NB_HEADS_PER_GROUP
NB_WIDTH = NB_HEADS * HEAD_DIM
ALIBI_MAX_EXP = 8.0
LOCAL_QBLOCK = 64
N_IN = 3 * NA_WIDTH + 3 * NB_WIDTH + 2 * D_MODEL
NORM_EPS = 1e-6
ATTN_SCALE = HEAD_DIM ** -0.5


def _rmsnorm(x, g):
    xf = x.astype(jnp.float32)
    y = xf * lax.rsqrt(jnp.mean(xf * xf, axis=-1, keepdims=True) + NORM_EPS)
    return (y * g.astype(jnp.float32)).astype(x.dtype)

def _swiglu(x, w_gate, w_up, w_down):
    return (jax.nn.silu(x @ w_gate) * (x @ w_up)) @ w_down

def _neighbourhood_attention(q, k, v, rpb):
    B, T, H, Dh = q.shape
    rows = T // GRID_W
    kh = min(NA_ROWS, rows)
    r = jnp.arange(rows)
    row0 = jnp.clip(r - kh // 2, 0, rows - kh)
    key_rows = row0[:, None] + jnp.arange(kh)[None, :]
    c = jnp.arange(GRID_W)
    col0 = jnp.clip(c - NA_COLS // 2, 0, GRID_W - NA_COLS)
    col_ok = (c[None, :] >= col0[:, None]) & (c[None, :] < col0[:, None] + NA_COLS)
    col_rel = jnp.clip(c[None, :] - c[:, None], -(NA_COLS - 1), NA_COLS - 1)
    row_rel = key_rows - r[:, None]
    bias = rpb[:, (row_rel + NA_ROWS - 1)[:, None, :, None],
               (col_rel + NA_COLS - 1)[None, :, None, :]]
    qg = q.reshape(B, rows, GRID_W, H, Dh)
    kg = k.reshape(B, rows, GRID_W, H, Dh)[:, key_rows]
    vg = v.reshape(B, rows, GRID_W, H, Dh)[:, key_rows]
    s = jnp.einsum('brqhd,brkwhd->bhrqkw', qg, kg).astype(jnp.float32) * ATTN_SCALE
    s = s + bias[None].astype(jnp.float32)
    s = jnp.where(col_ok[:, None, :], s, -jnp.inf)
    p = jax.nn.softmax(s.reshape(B, H, rows, GRID_W, kh * GRID_W), axis=-1)
    p = p.reshape(s.shape).astype(v.dtype)
    o = jnp.einsum('bhrqkw,brkwhd->brqhd', p, vg)
    return o.reshape(B, T, H * Dh)

def _banded_attention(q, k, v, half, dilation, slopes):
    N, H, L, Dh = q.shape
    nb = -(-L // LOCAL_QBLOCK)
    lp = nb * LOCAL_QBLOCK
    pad = lp - L
    qp = jnp.pad(q, ((0, 0), (0, 0), (0, pad), (0, 0))).reshape(N, H, nb, LOCAL_QBLOCK, Dh)
    kp = jnp.pad(k, ((0, 0), (0, 0), (half, half + pad), (0, 0)))
    vp = jnp.pad(v, ((0, 0), (0, 0), (half, half + pad), (0, 0)))
    kspan = LOCAL_QBLOCK + 2 * half
    kidx = jnp.arange(nb)[:, None] * LOCAL_QBLOCK + jnp.arange(kspan)[None, :]
    kblk = kp[:, :, kidx]
    vblk = vp[:, :, kidx]
    s = jnp.einsum('nhbqd,nhbkd->nhbqk', qp, kblk).astype(jnp.float32) * ATTN_SCALE
    qpos = jnp.arange(nb)[:, None] * LOCAL_QBLOCK + jnp.arange(LOCAL_QBLOCK)[None, :]
    kpos = kidx - half
    rel = kpos[:, None, :] - qpos[:, :, None]
    valid = ((jnp.abs(rel) <= half) & (kpos[:, None, :] >= 0) & (kpos[:, None, :] < L)) | (qpos[:, :, None] >= L)
    dist = (dilation * jnp.abs(rel)).astype(jnp.float32)
    s = s - slopes[:, None, None, None] * dist[None]
    s = jnp.where(valid, s, -jnp.inf)
    lse = jax.nn.logsumexp(s, axis=-1)
    p = jnp.exp(s - lse[..., None]).astype(v.dtype)
    o = jnp.einsum('nhbqk,nhbkd->nhbqd', p, vblk).reshape(N, H, lp, Dh)[:, :, :L]
    return o, lse.reshape(N, H, lp)[:, :, :L]

def _dilated_attention(q, k, v, dilation, half, slopes):
    B, T, H, Dh = q.shape
    L = T // dilation

    def to_res(a):
        return a.reshape(B, L, dilation, H, Dh).transpose(0, 2, 3, 1, 4).reshape(B * dilation, H, L, Dh)

    o, lse = _banded_attention(to_res(q), to_res(k), to_res(v), half, dilation, slopes)
    o = o.reshape(B, dilation, H, L, Dh).transpose(0, 3, 1, 2, 4).reshape(B, T, H, Dh)
    lse = lse.reshape(B, dilation, H, L).transpose(0, 3, 1, 2).reshape(B, T, H)
    return o, lse

def _dilated_mixture(q, k, v, slopes):
    B, T, _ = q.shape
    shp = (B, T, NB_GROUPS, NB_HEADS_PER_GROUP, HEAD_DIM)
    q, k, v = q.reshape(shp), k.reshape(shp), v.reshape(shp)
    outs, lses = [], []
    for g, (window, dilation) in enumerate(DIL_PAIRS):
        half = window // (2 * dilation)
        sl = slopes[g * NB_HEADS_PER_GROUP:(g + 1) * NB_HEADS_PER_GROUP]
        o, lse = _dilated_attention(q[:, :, g], k[:, :, g], v[:, :, g], dilation, half, sl)
        outs.append(o)
        lses.append(lse)
    alpha = jax.nn.softmax(jnp.stack(lses, axis=0), axis=0)
    o = jnp.stack(outs, axis=0) * alpha[..., None].astype(outs[0].dtype)
    return o.transpose(1, 2, 0, 3, 4).reshape(B, T, NB_WIDTH)

def second_inputs(seed: int = 0) -> dict:
    key = jax.random.key(seed)
    ks = jax.random.split(key, 20)

    def nrm(k, shape, scale):
        return jax.random.normal(k, shape, jnp.float32) * scale

    def gain(k):
        return 1.0 + 0.05 * jax.random.normal(k, (DEPTH_2, D_MODEL), jnp.float32)

    return {
        'x': nrm(ks[0], (BATCH, SEQ, D_MODEL), 1.0),
        'ffn1_pre_g': gain(ks[1]),
        'ffn1_w_gate': nrm(ks[2], (DEPTH_2, D_MODEL, D_FF), D_MODEL ** -0.5),
        'ffn1_w_up': nrm(ks[3], (DEPTH_2, D_MODEL, D_FF), D_MODEL ** -0.5),
        'ffn1_w_down': nrm(ks[4], (DEPTH_2, D_FF, D_MODEL), D_FF ** -0.5),
        'ffn1_post_g': gain(ks[5]),
        'mix_pre_g': gain(ks[6]),
        'w_in': nrm(ks[7], (DEPTH_2, D_MODEL, N_IN), D_MODEL ** -0.5),
        'na_rpb': nrm(ks[8], (DEPTH_2, NA_HEADS, 2 * NA_ROWS - 1, 2 * NA_COLS - 1), 0.1),
        'w_branch_a': nrm(ks[9], (DEPTH_2, NA_WIDTH, D_MODEL), NA_WIDTH ** -0.5),
        'w_branch_b': nrm(ks[10], (DEPTH_2, NB_WIDTH, D_MODEL), NB_WIDTH ** -0.5),
        'w_out': nrm(ks[11], (DEPTH_2, D_MODEL, D_MODEL), D_MODEL ** -0.5),
        'mix_post_g': gain(ks[12]),
        'ffn2_pre_g': gain(ks[13]),
        'ffn2_w_gate': nrm(ks[14], (DEPTH_2, D_MODEL, D_FF), D_MODEL ** -0.5),
        'ffn2_w_up': nrm(ks[15], (DEPTH_2, D_MODEL, D_FF), D_MODEL ** -0.5),
        'ffn2_w_down': nrm(ks[16], (DEPTH_2, D_FF, D_MODEL), D_FF ** -0.5),
        'ffn2_post_g': gain(ks[17]),
    }

def second_block(x, ffn1_pre_g, ffn1_w_gate, ffn1_w_up, ffn1_w_down, ffn1_post_g,
              mix_pre_g, w_in, na_rpb, w_branch_a, w_branch_b, w_out, mix_post_g,
              ffn2_pre_g, ffn2_w_gate, ffn2_w_up, ffn2_w_down, ffn2_post_g):
    B, T, _ = x.shape
    slopes = jnp.exp2(-ALIBI_MAX_EXP * (jnp.arange(NB_HEADS, dtype=jnp.float32) + 1.0) / NB_HEADS)
    widths = [NA_WIDTH] * 3 + [NB_WIDTH] * 3 + [D_MODEL]
    splits = [int(s) for s in np.cumsum(widths)]
    for l in range(DEPTH_2):
        f = _swiglu(_rmsnorm(x, ffn1_pre_g[l]), ffn1_w_gate[l], ffn1_w_up[l], ffn1_w_down[l])
        x = x + 0.5 * _rmsnorm(f, ffn1_post_g[l])
        h = _rmsnorm(x, mix_pre_g[l])
        proj = h @ w_in[l]
        qa, ka, va, qb, kb, vb, gate_a, gate_b = jnp.split(proj, splits, axis=-1)
        ha = (B, T, NA_HEADS, HEAD_DIM)
        ya = _neighbourhood_attention(qa.reshape(ha), ka.reshape(ha), va.reshape(ha), na_rpb[l]) @ w_branch_a[l]
        yb = _dilated_mixture(qb, kb, vb, slopes) @ w_branch_b[l]
        merged = jax.nn.sigmoid(gate_a) * ya + jax.nn.sigmoid(gate_b) * yb
        x = x + _rmsnorm(merged @ w_out[l], mix_post_g[l])
        f = _swiglu(_rmsnorm(x, ffn2_pre_g[l]), ffn2_w_gate[l], ffn2_w_up[l], ffn2_w_down[l])
        x = x + 0.5 * _rmsnorm(f, ffn2_post_g[l])
    return x


def setup_inputs(seed=0):
    out = dict(first_inputs(seed))
    for name, value in second_inputs(seed + 1).items():
        if name != "x":
            out[name + "_2"] = value
    return out


def reference(
    x, positions, g_pre_mix, w_in, ck_pe, ck_w1, ck_b1, ck_w2, cv_pe, cv_w1, cv_b1, cv_w2,
    w_proj_nsa, w_proj_sb, w_out, g_post_mix, g_pre_ffn, w_up, conv_w, conv_b, w_down,
    g_post_ffn, ffn1_pre_g_2, ffn1_w_gate_2, ffn1_w_up_2, ffn1_w_down_2, ffn1_post_g_2,
    mix_pre_g_2, w_in_2, na_rpb_2, w_branch_a_2, w_branch_b_2, w_out_2, mix_post_g_2,
    ffn2_pre_g_2, ffn2_w_gate_2, ffn2_w_up_2, ffn2_w_down_2, ffn2_post_g_2,
):
    x = first_block(
        x, positions, g_pre_mix, w_in, ck_pe, ck_w1, ck_b1, ck_w2, cv_pe, cv_w1, cv_b1, cv_w2,
        w_proj_nsa, w_proj_sb, w_out, g_post_mix, g_pre_ffn, w_up, conv_w, conv_b, w_down,
        g_post_ffn,
    )
    return second_block(
        x, ffn1_pre_g_2, ffn1_w_gate_2, ffn1_w_up_2, ffn1_w_down_2, ffn1_post_g_2, mix_pre_g_2,
        w_in_2, na_rpb_2, w_branch_a_2, w_branch_b_2, w_out_2, mix_post_g_2, ffn2_pre_g_2,
        ffn2_w_gate_2, ffn2_w_up_2, ffn2_w_down_2, ffn2_post_g_2,
    )


_drawn_inputs = setup_inputs


def setup_inputs(seed=0):
    import zlib

    import numpy as np

    out = dict(_drawn_inputs(seed))
    spreads = {}
    factors = {'ck_pe': 28.492,
     'ck_b1': 48.519,
     'cv_pe': 4.859,
     'cv_b1': 7.888,
     'conv_b': 4.051,
     'g_post_ffn': 3.237,
     'ffn1_pre_g_2': 3.345,
     'ffn1_post_g_2': 4.931,
     'na_rpb_2': 2.773,
     'mix_post_g_2': 2.782,
     'ffn2_pre_g_2': 3.945,
     'ffn2_post_g_2': 5.8}
    for name, (base, spread) in spreads.items():
        noise = np.random.default_rng([zlib.crc32(name.encode()), seed]).standard_normal(out[name].shape)
        drawn = base * np.exp(spread * noise) if base else spread * noise
        out[name] = jnp.asarray(drawn.astype(out[name].dtype))
    for name, factor in factors.items():
        out[name] = (out[name] * factor).astype(out[name].dtype)
    return out
```

```python
import concourse.bass as bass
from concourse import mybir
from contextlib import ExitStack
import numpy as np

P = 128
T = 512
D = 1024
KT = D // P
TT = T // P
HD = 64
FF = 2816
FT = FF // P
FH = FT // 2
DEPTH = 2
NCMP = 31
CMPL = 32
EPS = 1e-6
NEG = -1e30
FAR = 1e32
QSCALE = HD ** -0.5
NBH = 12
SLOPES = [float(np.exp2(np.float32(-8.0 * (h + 1.0) / NBH))) for h in range(NBH)]
UL = 70
VL = UL // 2
UNITS = DEPTH * UL + 111
def _columns(parts):
    cols, at = {}, 0
    for name, n in parts:
        cols[name] = (at, n)
        at += n
    return cols, at


CONST_COLS, CONST_N = _columns((("ident", P), ("negtri", P), ("causal", P), ("strictneg", P), ("strict01", P),
                                ("cmpadd", TT * NCMP), ("cmpmul", TT * NCMP), ("invfreq", 1), ("sinsign", 1)))
CONST2_COLS, CONST2_N = _columns((("dist0", 3 * P), ("dist1", P), ("dist2", P), ("colmask", HD), ("sel", 2 * P)))
ORDER = (1, 4, 4)
TOEP = 65 * 64
TOEP_AT, TOEP_PAD = 16, 64
GAINS = 14
CONVN = DEPTH * 4 * 2 * FT
TABLE_DMAS = 1 + DEPTH * (4 + 2 * 3)
TWO_PI = 2 * np.pi
TURN_PARTS = (6.28125, 0.0019340515136718750, 2 * np.pi - 6.28125 - 0.0019340515136718750)
ROUND = 1.5 * 2.0 ** 23
PI_IN = 3.1415925


def shape_constants():
    c, c2 = np.zeros((P, CONST_N), np.float32), np.zeros((P, CONST2_N), np.float32)

    def put(name, a):
        to, (at, n) = (c, CONST_COLS[name]) if name in CONST_COLS else (c2, CONST2_COLS[name])
        to[:a.shape[0], at:at + n] = a

    r = np.arange(P)
    put("ident", np.eye(P))
    put("negtri", np.where(r[:, None] >= r[None, :], -1.0, 0.0))
    put("causal", np.where(r[None, :] <= r[:, None], 0.0, NEG))
    put("strictneg", np.where(r[:, None] < r[None, :], 0.0, NEG))
    put("strict01", np.where(r[:, None] < r[None, :], 1.0, 0.0))
    rel = np.abs(np.arange(3 * P)[None, :] - P - r[:, None])
    put("dist0", np.where(rel <= 64, rel, FAR))
    rel = np.abs(r[None, :] - r[:, None])
    put("dist1", np.where(rel <= 64, 4 * rel, FAR))
    put("dist2", np.where(rel % 4 == 0, 4 * rel, FAR))
    tok = (np.arange(TT) * P)[None, :, None] + r[:, None, None]
    ok = (np.arange(NCMP) * 16 + CMPL - 1)[None, None, :] <= tok
    put("cmpadd", np.where(ok, 0.0, NEG).reshape(P, -1))
    put("cmpmul", ok.astype(np.float32).reshape(P, -1))
    col = r % 64
    first = np.clip(col - 8, 0, 48)
    cw = np.arange(64)[None, :]
    put("colmask", np.where((cw >= first[:, None]) & (cw < first[:, None] + 16), 0.0, NEG))
    half = np.arange(32, dtype=np.float32) / np.float32(32)
    put("invfreq", np.power(np.float32(10000.0), -half).astype(np.float32)[r % 32][:, None])
    put("sinsign", np.where(r % 64 < 32, -1.0, 1.0)[:, None])
    sel = np.zeros((4, 2, P), np.float32)
    for h in range(4):
        sel[h, h // 2, (h % 2) * 64:(h % 2) * 64 + 64] = 1.0
    put("sel", sel.reshape(4, 2 * P))
    return c, c2


def build(nc, A, consts, consts2, toep, out):
    f32, f32r, bf16, i32 = mybir.dt.float32, mybir.dt.float32r, mybir.dt.bfloat16, mybir.dt.int32
    ALU = mybir.AluOpType
    ACT = mybir.ActivationFunctionType
    AX = mybir.AxisListType
    ctx = ExitStack()
    with ctx:
        def sem(name):
            return ctx.enter_context(nc.semaphore(name))

        def keep(name, shape, dt=f32):
            return ctx.enter_context(nc.sbuf_tensor(name, shape, dt))

        x = keep("x", [P, KT, T])
        raw = keep("raw", [P, 2, 2048])
        whi = keep("whi", [P, 2, 2048], f32r)
        wlo = keep("wlo", [P, 2, 2048], f32r)
        cst = keep("cst", [P, CONST_N])
        gains = keep("gains", [P, GAINS * KT])
        negones = keep("negones", [P, P])
        ident_bf = keep("ident_bf", [P, P], bf16)
        causal_bf = keep("causal_bf", [P, P], bf16)
        strict_bf = keep("strict_bf", [P, P], bf16)
        sq = keep("sq", [P, 2, T])
        acc = keep("acc", [P, T])
        rstd = keep("rstd", [P, T])
        tmp = keep("tmp", [P, 2, T])
        warm = keep("warm", [P, 4])
        rs, tg, tu = sq, sq, tmp

        def C(name):
            at, n = CONST_COLS[name]
            return cst[:, at:at + n]

        ident = C("ident")

        class Region:

            def __enter__(self):
                self.stack = ExitStack()
                self.stack.__enter__()
                return self

            def get(self, name, shape, dt=f32):
                return self.stack.enter_context(nc.sbuf_tensor(name, shape, dt))

            def __exit__(self, *a):
                self.stack.__exit__(*a)

        with Region() as r:
            branch = r.get("branch", [P, KT, T])
        hh = keep("hh", [P, KT, T], f32r)
        hl = keep("hl", [P, KT, T], f32r)
        with Region() as r:
            xin = r.get("xin", [P, TT, D])
            grows = r.get("grows", [GAINS * KT, P])
        with Region() as r:
            cosT = r.get("cosT", [P, T])
            sinT = r.get("sinT", [P, T])
            convc = r.get("convc", [P, CONVN])
            peT = r.get("peT", [P, DEPTH * 2, CMPL])
            cb1 = r.get("cb1", [HD, DEPTH * 2])
            with Region() as q:
                a1hi = q.get("a1hi", [P, FT, T], f32r)
                a1lo = q.get("a1lo", [P, FT, T], f32r)
            with Region() as q:
                posi = q.get("posi", [P, T], i32)
                ang = q.get("ang", [P, T])
                trn = q.get("trn", [P, T])
                trr = q.get("trr", [P, T])
                crows = q.get("crows", [88, 4, P])
                perows = q.get("perows", [CMPL, DEPTH * 2, P])
            with Region() as q:
                onhi = q.get("onhi", [P, 4, T], f32r)
                onlo = q.get("onlo", [P, 4, T], f32r)
                with Region() as n:
                    nqT = n.get("nqT", [P, 4, T])
                    kT = n.get("kT", [P, 4, T])
                    kcT = n.get("kcT", [P, 2, NCMP])
                    vcpad = n.get("vcpad", [NCMP, 2, 3 * HD])
                    vpad = n.get("vpad", [P, 2, TT * 2, 3 * HD])
                    gate = n.get("gate", [P, TT, 24])
                    cs = n.get("cs", [P, 32, NCMP])
                    cstat = n.get("cstat", [P, 3, 32])
                    nstat = n.get("nstat", [P, 4, 64])
                    with Region() as m:
                        kvA = m.get("kvA", [P, 2, T])
                        kvB = m.get("kvB", [P, 2, T])
                        w1 = m.get("w1", [P, 2, CMPL, HD])
                        w2 = m.get("w2", [HD, 2, HD])
                        w2pad = m.get("w2pad", [HD, 3 * HD])
                        hid = m.get("hid", [HD, 2, 2 * NCMP])
                    with Region() as m:
                        nP = m.get("nP", [P, 2, 1280])
                        nPT = m.get("nPT", [P, 2, 1280])
                        pcT = m.get("pcT", [NCMP, 2, T])
                oshi = q.get("oshi", [P, 4, T], f32r)
                oslo = q.get("oslo", [P, 4, T], f32r)
                with Region() as n:
                    sqT = n.get("sqT", [P, 4, T])
                    skT = n.get("skT", [P, 4, T])
                    svp = n.get("svp", [P, 2, TT * 2, 3 * HD])
                    sE = n.get("sE", [P, 1280])
                    sL = n.get("sL", [P, 2, 1280])
                    sW = n.get("sW", [P, 2, 1280])
                with Region() as n:
                    yhi = n.get("yhi", [P, KT, T], f32r)
                    ylo = n.get("ylo", [P, KT, T], f32r)
                    ga = n.get("ga", [P, T])
                    gb = n.get("gb", [P, T])
        with Region() as r:
            with Region() as q:
                a2hi = q.get("a2hi", [P, FT, T], f32r)
                a2lo = q.get("a2lo", [P, FT, T], f32r)
            with Region() as q:
                cst2 = q.get("cst2", [P, CONST2_N])
                zeros_bf = q.get("zeros_bf", [P, T], bf16)
                oahi = q.get("oahi", [P, 4, T], f32r)
                oalo = q.get("oalo", [P, 4, T], f32r)
                with Region() as n:
                    aqT = n.get("aqT", [P, 4, T])
                    akT = n.get("akT", [P, 4, T])
                    avp = n.get("avp", [P, 2, TT * 2, 3 * HD])
                    tab = n.get("tab", [P, 2, 14 * HD])
                    aP = n.get("aP", [P, 2, 2048])
                    aPT = n.get("aPT", [P, 2, 2048])
                    astat = n.get("astat", [P, 3, 32])
                obhi = q.get("obhi", [P, 6, T], f32r)
                oblo = q.get("oblo", [P, 6, T], f32r)
                with Region() as n:
                    bqT = n.get("bqT", [P, 2, T])
                    bkT = n.get("bkT", [P, 2, T])
                    bvp = n.get("bvp", [P, TT * 2, 3 * HD])
                    ob = n.get("ob", [P, 6, T])
                    bstat = n.get("bstat", [P, 3, 48])
                    lse = n.get("lse", [P, 48])
                    with Region() as m:
                        bP = m.get("bP", [P, 2, 1280])
                        bPT = m.get("bPT", [P, 2, 1280])
                    with Region() as m:
                        lseT = m.get("lseT", [4, 3, T])
                        alp = m.get("alp", [4, 3, T])
                        mz = m.get("mz", [4, 2, T])
                with Region() as n:
                    y2hi = n.get("y2hi", [P, KT, T], f32r)
                    y2lo = n.get("y2lo", [P, KT, T], f32r)
                    ga2 = n.get("ga2", [P, T])
                    gb2 = n.get("gb2", [P, T])
        with Region() as r:
            ostage = r.get("ostage", [P, TT, D])

        def C2(name):
            at, n = CONST2_COLS[name]
            return cst2[:, at:at + n]

        bank = [ctx.enter_context(nc.psum_tensor(f"bank{i}", [P, 512], f32)) for i in range(8)]
        NORM, MISC = bank[5], bank[3]

        w_loaded = [sem("w_loaded0"), sem("w_loaded1")]
        hi_ready = sem("hi_ready")
        lo_ready = sem("lo_ready")
        tile_done = sem("tile_done")
        dve_read = sem("dve_read")
        SEMS = {}
        for name in """const_in const2_in start_in table_in zeros_set toep_zero toep_filled
            start_x gains_t gains_set tables_t tables_copied ang_ready sin_done tables_ready negones_set
            x_ready sq_done sq_used var_done ms_done sd_done h_set hh_ready h_ready
            rs_ready rope_done k_exchanged cmp_in w2_staged kvAB_ready pads_zeroed v_ready gate_ready
            cmp_hid cmp_act cmp_out cmp_ready cs_done cs_masked cs_exp cs_probs cmp_pv
            sqk_act sqk_dve svp_zeroed z_done l_done L_ready arg_done w_ready spv_done so_hi so_lo
            gates_set y_set y2_hi y_ready
            aff_done conv_done gelu_done act_mul act_hi_done act_ready
            aqk_act aqk_dve avp_zeroed tab_in0 tab_in1 tab_used
            bqk_act bqk_dve bvp_zeroed ob_done ob_copied ln_done lse_ready lseT_done lseT_ready mx_ready aexp_done
            alpha_ready alpha_b alpha_used ob_hi ob_ready out_t out_ca out_cd out_st""".split():
            SEMS[name] = sem(name)
        S = type("Named", (), SEMS)

        class Rows:

            def __init__(self, name, items, keys, width, Pb, PTb, stat, lead=0, group=1, item0=0):
                self.items, self.keys, self.P, self.PT, self.stat = items, keys, Pb, PTb, stat
                self.lead, self.group, self.item0 = lead, group, item0
                self.s_done, self.max_done, self.exp_done, self.p_ready = (
                    sem(name + "_scores"), sem(name + "_max"), sem(name + "_exp"), sem(name + "_scaled"))
                self.t_done = sem(name + "_transposed")
                self.copied = [sem(name + "_copied_act"), sem(name + "_copied_dve")]
                self.pv_done, self.o_hi, self.o_free = sem(name + "_pv"), sem(name + "_ohi"), sem(name + "_ofree")
                self.off, at = [], 0
                for i in range(TT):
                    self.off.append(at)
                    at += (keys(i)[1] - keys(i)[0]) * P
                self.ptoff, at = [], 0
                for j in range(TT):
                    self.ptoff.append(at)
                    at += len(self.queries(j)) * P
                assert at <= width
                self.bias_done = sem(name + "_biased")
                self.fills = lead * (len(items) // group) + TT * len(items)
                self.scores = TT * len(items)

            def queries(self, j):
                return [i for i in range(TT) if self.keys(i)[0] <= j < self.keys(i)[1]]

            def fill(self, n, j):
                return (n // self.group + 1) * self.lead + TT * n + j

        nsa_items = [dict(h=2 * (n // 4) + (n // 2) % 2, b=n % 2) for n in range(16)]
        nsa = Rows("nsa", nsa_items, lambda i: (0, i + 1), 1280, nP, nPT, nstat, lead=2, group=4)
        na = Rows("na", [dict(h=h) for h in range(8)], lambda i: (0, TT), 2048, aP, aPT, astat)
        DIL = [Rows(f"dil{g}", [dict(h=h) for h in range(4)],
                    (lambda i: (max(0, i - 1), min(TT, i + 2))) if g == 0 else (lambda i: (i, i + 1)),
                    1280, bP, bPT, bstat, item0=4 * g) for g in range(3)]

        block = ctx.enter_context(nc.Block())
        w_in, w_in2 = A["w_in"], A["w_in_2"]

        @block.sync
        def _(sp):
            def unit(v, s, parts):
                sp.wait_ge(lo_ready, 2 * v + s + 1)
                for dst, src in parts:
                    sp.dma_start(dst, src).then_inc(w_loaded[s], 16)

            def wide(W, c0, s):
                src = W.rearrange("(k p) c -> p k c", p=P)[:, :, bass.ds(c0, 256)]
                dst = raw[:, s, :].rearrange("p (k c) -> p k c", k=8)
                return [(dst[:, 0:4], src[:, 0:4]), (dst[:, 4:8], src[:, 4:8])]

            def twin(Wa, ca, Wb, cb, s):
                dst = raw[:, s, :].rearrange("p (k t c) -> p k t c", k=8, t=2)
                return [(dst[:, :, i], W.rearrange("(k p) c -> p k c", p=P)[:, :, bass.ds(c, P)])
                        for i, (W, c) in enumerate(((Wa, ca), (Wb, cb)))]

            def half_rows(W, m, half, s):
                src = W[half * FH * P:(half + 1) * FH * P, bass.ds(m * P, P)].rearrange("(k p) c -> p k c", p=P)
                dst = raw[:, s, 0:FH * P].rearrange("p (k c) -> p k c", k=FH)
                return [(dst[:, 0:6], src[:, 0:6]), (dst[:, 6:FH], src[:, 6:FH])]

            def stacked(Wa, ka, Wb, kb, m, s):
                dst = raw[:, s, 0:(ka + kb) * P].rearrange("p (k c) -> p k c", k=ka + kb)
                return [(dst[:, k0:k1], W.rearrange("(k p) c -> p k c", p=P)[:, :, bass.ds(m * P, P)])
                        for W, k0, k1 in ((Wa, 0, ka), (Wb, ka, ka + kb))]

            sp.dma_start(cst[:, :], consts).then_inc(S.const_in, 16)
            for i in range(TT):
                sp.dma_start(xin[:, i, :], A["x"][0, i * P:(i + 1) * P, :]).then_inc(S.start_in, 16)
            norms = [("g_pre_mix", 0), ("g_post_mix", 0), ("g_pre_ffn", 0), ("g_post_ffn", 0),
                     ("g_pre_mix", 1), ("g_post_mix", 1), ("g_pre_ffn", 1), ("g_post_ffn", 1),
                     ("ffn1_pre_g_2", 0), ("ffn1_post_g_2", 0), ("mix_pre_g_2", 0), ("mix_post_g_2", 0),
                     ("ffn2_pre_g_2", 0), ("ffn2_post_g_2", 0)]
            for n, (name, l) in enumerate(norms):
                sp.dma_start(grows[n * KT:(n + 1) * KT, :], A[name][l].rearrange("(k p) -> k p", p=P)).then_inc(S.start_in, 16)
            sp.wait_ge(S.x_ready, KT)
            sp.wait_ge(S.gains_set, 1)
            sp.dma_start(posi[:, :], A["positions"].broadcast_to([P, T])).then_inc(S.table_in, 16)
            for l in range(DEPTH):
                for c, name, k in ((2 * l, "conv_w", 0), (2 * l, "conv_w", 1), (2 * l + 1, "conv_w", 2), (2 * l + 1, "conv_b", None)):
                    src = A[name][l] if k is None else A[name][l, k]
                    r0 = 0 if (k == 0 or k == 2) else 44
                    sp.dma_start(crows[r0:r0 + 44, c, :], src.rearrange("(k p) -> k p", p=P)).then_inc(S.table_in, 16)
                for kv, name in enumerate(("ck", "cv")):
                    for d in range(2):
                        sp.dma_start(perows[:, 2 * l + kv, d * HD:(d + 1) * HD], A[name + "_pe"][l]).then_inc(S.table_in, 16)
                    sp.dma_start(cb1[:, 2 * l + kv:2 * l + kv + 1], A[name + "_b1"][l].rearrange("(p o) -> p o", o=1)).then_inc(S.table_in, 16)

            with sp.Fori(0, DEPTH) as l:
                v0 = l * VL
                W = w_in[l]
                for i in range(2):
                    unit(v0, i, wide(W, 256 * i, i))
                sp.wait_ge(S.x_ready, KT * (2 * l + 1))
                sp.wait_ge(S.tables_ready, 1)
                for kv, name in enumerate(("ck", "cv")):
                    for d in range(2):
                        sp.dma_start(w1[d * HD:(d + 1) * HD, kv], A[name + "_w1"][l].rearrange("(p d) h -> d p h", d=HD)).then_inc(S.cmp_in, 16)
                    sp.dma_start(w2[:, kv, :], A[name + "_w2"][l]).then_inc(S.cmp_in, 16)
                for i in range(3):
                    unit(v0 + 1 + i // 2, i % 2, wide(W, 512 + 256 * i, i % 2))
                dst = raw[:, 1, :].rearrange("p (k c) -> p k c", k=8)[:, :, 0:24]
                src = W[:, 1280:1304].rearrange("(k p) c -> p k c", p=P)
                unit(v0 + 2, 1, [(dst[:, 0:4], src[:, 0:4]), (dst[:, 4:8], src[:, 4:8])])
                with sp.Fori(0, 3) as i:
                    for s in range(2):
                        unit(v0 + 3 + i, s, wide(W, 1304 + 512 * i + 256 * s, s))
                with sp.Fori(0, KT) as m:
                    unit(v0 + 6 + m, 0, twin(W, 2840 + P * m, W, 2840 + D + P * m, 0))
                    unit(v0 + 6 + m, 1, stacked(A["w_proj_nsa"][l], 4, A["w_proj_sb"][l], 4, m, 1))
                with sp.Fori(0, 2) as i:
                    for s in range(2):
                        unit(v0 + 14 + i, s, wide(A["w_out"][l], 512 * i + 256 * s, s))
                with sp.Fori(0, FH) as i:
                    for s in range(2):
                        unit(v0 + 16 + i, s, twin(A["w_up"][l], (2 * i + s) * P, A["w_up"][l], (2 * i + s) * P + FF, s))
                with sp.Fori(0, KT) as m:
                    for s in range(2):
                        unit(v0 + 27 + m, s, half_rows(A["w_down"][l], m, s, s))

            v2 = DEPTH * VL

            def ffn(v, pre):
                with sp.Fori(0, FH) as i:
                    for s in range(2):
                        unit(v + i, s, twin(A[pre + "_w_gate_2"][0], (2 * i + s) * P, A[pre + "_w_up_2"][0], (2 * i + s) * P, s))
                with sp.Fori(0, KT) as m:
                    for s in range(2):
                        unit(v + FH + m, s, half_rows(A[pre + "_w_down_2"][0], m, s, s))

            ffn(v2, "ffn1")
            sp.wait_ge(tile_done, 2 * (DEPTH * UL + 38))
            sp.dma_start(cst2[:, :], consts2).then_inc(S.const2_in, 16)
            W = w_in2[0]
            with sp.Fori(0, 3) as i:
                for s in range(2):
                    unit(v2 + 19 + i, s, wide(W, 512 * i + 256 * s, s))
            for g in range(3):
                for c in range(3):
                    u = 44 + 3 * g + c
                    unit(v2 + u // 2, u % 2, wide(W, 1536 + 768 * c + 256 * g, u % 2))
            with sp.Fori(0, KT) as m:
                unit(v2 + 26 + m, 1, twin(W, (m + 30) * P, W, (m + 38) * P, 1))
                unit(v2 + 27 + m, 0, stacked(A["w_branch_a_2"][0], 4, A["w_branch_b_2"][0], 6, m, 0))
            unit(v2 + 34, 1, wide(A["w_out_2"][0], 0, 1))
            unit(v2 + 35, 0, wide(A["w_out_2"][0], 256, 0))
            unit(v2 + 35, 1, wide(A["w_out_2"][0], 512, 1))
            unit(v2 + 36, 0, wide(A["w_out_2"][0], 768, 0))
            with sp.Fori(0, FH) as i:
                for s in range(2):
                    unit(v2 + 36 + i + (1 + s) // 2, (1 + s) % 2, twin(A["ffn2_w_gate_2"][0], (2 * i + s) * P, A["ffn2_w_up_2"][0], (2 * i + s) * P, (1 + s) % 2))
            with sp.Fori(0, KT) as m:
                for s in range(2):
                    unit(v2 + 47 + m + (1 + s) // 2, (1 + s) % 2, half_rows(A["ffn2_w_down_2"][0], m, s, (1 + s) % 2))
            for i in range(TT):
                sp.wait_ge(S.out_ca, i + 1)
                sp.wait_ge(S.out_cd, i + 1)
                sp.dma_start(out[0, i * P:(i + 1) * P, :], ostage[:, i, :]).then_inc(S.out_st, 16)
            sp.wait_ge(S.out_st, 16 * TT)

        @block.gpsimd
        def _(pool):
            pool.memset(warm[:, 0:1], 0.0).then_inc(lo_ready, 2)

            def rest(v, s):
                pool.wait_ge(hi_ready, 2 * v + s + 1)
                pool.tensor_tensor(wlo[:, s, :], raw[:, s, :], whi[:, s, :].bitcast(f32), ALU.subtract).then_inc(lo_ready, 1)

            with pool.Fori(0, UNITS // 2) as v:
                for s in range(2):
                    rest(v, s)
            rest(UNITS // 2, 0)

        @block.scalar
        def _(act):
            def upper(v, s, first=False):
                act.wait_ge(w_loaded[s], 32 * (v + 1))
                if not first:
                    act.wait_ge(tile_done, 4 * v + 2 * s - 2)
                act.activation(whi[:, s, :], raw[:, s, :], ACT.Copy).then_inc(hi_ready, 1)

            def tile(v, s, mt):
                act.wait_ge(tile_done, 4 * v + 2 * s + mt + 1)

            def root(n):
                act.wait_ge(S.ms_done, n + 1)
                act.activation(acc[:, :], acc[:, :], ACT.Sqrt).then_inc(S.sd_done, 1)

            def pre_norm(n, m):
                for k in range(KT):
                    act.wait_ge(S.x_ready, KT * m + k + 1)
                    if k >= 2:
                        act.wait_ge(S.sq_used, KT * n + k - 1)
                    act.activation(sq[:, k % 2], x[:, k], ACT.Square).then_inc(S.sq_done, 1)
                root(n)
                for k in range(KT):
                    act.wait_ge(S.h_set, KT * m + k + 1)
                    act.activation(hh[:, k], tmp[:, k % 2], ACT.Copy).then_inc(S.hh_ready, 1)

            def row_exp(st, n, base, from_bank):
                for i in range(TT):
                    lo, hi = st.keys(i)
                    w = (hi - lo) * P
                    a = TT * n + i
                    col = TT * (n + st.item0) + i
                    act.wait_ge(st.max_done, base(st.scores) + a + 1)
                    if i == 0 and n >= 2:
                        act.wait_ge(st.t_done, base(st.fills) + st.fill(n - 2, TT - 1) + 1)
                    pr = st.P[:, n % 2, st.off[i]:st.off[i] + w]
                    act.activation(pr, bank[a % 3][:, 0:w] if from_bank else pr, ACT.Exp,
                                   bias=st.stat[:, 0, col:col + 1], accum_out=st.stat[:, 1, col:col + 1]).then_inc(st.exp_done, 1)

            def row_copies(st, n, base):
                for j in range(TT):
                    f = st.fill(n, j)
                    if f % 2:
                        continue
                    qs = st.queries(j)
                    act.wait_ge(st.t_done, base(st.fills) + f + 1)
                    if n >= 2:
                        act.wait_ge(st.pv_done, base(len(st.items)) + n - 1)
                    act.activation(st.PT[:, n % 2, st.ptoff[j]:st.ptoff[j] + len(qs) * P],
                                   bank[4 + f % 2][:, qs[0] * P:(qs[-1] + 1) * P], ACT.Copy).then_inc(st.copied[0], 1)

            def down(v, s0, n):
                with act.Fori(0, KT // 2) as i:
                    for q in range(2):
                        for half in range(2):
                            vv, s = v + 2 * i + (s0 + 2 * q + half) // 2, (s0 + half) % 2
                            tile(vv, s, 1)
                            if half == 1:
                                act.wait_ge(S.sq_used, KT * n + 2 * i + q - 1)
                                act.activation(sq[:, q], bank[2 * q][:, :], ACT.Square).then_inc(S.sq_done, 1)
                            upper(vv + 1, s)
                root(n)

            def out_proj(v, s0, n):
                for i in range(4):
                    vv, s = v + (s0 + i) // 2, (s0 + i) % 2
                    for mt in range(2):
                        k = 2 * i + mt
                        tile(vv, s, mt)
                        act.wait_ge(S.sq_used, KT * n + k - 1)
                        act.activation(sq[:, k % 2], bank[2 * s + mt][:, :], ACT.Square).then_inc(S.sq_done, 1)
                    upper(vv + 1, s)
                root(n)

            def merge(v, s, yb, gab, yn):
                act.wait_ge(S.y_set, yn + 1)
                tile(v, s, 0)
                act.activation(gab[0][:, :], bank[2 * s][:, :], ACT.Sigmoid)
                tile(v, s, 1)
                act.activation(gab[1][:, :], bank[2 * s + 1][:, :], ACT.Sigmoid).then_inc(S.gates_set, 1)
                upper(v + 1, s)
                act.wait_ge(S.y_set, yn + 2)
                act.activation(yb, tmp[:, 0], ACT.Copy).then_inc(S.y2_hi, 1)
                upper(v + 1 + s, 1 - s)

            act.wait_ge(S.zeros_set, 1)
            act.dma_start(bass.AP(tensor=toep.tensor, offset=0, ap=[[TOEP, 120], [416, 10], [1, 416]]),
                          acc[0:120, 0:416].rearrange("p (o c) -> p o c", o=1).broadcast_to([120, 10, 416])).then_inc(S.toep_zero, 16)
            act.dma_start(bass.AP(tensor=toep.tensor, offset=120 * TOEP, ap=[[TOEP_PAD, 1], [1, TOEP_PAD]]), acc[0:1, 0:TOEP_PAD]).then_inc(S.toep_zero, 16)
            act.wait_ge(S.toep_zero, 32)
            act.dma_start(bass.AP(tensor=toep.tensor, offset=TOEP_AT - 15, ap=[[TOEP, 120], [65, HD], [1, 31]]),
                          bass.AP(tensor=A["na_rpb_2"].tensor, offset=0, ap=[[31, 120], [0, HD], [1, 31]])).then_inc(S.toep_filled, 16)
            upper(0, 0, True)
            upper(0, 1, True)
            act.wait_ge(S.ang_ready, 1)
            act.activation(sinT[:, :], trr[:, :], ACT.Sin).then_inc(S.sin_done, 1)
            act.wait_ge(S.ang_ready, 2)
            act.activation(cosT[:, :], ang[:, :], ACT.Sin).then_inc(S.sin_done, 1)
            act.wait_ge(S.tables_t, 1)
            act.activation(peT[:, :, :], bank[6][:, 0:4 * CMPL].rearrange("p (a c) -> p a c", a=4), ACT.Copy)
            act.activation(convc[:, :], bank[7][:, 0:CONVN], ACT.Copy).then_inc(S.tables_copied, 1)

            with act.Fori(0, DEPTH) as l:
                v0 = l * VL
                base = lambda c, l=l: l * c
                pre_norm(4 * l, 2 * l)
                rope = []

                def turned(v, s, mt, scale):
                    r = len(rope)
                    tile(v, s, mt)
                    if r >= 2:
                        act.wait_ge(S.rope_done, 7 * l + r - 1)
                    for qd in range(4):
                        to = 32 * (qd ^ 1)
                        o = act.activation(rs[to:to + 32, r % 2], bank[2 * s + mt][32 * qd:32 * qd + 32, :], ACT.Copy, scale=scale)
                    o.then_inc(S.rs_ready, 1)
                    rope.append(r)

                for i in range(2):
                    for mt in range(2):
                        turned(v0, i, mt, QSCALE)
                    upper(v0 + 1, i)
                turned(v0 + 1, 0, 0, 1.0)
                upper(v0 + 2, 0)
                for b, (v, s) in enumerate(((v0 + 1, 1), (v0 + 2, 0))):
                    turned(v, s, 0, 1.0)
                    tile(v, s, 1)
                    act.wait_ge(S.pads_zeroed, l + 1)
                    act.activation(vpad[:, b, :, HD:2 * HD], bank[2 * s + 1][:, :].rearrange("p (a c) -> p a c", a=TT * 2), ACT.Copy).then_inc(S.v_ready, 1)
                    upper(v + 1, s)
                tile(v0 + 2, 1, 1)
                act.activation(gate[:, :, :], bank[2][:, 0:TT * 24].rearrange("p (a c) -> p a c", a=TT), ACT.Sigmoid).then_inc(S.gate_ready, 1)
                upper(v0 + 3, 1)
                act.wait_ge(S.rope_done, 7 * l + 7)
                for b in range(2):
                    for g in range(2):
                        o = act.activation(kT[(1 - g) * HD:(2 - g) * HD, 2 + b], kT[g * HD:(g + 1) * HD, b], ACT.Copy)
                o.then_inc(S.k_exchanged, 1)
                for kv in range(2):
                    act.wait_ge(S.cmp_hid, 2 * l + 2)
                    for g in range(2):
                        o = act.activation(hid[:, kv, g * NCMP:(g + 1) * NCMP], bank[6 + g][0:HD, kv * 64:kv * 64 + NCMP],
                                           ACT.Gelu_apprx_tanh, bias=cb1[:, bass.ds(2 * l + kv, 1)])
                    o.then_inc(S.cmp_act, 1)
                act.wait_ge(S.cmp_out, l + 1)
                act.activation(kcT[:, 0], bank[4][:, 0:NCMP], ACT.Copy)
                for g in range(2):
                    act.activation(kcT[(1 - g) * HD:(2 - g) * HD, 1], bank[4][g * HD:(g + 1) * HD, 0:NCMP], ACT.Copy)
                act.wait_ge(S.pads_zeroed, l + 1)
                act.activation(vcpad[:, :, HD:2 * HD], bank[4][0:NCMP, 64:192].rearrange("p (a c) -> p a c", a=2), ACT.Copy).then_inc(S.cmp_ready, 1)
                act.wait_ge(S.cs_masked, l + 1)
                act.activation(cs[:, :, :], cs[:, :, :], ACT.Exp).then_inc(S.cs_exp, 1)

                row_exp(nsa, 0, base, True)
                for n in range(16):
                    t = n // 4
                    if n % 4 == 0:
                        act.wait_ge(nsa.t_done, nsa.fills * l + 18 * t + 1)
                        if t >= 1:
                            act.wait_ge(S.cmp_pv, 4 * l + t)
                        act.activation(pcT[:, 0], bank[4][0:NCMP, :], ACT.Copy).then_inc(nsa.copied[0], 1)
                    if n + 1 < 16:
                        row_exp(nsa, n + 1, base, True)
                    row_copies(nsa, n, base)
                    if n % 4 == 3:
                        act.wait_ge(nsa.pv_done, 16 * l + n + 1)
                        act.activation(onhi[:, t], bank[6 + t % 2][:, :], ACT.Copy).then_inc(nsa.o_hi, 1)

                for c in range(2):
                    for s in range(2):
                        tile(v0 + 3 + c, s, 0)
                        act.activation((sqT, skT)[c][:, 2 * s], bank[2 * s][:, :], ACT.Copy, scale=QSCALE if c == 0 else 1.0).then_inc(S.sqk_act, 1)
                        upper(v0 + 4 + c, s)
                for s in range(2):
                    tile(v0 + 5, s, 0)
                    act.wait_ge(S.svp_zeroed, l + 1)
                    for hf in range(2):
                        o = act.activation(svp[:, s, 0:4, 2 * HD * hf:2 * HD * hf + HD],
                                           bank[2 * s][:, :].rearrange("p (a h c) -> p a h c", a=4, h=2)[:, :, hf], ACT.Copy)
                    o.then_inc(S.sqk_act, 1)
                    upper(v0 + 6, s)

                def sb_soft(h):
                    act.wait_ge(S.z_done, 8 * l + h + 1)
                    if h >= 1:
                        act.wait_ge(S.L_ready, 8 * l + h)
                    for b, (c0, w) in enumerate(((0, 512), (512, 512), (1024, 256))):
                        act.activation(sE[:, c0:c0 + w], bank[3 * (h % 2) + b][:, 0:w], ACT.Abs)
                    act.drain()
                    act.activation(sE[:, :], sE[:, :], ACT.Exp, scale=-1.0)
                    act.drain()
                    act.activation(sE[:, :], sE[:, :], ACT.Ln, bias=1.0).then_inc(S.l_done, 1)

                sb_soft(0)
                for h in range(8):
                    if h + 1 < 8:
                        sb_soft(h + 1)
                    act.wait_ge(S.arg_done, 8 * l + h + 1)
                    if h >= 2:
                        act.wait_ge(S.spv_done, 8 * l + h - 1)
                    for b, (c0, w) in enumerate(((0, 512), (512, 512), (1024, 256))):
                        o = act.activation(sW[:, h % 2, c0:c0 + w], bank[3 * (h % 2) + b][:, 0:w], ACT.Exp)
                    o.then_inc(S.w_ready, 1)
                    if h % 2 == 1:
                        t = h // 2
                        act.wait_ge(S.spv_done, 8 * l + h + 1)
                        act.activation(oshi[:, t], bank[6 + t % 2][:, :], ACT.Copy).then_inc(S.so_hi, 1)

                with act.Fori(0, KT) as m:
                    merge(v0 + 6 + m, 0, yhi[:, bass.ds(m, 1)].rearrange("p o t -> p (o t)"), (ga, gb), 8 * l + m)

                out_proj(v0 + 14, 0, 4 * l + 1)
                pre_norm(4 * l + 2, 2 * l + 1)

                with act.Fori(0, FH) as i:
                    for s in range(2):
                        v = v0 + 16 + i
                        f = 2 * i + s
                        for mt, dst in ((0, tg), (1, tu)):
                            tile(v, s, mt)
                            act.wait_ge(S.act_ready, FT * l + f + 1)
                            at = 176 * l + f + FT * mt
                            act.activation(dst[:, 0], bank[2 * s + mt][:, :], ACT.Identity,
                                           bias=convc[:, bass.ds(at + 132, 1)], scale=convc[:, bass.ds(at + 88, 1)]).then_inc(S.aff_done, 1)
                        act.wait_ge(S.conv_done, 2 * FT * l + 2 * f + 1)
                        act.activation(tg[:, 1], tg[:, 0], ACT.Gelu_apprx_tanh).then_inc(S.gelu_done, 1)
                        act.wait_ge(S.act_mul, FT * l + f + 1)
                        act.activation(a1hi[:, bass.ds(f, 1)].rearrange("p o t -> p (o t)"), tu[:, 1], ACT.Copy).then_inc(S.act_hi_done, 1)
                        upper(v + 1, s)
                down(v0 + 27, 0, 4 * l + 3)

            v2 = DEPTH * VL
            zero = lambda c: 0

            def ffn2(u0, n, m, f0):
                pre_norm(n, m)
                with act.Fori(0, FH) as i:
                    for q in range(2):
                        v, s = v2 + i + (u0 + q) // 2, (u0 + q) % 2
                        f = f0 + 2 * i + q
                        tile(v, s, 0)
                        act.wait_ge(S.act_ready, f + 1)
                        act.activation(tg[:, 0], bank[2 * s][:, :], ACT.Silu).then_inc(S.gelu_done, 1)
                        act.wait_ge(S.act_mul, f + 1)
                        act.activation(a2hi[:, bass.ds(2 * i + q, 1)].rearrange("p o t -> p (o t)"), tu[:, 1], ACT.Copy).then_inc(S.act_hi_done, 1)
                        upper(v + 1, s)

            ffn2(0, 8, 4, DEPTH * FT)
            down(v2 + 11, 0, 9)
            pre_norm(10, 5)
            for c in range(2):
                for s in range(2):
                    tile(v2 + 19 + c, s, 0)
                    act.activation((aqT, akT)[c][:, 2 * s], bank[2 * s][:, :], ACT.Copy, scale=QSCALE if c == 0 else 1.0).then_inc(S.aqk_act, 1)
                    upper(v2 + 20 + c, s)
            for s in range(2):
                tile(v2 + 21, s, 0)
                act.wait_ge(S.avp_zeroed, 1)
                for hf in range(2):
                    o = act.activation(avp[:, s, 0:4, 2 * HD * hf:2 * HD * hf + HD],
                                       bank[2 * s][:, :].rearrange("p (a h c) -> p a h c", a=4, h=2)[:, :, hf], ACT.Copy)
                o.then_inc(S.aqk_act, 1)
                upper(v2 + 22, s)

            def load_table(h):
                for r2 in range(2):
                    src = bass.AP(tensor=toep.tensor, offset=TOEP_AT + (h * 15 + 1 - r2) * TOEP, ap=[[HD, HD], [TOEP, 14], [1, HD]])
                    act.dma_start(tab[r2 * HD:(r2 + 1) * HD, h % 2, :].rearrange("p (u c) -> p u c", u=14), src).then_inc((S.tab_in0, S.tab_in1)[h % 2], 16)

            act.wait_ge(S.toep_filled, 16)
            load_table(0)
            load_table(1)
            row_exp(na, 0, zero, False)
            for n in range(8):
                if n + 1 < 8:
                    row_exp(na, n + 1, zero, False)
                row_copies(na, n, zero)
                if n + 2 < 8:
                    act.wait_ge(S.tab_used, n + 1)
                    load_table(n + 2)
                if n % 2 == 1:
                    t = n // 2
                    act.wait_ge(na.pv_done, n + 1)
                    act.activation(oahi[:, t], bank[6 + t % 2][:, :], ACT.Copy).then_inc(na.o_hi, 1)

            for g, st in enumerate(DIL):
                dil = ORDER[g]
                for c in range(3):
                    u = 44 + 3 * g + c
                    v, s = v2 + u // 2, u % 2
                    tile(v, s, 0)
                    if c < 2:
                        if g > 0 and c == 0:
                            act.wait_ge(DIL[g - 1].pv_done, 4)
                        act.activation((bqT, bkT)[c][:, 0].rearrange("p (r l) -> p r l", r=dil),
                                       bank[2 * s][:, :].rearrange("p (l r) -> p r l", r=dil), ACT.Copy,
                                       scale=QSCALE if c == 0 else 1.0).then_inc(S.bqk_act, 1)
                    else:
                        act.wait_ge(S.bvp_zeroed, 1)
                        for hf in range(2):
                            o = act.activation(bvp[:, 0:4, 2 * HD * hf:2 * HD * hf + HD],
                                               bank[2 * s][:, :].rearrange("p (a h c) -> p a h c", a=4, h=2)[:, :, hf], ACT.Copy)
                        o.then_inc(S.bqk_act, 1)
                    upper(v + 1, s)
                row_exp(st, 0, zero, False)
                for n in range(4):
                    if n + 1 < 4:
                        row_exp(st, n + 1, zero, False)
                    row_copies(st, n, zero)
                    if n % 2 == 1:
                        act.wait_ge(S.ob_done, 2 * g + n // 2 + 1)
                        act.activation(ob[:, 2 * g + n // 2].rearrange("p (l r) -> p r l", r=dil),
                                       bank[6 + n // 2][:, :].rearrange("p (r l) -> p r l", r=dil), ACT.Copy).then_inc(S.ob_copied, 1)
            act.wait_ge(DIL[2].p_ready, 16)
            act.activation(lse[:, :], bstat[:, 1, :], ACT.Ln).then_inc(S.ln_done, 1)
            act.wait_ge(S.lseT_done, 1)
            for g in range(3):
                dil = ORDER[g]
                o = act.activation(lseT[:, g].rearrange("p (l r) -> p r l", r=dil),
                                   bank[g][0:4, :].rearrange("p (r l) -> p r l", r=dil), ACT.Copy)
            o.then_inc(S.lseT_ready, 1)
            act.wait_ge(S.mx_ready, 1)
            act.activation(alp[:, :, :], alp[:, :, :], ACT.Exp).then_inc(S.aexp_done, 1)
            for t in range(6):
                act.wait_ge(S.alpha_used, t + 1)
                act.activation(obhi[:, t], ob[:, t], ACT.Copy).then_inc(S.ob_hi, 1)

            with act.Fori(0, KT) as m:
                merge(v2 + 26 + m, 1, y2hi[:, bass.ds(m, 1)].rearrange("p o t -> p (o t)"), (ga2, gb2), 8 * DEPTH + m)
            out_proj(v2 + 34, 1, 11)
            ffn2(73, 12, 6, DEPTH * FT + FT)

            last = KT // 2 - 1
            with act.Fori(0, last) as i:
                for q in range(2):
                    for half in range(2):
                        vv, s = v2 + 47 + 2 * i + (1 + 2 * q + half) // 2, (1 + half) % 2
                        tile(vv, s, 1)
                        if half == 1:
                            act.wait_ge(S.sq_used, KT * 13 + 2 * i + q - 1)
                            act.activation(sq[:, q], bank[2 - 2 * q][:, :], ACT.Square).then_inc(S.sq_done, 1)
                        upper(vv + 1, s)
            for q in range(2):
                for half in range(2):
                    vv, s = v2 + 47 + 2 * last + (1 + 2 * q + half) // 2, (1 + half) % 2
                    tile(vv, s, 1)
                    if half == 1:
                        act.wait_ge(S.sq_used, KT * 13 + 2 * last + q - 1)
                        act.activation(sq[:, q], bank[2 - 2 * q][:, :], ACT.Square).then_inc(S.sq_done, 1)
                    if q == 0:
                        upper(vv + 1, s)
            root(13)
            for i in range(TT):
                act.wait_ge(S.out_t, 2 * i + 1)
                act.activation(ostage[:, i, 0:512], bank[(2 * i) % 4][:, :], ACT.Copy).then_inc(S.out_ca, 1)

        @block.vector
        def _(dve):
            def tile(v, s, mt):
                dve.drain()
                dve.wait_ge(tile_done, 4 * v + 2 * s + mt + 1)

            def pre_norm(n, m):
                for k in range(KT):
                    dve.drain()
                    dve.wait_ge(S.sq_done, KT * n + k + 1)
                    if k == 0:
                        dve.tensor_copy(acc[:, :], sq[:, 0]).then_inc(S.sq_used, 1)
                    else:
                        dve.tensor_tensor(acc[:, :], acc[:, :], sq[:, k % 2], ALU.add).then_inc(S.sq_used, 1)
                inverse_root(n)

                def lower(k):
                    dve.wait_ge(S.hh_ready, KT * m + k + 1)
                    dve.tensor_tensor(hl[:, k], tmp[:, k % 2], hh[:, k].bitcast(f32), ALU.subtract).then_inc(S.h_ready, 1)

                for k in range(KT):
                    dve.drain()
                    dve.scalar_tensor_tensor(tmp[:, k % 2], x[:, k], gains[:, bass.ds(KT * n + k, 1)], rstd[:, :],
                                             ALU.mult, ALU.mult).then_inc(S.h_set, 1)
                    if k >= 1:
                        lower(k - 1)
                lower(KT - 1)

            def inverse_root(n):
                dve.drain()
                dve.wait_ge(S.var_done, n + 1)
                dve.tensor_scalar(acc[:, :], NORM[:, :], -1.0 / D, EPS, ALU.mult, ALU.add).then_inc(S.ms_done, 1)
                dve.wait_ge(S.sd_done, n + 1)
                dve.reciprocal(rstd[:, :], acc[:, :])
                dve.drain()

            def add_square(n, k, slot, first):
                dve.wait_ge(S.sq_done, KT * n + k + 1)
                if first:
                    dve.tensor_copy(acc[:, :], sq[:, slot]).then_inc(S.sq_used, 1)
                else:
                    dve.tensor_tensor(acc[:, :], acc[:, :], sq[:, slot], ALU.add).then_inc(S.sq_used, 1)

            def post_norm(n, scale):
                inverse_root(n)
                for k in range(KT):
                    dve.drain()
                    dve.scalar_tensor_tensor(tmp[:, k % 2], branch[:, k], gains[:, bass.ds(KT * n + k, 1)], rstd[:, :],
                                             ALU.mult, ALU.mult)
                    dve.drain()
                    dve.scalar_tensor_tensor(x[:, k], tmp[:, k % 2], scale, x[:, k], ALU.mult, ALU.add).then_inc(S.x_ready, 1)

            def down(v, s0, n):
                with dve.Fori(0, KT // 2) as i:
                    for q in range(2):
                        dve.drain().then_inc(dve_read, 1)
                        vv, s = v + 2 * i + (s0 + 2 * q + 1) // 2, (s0 + 1) % 2
                        tile(vv, s, 1)
                        k = 2 * i + q
                        dve.wait_ge(S.sq_done, KT * n + k + 1)
                        dve.tensor_copy(branch[:, bass.ds(k, 1)].rearrange("p o t -> p (o t)"), bank[(2 * s0 + 2 * q) % 4][:, :])
                        dve.tensor_tensor(acc[:, :], acc[:, :], sq[:, q], ALU.add).then_inc(S.sq_used, 1)
                        dve.drain().then_inc(dve_read, 1)

            def out_proj(v, s0, n):
                for i in range(4):
                    vv, s = v + (s0 + i) // 2, (s0 + i) % 2
                    for mt in range(2):
                        k = 2 * i + mt
                        tile(vv, s, mt)
                        add_square(n, k, k % 2, k == 0)
                        o = dve.tensor_copy(branch[:, k], bank[2 * s + mt][:, :])
                        if mt == 1:
                            o.then_inc(dve_read, 1)

            def row_max(st, n, base, table=None, slopes=None):
                dve.drain()
                for i in range(TT):
                    lo, hi = st.keys(i)
                    w = (hi - lo) * P
                    a = TT * n + i
                    col = TT * (n + st.item0) + i
                    dve.wait_ge(st.s_done, base(st.scores) + a + 1)
                    src = bank[a % 3][:, 0:w]
                    if table is not None or slopes is not None:
                        if i == 0 and n >= 2:
                            dve.wait_ge(st.t_done, base(st.fills) + st.fill(n - 2, TT - 1) + 1)
                        pr = st.P[:, n % 2, st.off[i]:st.off[i] + w]
                        if table is not None:
                            dve.tensor_tensor(pr, src, table[:, (6 - 2 * i) * HD:(14 - 2 * i) * HD], ALU.add).then_inc(st.bias_done, 1)
                        else:
                            dist = slopes[0][:, (lo - i + 1) * P:(hi - i + 1) * P] if slopes[2] else slopes[0]
                            dve.scalar_tensor_tensor(pr, dist, -slopes[1], src, ALU.mult, ALU.add).then_inc(st.bias_done, 1)
                        dve.drain()
                        src = pr
                    dve.tensor_reduce(st.stat[:, 0, col:col + 1], src, AX.X, ALU.max, negate=True).then_inc(st.max_done, 1)

            def row_scale(st, n, base, gates=None):
                dve.drain()
                dve.wait_ge(st.exp_done, base(st.scores) + TT * n + TT)
                c0 = TT * (n + st.item0)
                dve.reciprocal(st.stat[:, 2, c0:c0 + TT], st.stat[:, 1, c0:c0 + TT])
                dve.drain()
                if gates is not None:
                    dve.tensor_tensor(st.stat[:, 2, c0:c0 + TT], st.stat[:, 2, c0:c0 + TT], gates, ALU.mult)
                    dve.drain()
                for i in range(TT):
                    lo, hi = st.keys(i)
                    pr = st.P[:, n % 2, st.off[i]:st.off[i] + (hi - lo) * P]
                    dve.tensor_scalar(pr, pr, st.stat[:, 2, c0 + i:c0 + i + 1], None, ALU.mult).then_inc(st.p_ready, 1)

            def row_copies(st, n, base):
                for j in range(TT):
                    f = st.fill(n, j)
                    if f % 2 == 0:
                        continue
                    qs = st.queries(j)
                    dve.drain()
                    dve.wait_ge(st.t_done, base(st.fills) + f + 1)
                    if n >= 2:
                        dve.wait_ge(st.pv_done, base(len(st.items)) + n - 1)
                    dve.tensor_copy(st.PT[:, n % 2, st.ptoff[j]:st.ptoff[j] + len(qs) * P],
                                    bank[4 + f % 2][:, qs[0] * P:(qs[-1] + 1) * P]).then_inc(st.copied[1], 1)

            def merged(v, s, yn, lo_t):
                gab = (ga, gb) if lo_t is ylo else (ga2, gb2)
                dve.drain().then_inc(dve_read, 1)
                v, s = v + s, 1 - s
                tile(v, s, 0)
                dve.wait_ge(S.gates_set, yn + 1)
                dve.tensor_tensor(tmp[:, 0], bank[2 * s][:, :], gab[0][:, :], ALU.mult)
                tile(v, s, 1)
                dve.tensor_tensor(tmp[:, 1], bank[2 * s + 1][:, :], gab[1][:, :], ALU.mult).then_inc(dve_read, 1)
                dve.drain()
                dve.tensor_tensor(tmp[:, 0], tmp[:, 0], tmp[:, 1], ALU.add).then_inc(S.y_set, 1)
                dve.wait_ge(S.y2_hi, yn + 1)

            dve.memset(acc[:, :], 0.0).then_inc(S.zeros_set, 1)
            dve.memset(warm[:, 1:2], 0.0).then_inc(dve_read, 2)
            dve.memset(warm[:, 2:3], 0.0).then_inc(S.y_set, 1)
            dve.memset(warm[:, 3:4], 0.0).then_inc(S.act_ready, 1)
            dve.memset(negones[:, :], -1.0).then_inc(S.negones_set, 1)
            dve.wait_ge(S.const_in, 16)
            dve.tensor_copy(ident_bf[:, :], ident)
            dve.tensor_copy(causal_bf[:, :], C("causal"))
            dve.tensor_copy(strict_bf[:, :], C("strictneg"))
            dve.wait_ge(S.gains_t, 1)
            dve.tensor_copy(gains[:, :], bank[4][:, 0:GAINS * KT]).then_inc(S.gains_set, 1)
            for k in range(KT):
                dve.wait_ge(S.start_x, k + 1)
                dve.tensor_copy(x[:, k], bank[k % 4][:, :]).then_inc(S.x_ready, 1)
            dve.wait_ge(S.table_in, 16 * TABLE_DMAS)
            dve.tensor_copy(trr[:, :], posi[:, :])
            dve.drain()
            dve.tensor_scalar(ang[:, :], trr[:, :], C("invfreq"), None, ALU.mult)
            dve.drain()

            def reduced(dst, turn, add):
                dve.tensor_scalar(trn[:, :], ang[:, :], 1.0 / TWO_PI, turn, ALU.mult, ALU.add)
                dve.drain()
                dve.tensor_scalar(trn[:, :], trn[:, :], ROUND, None, ALU.add)
                dve.drain()
                dve.tensor_scalar(trn[:, :], trn[:, :], ROUND, None, ALU.subtract)
                src = ang
                for part in TURN_PARTS:
                    dve.drain()
                    dve.scalar_tensor_tensor(dst[:, :], trn[:, :], -part, src[:, :], ALU.mult, ALU.add)
                    src = dst
                dve.drain()
                if add:
                    dve.tensor_scalar(dst[:, :], dst[:, :], add, None, ALU.add)
                    dve.drain()
                dve.tensor_scalar(dst[:, :], dst[:, :], PI_IN, -PI_IN, ALU.min, ALU.max).then_inc(S.ang_ready, 1)

            reduced(trr, 0.0, 0.0)
            reduced(ang, 0.25, TWO_PI / 4)
            dve.wait_ge(S.sin_done, 2)
            dve.tensor_scalar(sinT[:, :], sinT[:, :], C("sinsign"), None, ALU.mult)
            dve.wait_ge(S.tables_copied, 1)
            dve.drain().then_inc(S.tables_ready, 1)
            dve.wait_ge(S.toep_zero, 32)

            with dve.Fori(0, DEPTH) as l:
                v0 = l * VL
                base = lambda c, l=l: l * c
                dve.memset(vpad[:, :, :, 0:HD], 0.0)
                dve.memset(vpad[:, :, :, 2 * HD:3 * HD], 0.0)
                dve.memset(vcpad[:, :, 0:HD], 0.0)
                dve.memset(vcpad[:, :, 2 * HD:3 * HD], 0.0).then_inc(S.pads_zeroed, 1)
                pre_norm(4 * l, 2 * l)
                rope = []

                def roped(v, s, mt, scale, out, last_read):
                    r = len(rope)
                    tile(v, s, mt)
                    dve.wait_ge(S.rs_ready, 7 * l + r + 1)
                    o = dve.scalar_tensor_tensor(tmp[:, 0], bank[2 * s + mt][:, :], scale, cosT[:, :], ALU.mult, ALU.mult)
                    if last_read:
                        o.then_inc(dve_read, 1)
                    dve.tensor_tensor(tmp[:, 1], rs[:, r % 2], sinT[:, :], ALU.mult)
                    dve.drain()
                    dve.tensor_tensor(out, tmp[:, 0], tmp[:, 1], ALU.add).then_inc(S.rope_done, 1)
                    rope.append(r)

                for i in range(2):
                    for mt in range(2):
                        roped(v0, i, mt, QSCALE, nqT[:, 2 * i + mt], mt == 1)
                roped(v0 + 1, 0, 0, 1.0, kvB[:, 0], False)
                dve.drain()
                tile(v0 + 1, 0, 1)

                def with_pe(dst, src, kv, first):
                    pe_row = peT[:, bass.ds(2 * l + kv, 1), first:first + 16].broadcast_to([P, CMPL, 16])
                    return dve.tensor_tensor(dst.rearrange("p (n c) -> p n c", c=16), src.rearrange("p (n c) -> p n c", c=16), pe_row, ALU.add)

                with_pe(kvA[:, 0], kvB[:, 0], 0, 0)
                dve.drain()
                with_pe(kvB[:, 0], kvB[:, 0], 0, 16)
                with_pe(kvA[:, 1], bank[1][:, :], 1, 0)
                with_pe(kvB[:, 1], bank[1][:, :], 1, 16).then_inc(dve_read, 1)
                dve.wait_ge(S.cmp_in, 96 * (l + 1))
                dve.memset(w2pad[:, HD:2 * HD], 0.0)
                dve.tensor_copy(w2pad[:, 0:HD], w2[:, 0])
                dve.tensor_copy(w2pad[:, 2 * HD:3 * HD], w2[:, 0])
                dve.drain().then_inc(S.kvAB_ready, 1)
                roped(v0 + 1, 1, 0, 1.0, kT[:, 0], True)
                roped(v0 + 2, 0, 0, 1.0, kT[:, 1], True)
                dve.drain().then_inc(dve_read, 1)

                dve.wait_ge(S.cs_done, l + 1)
                madd = C("cmpadd").rearrange("p (o i c) -> p o i c", o=1, i=TT).broadcast_to([P, 4, TT, NCMP])
                mmul = C("cmpmul").rearrange("p (o i c) -> p o i c", o=1, i=TT).broadcast_to([P, 8, TT, NCMP])
                for b in range(2):
                    dve.tensor_tensor(cs[:, :].rearrange("p (t g i) c -> p g t i c", g=2, i=TT)[:, b],
                                      bank[b][:, :].rearrange("p (h i c) -> p h i c", h=4, i=TT)[:, :, :, 0:NCMP], madd, ALU.add)
                dve.drain()
                dve.tensor_reduce(cstat[:, 0], cs[:, :, :], AX.X, ALU.max)
                dve.drain()

                def over(k):
                    return cstat[:, k].rearrange("p (s o) -> p s o", o=1).broadcast_to([P, 32, NCMP])

                dve.tensor_tensor(cs[:, :, :], cs[:, :, :], over(0), ALU.subtract)
                dve.drain().then_inc(S.cs_masked, 1)
                dve.wait_ge(S.cs_exp, l + 1)
                dve.tensor_reduce(cstat[:, 1], cs[:, :, :], AX.X, ALU.add)
                dve.drain()
                dve.reciprocal(cstat[:, 2], cstat[:, 1])
                dve.tensor_tensor(cs[:, :, :].rearrange("p (h i) c -> p h i c", i=TT), cs[:, :, :].rearrange("p (h i) c -> p h i c", i=TT), mmul, ALU.mult)
                dve.drain()
                dve.wait_ge(S.gate_ready, l + 1)
                dve.tensor_tensor(cstat[:, 2].rearrange("p (h i) -> p h i", i=TT), cstat[:, 2].rearrange("p (h i) -> p h i", i=TT),
                                  gate[:, :, :].rearrange("p i (h b) -> p h i b", b=3)[:, :, :, 0], ALU.mult)
                dve.drain()
                dve.tensor_tensor(cs[:, :, :], cs[:, :, :], over(2), ALU.mult)
                dve.drain().then_inc(S.cs_probs, 1)

                def nsa_gate(n):
                    it = nsa.items[n]
                    return gate[:, :, 3 * it["h"] + 1 + it["b"]]

                row_max(nsa, 0, base)
                for n in range(16):
                    t = n // 4
                    if n % 4 == 0:
                        dve.wait_ge(nsa.t_done, nsa.fills * l + 18 * t + 2)
                        if t >= 1:
                            dve.wait_ge(S.cmp_pv, 4 * l + t)
                        dve.tensor_copy(pcT[:, 1], bank[5][0:NCMP, :]).then_inc(nsa.copied[1], 1)
                    if n + 1 < 16:
                        row_max(nsa, n + 1, base)
                    row_scale(nsa, n, base, nsa_gate(n))
                    row_copies(nsa, n, base)
                    if n % 4 == 3:
                        dve.wait_ge(nsa.o_hi, 4 * l + t + 1)
                        dve.tensor_tensor(onlo[:, t], bank[6 + t % 2][:, :], onhi[:, t].bitcast(f32), ALU.subtract).then_inc(nsa.o_free, 1)

                dve.memset(svp[:, :, :, HD:2 * HD], 0.0).then_inc(S.svp_zeroed, 1)
                for c in range(2):
                    for s in range(2):
                        tile(v0 + 3 + c, s, 1)
                        dve.tensor_scalar((sqT, skT)[c][:, 2 * s + 1], bank[2 * s + 1][:, :], QSCALE if c == 0 else 1.0, None, ALU.mult).then_inc(S.sqk_dve, 1)
                        dve.drain().then_inc(dve_read, 1)
                for s in range(2):
                    tile(v0 + 5, s, 1)
                    for hf in range(2):
                        o = dve.tensor_copy(svp[:, s, 4:8, 2 * HD * hf:2 * HD * hf + HD],
                                            bank[2 * s + 1][:, :].rearrange("p (a h c) -> p a h c", a=4, h=2)[:, :, hf])
                    o.then_inc(S.sqk_dve, 1)
                    dve.drain().then_inc(dve_read, 1)

                Z = ((0, 512), (512, 512), (1024, 256))

                def sb_softplus(h):
                    dve.drain()
                    dve.wait_ge(S.l_done, 8 * l + h + 1)
                    if h >= 2:
                        dve.wait_ge(S.arg_done, 8 * l + h - 1)
                    for b, (c0, w) in enumerate(Z):
                        dve.scalar_tensor_tensor(sL[:, h % 2, c0:c0 + w], bank[3 * (h % 2) + b][:, 0:w], 0.0, sE[:, c0:c0 + w], ALU.max, ALU.add)
                    dve.drain()
                    for at in (0, 512, 896, 1024):
                        o = dve.tensor_tensor(sL[:, h % 2, at:at + P], sL[:, h % 2, at:at + P], C("strict01"), ALU.mult)
                    o.then_inc(S.L_ready, 1)

                for h in range(8):
                    sb_softplus(h)
                    if h % 2 == 0 and h >= 2:
                        t = h // 2 - 1
                        dve.wait_ge(S.so_hi, 4 * l + t + 1)
                        dve.tensor_tensor(oslo[:, t], bank[6 + t % 2][:, :], oshi[:, t].bitcast(f32), ALU.subtract).then_inc(S.so_lo, 1)
                dve.wait_ge(S.so_hi, 4 * l + 4)
                dve.tensor_tensor(oslo[:, 3], bank[7][:, :], oshi[:, 3].bitcast(f32), ALU.subtract).then_inc(S.so_lo, 1)

                with dve.Fori(0, KT) as m:
                    merged(v0 + 6 + m, 0, 8 * l + m, ylo)
                    dve.tensor_tensor(ylo[:, bass.ds(m, 1)].rearrange("p o t -> p (o t)"), tmp[:, 0],
                                      yhi[:, bass.ds(m, 1)].rearrange("p o t -> p (o t)").bitcast(f32), ALU.subtract).then_inc(S.y_ready, 1)
                out_proj(v0 + 14, 0, 4 * l + 1)
                post_norm(4 * l + 1, 1.0)
                pre_norm(4 * l + 2, 2 * l + 1)

                with dve.Fori(0, FH) as i:
                    for s in range(2):
                        v = v0 + 16 + i
                        f = 2 * i + s
                        for mt, dst in ((0, tg), (1, tu)):
                            tile(v, s, mt)
                            at = 176 * l + f + FT * mt
                            dve.wait_ge(S.aff_done, 2 * FT * l + 2 * f + mt + 1)
                            ps = bank[2 * s + mt]
                            dve.scalar_tensor_tensor(dst[:, 0, 1:T], ps[:, 0:T - 1], convc[:, bass.ds(at + 44, 1)], dst[:, 0, 1:T], ALU.mult, ALU.add)
                            dve.drain()
                            o = dve.scalar_tensor_tensor(dst[:, 0, 2:T], ps[:, 0:T - 2], convc[:, bass.ds(at, 1)], dst[:, 0, 2:T], ALU.mult, ALU.add)
                            o.then_inc(S.conv_done, 1)
                        dve.drain().then_inc(dve_read, 1)
                        dve.wait_ge(S.gelu_done, FT * l + f + 1)
                        dve.tensor_tensor(tu[:, 1], tg[:, 1], tu[:, 0], ALU.mult).then_inc(S.act_mul, 1)
                        dve.wait_ge(S.act_hi_done, FT * l + f + 1)
                        dve.tensor_tensor(a1lo[:, bass.ds(f, 1)].rearrange("p o t -> p (o t)"), tu[:, 1],
                                          a1hi[:, bass.ds(f, 1)].rearrange("p o t -> p (o t)").bitcast(f32), ALU.subtract).then_inc(S.act_ready, 1)
                dve.memset(acc[:, :], 0.0)
                down(v0 + 27, 0, 4 * l + 3)
                post_norm(4 * l + 3, 1.0)

            v2 = DEPTH * VL
            zero = lambda c: 0

            def ffn2(u0, n, m, f0):
                pre_norm(n, m)
                with dve.Fori(0, FH) as i:
                    for q in range(2):
                        v, s = v2 + i + (u0 + q) // 2, (u0 + q) % 2
                        f = f0 + 2 * i + q
                        tile(v, s, 1)
                        dve.wait_ge(S.gelu_done, f + 1)
                        dve.tensor_tensor(tu[:, 1], bank[2 * s + 1][:, :], tg[:, 0], ALU.mult).then_inc(S.act_mul, 1)
                        dve.drain().then_inc(dve_read, 1)
                        dve.wait_ge(S.act_hi_done, f + 1)
                        dve.tensor_tensor(a2lo[:, bass.ds(2 * i + q, 1)].rearrange("p o t -> p (o t)"), tu[:, 1],
                                          a2hi[:, bass.ds(2 * i + q, 1)].rearrange("p o t -> p (o t)").bitcast(f32), ALU.subtract).then_inc(S.act_ready, 1)
                dve.memset(acc[:, :], 0.0)

            ffn2(0, 8, 4, DEPTH * FT)
            down(v2 + 11, 0, 9)
            post_norm(9, 0.5)
            pre_norm(10, 5)

            dve.memset(avp[:, :, :, HD:2 * HD], 0.0).then_inc(S.avp_zeroed, 1)
            for c in range(2):
                for s in range(2):
                    tile(v2 + 19 + c, s, 1)
                    dve.tensor_scalar((aqT, akT)[c][:, 2 * s + 1], bank[2 * s + 1][:, :], QSCALE if c == 0 else 1.0, None, ALU.mult).then_inc(S.aqk_dve, 1)
                    dve.drain().then_inc(dve_read, 1)
            for s in range(2):
                tile(v2 + 21, s, 1)
                for hf in range(2):
                    o = dve.tensor_copy(avp[:, s, 4:8, 2 * HD * hf:2 * HD * hf + HD],
                                        bank[2 * s + 1][:, :].rearrange("p (a h c) -> p a h c", a=4, h=2)[:, :, hf])
                o.then_inc(S.aqk_dve, 1)
                dve.drain().then_inc(dve_read, 1)
            dve.wait_ge(S.const2_in, 16)

            def na_max(n):
                tb = tab[:, n % 2]
                dve.wait_ge((S.tab_in0, S.tab_in1)[n % 2], 32 * (n // 2 + 1))
                tv = tb.rearrange("p (u c) -> p u c", u=14)
                dve.tensor_tensor(tv, tv, C2("colmask").rearrange("p (o c) -> p o c", o=1).broadcast_to([P, 14, HD]), ALU.add)
                dve.drain()
                row_max(na, n, zero, table=tb)
                dve.drain().then_inc(S.tab_used, 1)

            na_max(0)
            for n in range(8):
                if n + 1 < 8:
                    na_max(n + 1)
                row_scale(na, n, zero)
                row_copies(na, n, zero)
                if n % 2 == 1:
                    t = n // 2
                    dve.wait_ge(na.o_hi, t + 1)
                    dve.tensor_tensor(oalo[:, t], bank[6 + t % 2][:, :], oahi[:, t].bitcast(f32), ALU.subtract).then_inc(na.o_free, 1)

            dve.memset(zeros_bf[:, :], 0.0)
            dve.memset(bvp[:, :, HD:2 * HD], 0.0).then_inc(S.bvp_zeroed, 1)
            for g, st in enumerate(DIL):
                dil = ORDER[g]
                for c in range(3):
                    u = 44 + 3 * g + c
                    v, s = v2 + u // 2, u % 2
                    tile(v, s, 1)
                    if c < 2:
                        dve.tensor_scalar((bqT, bkT)[c][:, 1].rearrange("p (r l) -> p r l", r=dil),
                                          bank[2 * s + 1][:, :].rearrange("p (l r) -> p r l", r=dil),
                                          QSCALE if c == 0 else 1.0, None, ALU.mult).then_inc(S.bqk_dve, 1)
                    else:
                        for hf in range(2):
                            o = dve.tensor_copy(bvp[:, 4:8, 2 * HD * hf:2 * HD * hf + HD],
                                                bank[2 * s + 1][:, :].rearrange("p (a h c) -> p a h c", a=4, h=2)[:, :, hf])
                        o.then_inc(S.bqk_dve, 1)
                    dve.drain().then_inc(dve_read, 1)
                dist = C2(f"dist{g}")
                row_max(st, 0, zero, slopes=(dist, SLOPES[4 * g], g == 0))
                for n in range(4):
                    if n + 1 < 4:
                        row_max(st, n + 1, zero, slopes=(dist, SLOPES[4 * g + n + 1], g == 0))
                    row_scale(st, n, zero)
                    row_copies(st, n, zero)
            dve.wait_ge(S.ln_done, 1)
            dve.tensor_tensor(lse[:, :], lse[:, :], bstat[:, 0, :], ALU.subtract).then_inc(S.lse_ready, 1)
            dve.wait_ge(S.lseT_ready, 1)
            dve.tensor_tensor(mz[:, 0], lseT[:, 0], lseT[:, 1], ALU.max)
            dve.drain()
            dve.tensor_tensor(mz[:, 0], mz[:, 0], lseT[:, 2], ALU.max)
            dve.drain()
            for g in range(3):
                o = dve.tensor_tensor(alp[:, g], lseT[:, g], mz[:, 0], ALU.subtract)
            o.then_inc(S.mx_ready, 1)
            dve.wait_ge(S.aexp_done, 1)
            dve.tensor_tensor(mz[:, 1], alp[:, 0], alp[:, 1], ALU.add)
            dve.drain()
            dve.tensor_tensor(mz[:, 1], mz[:, 1], alp[:, 2], ALU.add)
            dve.drain()
            dve.reciprocal(mz[:, 0], mz[:, 1])
            dve.drain()
            for g in range(3):
                o = dve.tensor_tensor(alp[:, g], alp[:, g], mz[:, 0], ALU.mult)
            o.then_inc(S.alpha_ready, 1)
            dve.wait_ge(S.ob_copied, 6)
            for t in range(6):
                dve.wait_ge(S.alpha_b, t + 1)
                dve.tensor_tensor(ob[:, t], ob[:, t], bank[t % 2][:, :], ALU.mult).then_inc(S.alpha_used, 1)
                dve.wait_ge(S.ob_hi, t + 1)
                dve.tensor_tensor(oblo[:, t], ob[:, t], obhi[:, t].bitcast(f32), ALU.subtract).then_inc(S.ob_ready, 1)

            with dve.Fori(0, KT) as m:
                merged(v2 + 26 + m, 1, 8 * DEPTH + m, y2lo)
                dve.tensor_tensor(y2lo[:, bass.ds(m, 1)].rearrange("p o t -> p (o t)"), tmp[:, 0],
                                  y2hi[:, bass.ds(m, 1)].rearrange("p o t -> p (o t)").bitcast(f32), ALU.subtract).then_inc(S.y_ready, 1)
            out_proj(v2 + 34, 1, 11)
            post_norm(11, 1.0)
            ffn2(73, 12, 6, DEPTH * FT + FT)
            down(v2 + 47, 1, 13)
            post_norm(13, 0.5)
            for i in range(TT):
                dve.wait_ge(S.out_t, 2 * i + 2)
                dve.tensor_copy(ostage[:, i, 512:1024], bank[(2 * i + 1) % 4][:, :]).then_inc(S.out_cd, 1)

        @block.tensor
        def _(pe):
            wh = [whi[:, s, :] for s in range(2)]
            wl = [wlo[:, s, :] for s in range(2)]

            def opened(v, s):
                pe.wait_ge(lo_ready, 2 * v + s + 3)
                pe.wait_ge(dve_read, 2 * v + s + 1)

            def three(out, wt, inp, start, stop, swap=False):
                for a, b, first, last in ((0, 0, True, False), (0, 1, False, False), (1, 0, False, True)):
                    l, r = (inp[a], wt[b]) if swap else (wt[a], inp[b])
                    o = pe.matmul(out, l, r, start=start and first, stop=stop and last)
                return o

            def cols(s, pattern, k, c0, n, **sizes):
                return [w[s].rearrange("p (k c) -> p k c", k=pattern)[:, k, c0:c0 + n] for w in (wh, wl)]

            def dense(v, s, inp, nk, width, tiles, ready=None):
                opened(v, s)
                for b, ks, c0 in tiles:
                    for j, (k, ki) in enumerate(ks):
                        if ready is not None:
                            ready(ki)
                        wt = [w[s][:, k * width + c0:k * width + c0 + P] for w in (wh, wl)]
                        o = three(bank[b][:, :], wt, [inp[0][:, ki], inp[1][:, ki]], j == 0, j == len(ks) - 1)
                    o.then_inc(tile_done, 1)

            H = (hh, hl)

            def two_tiles(v, s, inp=H, ready=None):
                ks = [(k, k) for k in range(KT)]
                dense(v, s, inp, KT, 256, [(2 * s, ks, 0), (2 * s + 1, ks, P)], ready)

            def tokens_major(v, s, n, c0, outs, order=None):
                for i in range(TT):
                    b, at = outs(i)
                    for k in range(KT):
                        inp = [(t[:, k, i * P:(i + 1) * P] if order is None else order(t, k, i)) for t in H]
                        wt = [w[s][:, k * 256 + c0:k * 256 + c0 + n] for w in (wh, wl)]
                        o = three(bank[b][:, at:at + n], wt, inp, k == 0, k == KT - 1, swap=True)
                    yield i, o

            def v_tiles(v, s, order=None):
                opened(v, s)
                for i, o in tokens_major(v, s, 256, 0, lambda i: (2 * s + i // 2, (i % 2) * 256), order):
                    if i % 2 == 1:
                        o.then_inc(tile_done, 1)

            def variance(n):
                pe.wait_ge(S.sq_used, KT * n + KT)
                pe.matmul(NORM[:, :], negones[:, :], acc[:, :], start=True, stop=True).then_inc(S.var_done, 1)

            def h_tiles(m):
                return lambda k: pe.wait_ge(S.h_ready, KT * m + k + 1)

            def down(v, s0, hi_t, lo_t, hidden):
                with pe.Fori(0, KT // 2) as i:
                    pe.wait_ge(S.act_ready, hidden + 1)
                    for q in range(2):
                        for half in range(2):
                            vv, s = v + 2 * i + (s0 + 2 * q + half) // 2, (s0 + half) % 2
                            opened(vv, s)
                            b = (2 * s0 + 2 * q) % 4
                            for j in range(FH):
                                wt = [w[s][:, j * P:(j + 1) * P] for w in (wh, wl)]
                                kk = half * FH + j
                                o = three(bank[b][:, :], wt, [hi_t[:, kk], lo_t[:, kk]], kk == 0, kk == FT - 1)
                                if j >= FH - 2:
                                    o.then_inc(tile_done, 1)

            def scores(st, n, base, q, k, causal):
                for i in range(TT):
                    lo, hi = st.keys(i)
                    w = (hi - lo) * P
                    a = TT * n + i
                    if a >= 3:
                        pe.wait_ge(st.exp_done if causal else st.bias_done, base(st.scores) + a - 2)
                    if not causal:
                        o = pe.matmul(bank[a % 3][:, 0:w], q(i), k(lo * P, hi * P), start=True, stop=True)
                    else:
                        if i > 0:
                            pe.matmul(bank[a % 3][:, 0:i * P], q(i), k(0, i * P), start=True, stop=True)
                        pe.matmul(bank[a % 3][:, i * P:w], q(i), k(i * P, w), start=True, stop=False)
                        o = pe.matmul(bank[a % 3][:, i * P:w], ident_bf[:, :], causal_bf[:, :], start=False, stop=True)
                    o.then_inc(st.s_done, 1)

            def free_fill(st, base, f):
                if f >= 2:
                    pe.wait_ge(st.copied[f % 2], base(st.fills // 2) + f // 2)

            def transposes(st, n, base):
                for j in range(TT):
                    f = st.fill(n, j)
                    free_fill(st, base, f)
                    qs = st.queries(j)
                    pe.wait_ge(st.p_ready, base(st.scores) + TT * n + qs[-1] + 1)
                    for i in qs:
                        at = st.off[i] + (j - st.keys(i)[0]) * P
                        o = pe.transpose(bank[4 + f % 2][:, i * P:(i + 1) * P], st.P[:, n % 2, at:at + P], ident)
                    o.then_inc(st.t_done, 1)

            def times_v(st, n, base, vt, obank, start=False, stop=False):
                for j in (0, 1, 2, 3) if start else (1, 2, 3, 0):
                    f = st.fill(n, j)
                    qs = st.queries(j)
                    pe.wait_ge(st.copied[f % 2], base(st.fills // 2) + f // 2 + 1)
                    w = len(qs) * P
                    o = pe.matmul(bank[obank][:, qs[0] * P:qs[0] * P + w], vt(j), st.PT[:, n % 2, st.ptoff[j]:st.ptoff[j] + w],
                                  start=start and j == 0, stop=stop and j == 0)
                o.then_inc(st.pv_done, 1)

            def add_zeros(b, start):
                return pe.matmul(bank[b][:, :], zeros_bf[:, 0:P], zeros_bf[:, :], start=start, stop=not start)

            pe.wait_ge(S.const_in, 16)
            pe.wait_ge(S.start_in, 16 * (TT + GAINS))
            pe.transpose(bank[4][:, 0:GAINS * KT], grows[:, :], ident[0:GAINS * KT, 0:GAINS * KT]).then_inc(S.gains_t, 1)
            for k in range(KT):
                if k >= 4:
                    pe.wait_ge(S.x_ready, k - 3)
                for i in range(TT):
                    o = pe.transpose(bank[k % 4][:, i * P:(i + 1) * P], xin[:, i, k * P:(k + 1) * P], ident)
                o.then_inc(S.start_x, 1)
            pe.wait_ge(S.table_in, 16 * TABLE_DMAS)
            for a in range(2 * DEPTH):
                pe.transpose(bank[6][:, a * CMPL:(a + 1) * CMPL], perows[:, a, :], ident[0:CMPL, 0:CMPL])
            for c in range(4):
                o = pe.transpose(bank[7][:, 88 * c:88 * (c + 1)], crows[:, c, :], ident[0:88, 0:88])
            o.then_inc(S.tables_t, 1)
            with pe.Fori(0, DEPTH) as l:
                pe.wait_ge(S.negones_set, 1)
                v0 = l * VL
                base = lambda c, l=l: l * c
                variance(4 * l)
                for i in range(2):
                    two_tiles(v0, i, H, h_tiles(2 * l) if i == 0 else None)
                two_tiles(v0 + 1, 0)
                for v, s in ((v0 + 1, 1), (v0 + 2, 0)):
                    ks = [(k, k) for k in range(KT)]
                    dense(v, s, H, KT, 256, [(2 * s, ks, 0)])
                    for i, o in tokens_major(v, s, P, P, lambda i: (2 * s + 1, i * P)):
                        pass
                    o.then_inc(tile_done, 1)
                pe.wait_ge(S.kvAB_ready, l + 1)
                opened(v0 + 2, 1)
                for i, o in tokens_major(v0 + 2, 1, 24, 0, lambda i: (2, i * 24)):
                    if i >= 2:
                        o.then_inc(tile_done, 1)

                for kv in range(2):
                    for g in range(2):
                        rows = slice(g * HD, (g + 1) * HD)
                        for p in range(CMPL):
                            src = (kvA if p < 16 else kvB)[rows, kv].rearrange("p (n c) -> p n c", c=16)
                            src = src[:, 0:NCMP, p] if p < 16 else src[:, 1:NCMP + 1, p - 16]
                            o = pe.matmul(bank[6 + g][0:HD, kv * 64:kv * 64 + NCMP], w1[rows, kv, p, :], src,
                                          start=p == 0, stop=p == CMPL - 1)
                    o.then_inc(S.cmp_hid, 1)
                pe.wait_ge(S.cmp_act, 2 * l + 2)
                for g in range(2):
                    pe.matmul(bank[4][:, 0:NCMP], w2pad[:, g * HD:g * HD + P], hid[:, 0, g * NCMP:(g + 1) * NCMP], start=g == 0, stop=g == 1)
                for g in range(2):
                    o = pe.matmul(bank[4][0:NCMP, 64 + g * HD:128 + g * HD], hid[:, 1, g * NCMP:(g + 1) * NCMP], w2[:, 1, :], start=True, stop=True)
                o.then_inc(S.cmp_out, 1)

                def nsa_q(h, i):
                    return nqT[(h % 2) * HD:(h % 2 + 1) * HD, h // 2, i * P:(i + 1) * P]

                pe.wait_ge(S.cmp_ready, l + 1)
                pe.wait_ge(dve_read, UL * l + 8)
                pe.wait_ge(S.k_exchanged, l + 1)
                for h in range(8):
                    rows = slice((h % 2) * HD, (h % 2 + 1) * HD)
                    for i in range(TT):
                        at = ((h // 2) * TT + i) * 32
                        o = pe.matmul(bank[h % 2][:, at:at + NCMP], nsa_q(h, i), kcT[rows, int(h % 2 != h // 4)], start=True, stop=True)
                o.then_inc(S.cs_done, 1)
                pe.wait_ge(S.cs_masked, l + 1)

                def nsa_scores(n):
                    it = nsa.items[n]
                    g = it["h"] // 4
                    hf = it["h"] % 2
                    keys = kT[hf * HD:(hf + 1) * HD, it["b"] + (2 if hf != g else 0)]
                    scores(nsa, n, base, lambda i: nsa_q(it["h"], i), lambda a, b: keys[:, a:b], True)

                nsa_scores(0)
                pe.wait_ge(S.cs_probs, l + 1)
                pe.wait_ge(S.v_ready, 2 * l + 2)
                for n in range(16):
                    t, it = n // 4, nsa.items[n]
                    ob_bank = 6 + t % 2
                    if n % 4 == 0:
                        for hf in range(2):
                            f = 18 * t + hf
                            free_fill(nsa, base, f)
                            for i in range(TT):
                                o = pe.transpose(bank[4 + f % 2][0:NCMP, i * P:(i + 1) * P], cs[:, (2 * t + hf) * TT + i, :], ident)
                            o.then_inc(nsa.t_done, 1)
                        if t >= 2:
                            pe.wait_ge(nsa.o_free, 4 * l + t - 1)
                        for hf in range(2):
                            f = 18 * t + hf
                            pe.wait_ge(nsa.copied[hf], 36 * l + f // 2 + 1)
                            o = pe.matmul(bank[ob_bank][:, :], vcpad[:, t // 2, (1 - hf) * HD:(1 - hf) * HD + P], pcT[:, hf], start=hf == 0, stop=False)
                        o.then_inc(S.cmp_pv, 1)
                    if n + 1 < 16:
                        nsa_scores(n + 1)
                    transposes(nsa, n, base)
                    hf, g = it["h"] % 2, it["h"] // 4
                    times_v(nsa, n, base, lambda j: vpad[:, it["b"], 2 * j + g, (1 - hf) * HD:(1 - hf) * HD + P], ob_bank, False, n % 4 == 3)

                for c in range(2):
                    for s in range(2):
                        two_tiles(v0 + 3 + c, s)
                for s in range(2):
                    v_tiles(v0 + 5, s)
                pe.wait_ge(S.sqk_act, 6 * l + 6)
                pe.wait_ge(S.sqk_dve, 6 * l + 6)
                pe.wait_ge(nsa.o_free, 4 * l + 4)
                ZAT = {0: (0, 0, 0), 1: (1, 0, 512), 3: (1, 384, 896), 2: (2, 0, 1024)}

                def z_tile(h, j, stop):
                    rows, t = slice((h % 2) * HD, (h % 2 + 1) * HD), h // 2
                    b, c0, _ = ZAT[j]
                    return pe.matmul(bank[3 * (h % 2) + b][:, c0:c0 + T - j * P], skT[rows, t, j * P:(j + 1) * P],
                                     sqT[rows, t, j * P:T], start=True, stop=stop)

                def z_scores(h):
                    if h >= 2:
                        pe.wait_ge(S.w_ready, 8 * l + h - 1)
                    for j in (0, 1, 3, 2):
                        o = z_tile(h, j, True)
                    o.then_inc(S.z_done, 1)

                def z_minus_sums(h):
                    pe.wait_ge(S.L_ready, 8 * l + h + 1)
                    L = sL[:, h % 2]
                    for j in (0, 1, 3, 2):
                        b, c0, a0 = ZAT[j]
                        zb = bank[3 * (h % 2) + b]
                        w = T - j * P
                        z_tile(h, j, False)
                        pe.matmul(zb[:, c0:c0 + P], ident_bf[:, :], strict_bf[:, :], start=False, stop=False)
                        for j2 in range(j + 1, TT):
                            _, _, a2 = ZAT[j2]
                            w2_ = T - j2 * P
                            pe.matmul(zb[:, c0 + w - w2_:c0 + w], negones[:, :], L[:, a2:a2 + w2_], start=False, stop=False)
                        o = pe.matmul(zb[:, c0:c0 + w], C("negtri"), L[:, a0:a0 + w], start=False, stop=True)
                    o.then_inc(S.arg_done, 1)

                z_scores(0)
                for h in range(8):
                    if h + 1 < 8:
                        z_scores(h + 1)
                    z_minus_sums(h)
                    t, hf = h // 2, h % 2
                    if hf == 0 and t >= 2:
                        pe.wait_ge(S.so_lo, 4 * l + t - 1)
                    pe.wait_ge(S.w_ready, 8 * l + h + 1)
                    for j in (1, 2, 3, 0) if hf else (0, 1, 2, 3):
                        a0 = ZAT[j][2]
                        o = pe.matmul(bank[6 + t % 2][:, j * P:T], svp[:, t // 2, 2 * j + t % 2, hf * HD:hf * HD + P],
                                      sW[:, hf, a0:a0 + T - j * P], start=hf == 0 and j == 0, stop=hf == 1 and j == 0)
                    o.then_inc(S.spv_done, 1)

                with pe.Fori(0, KT) as m:
                    pe.wait_ge(S.w_ready, 8 * l + 8)
                    two_tiles(v0 + 6 + m, 0)
                    pe.wait_ge(S.so_lo, 4 * l + 4)
                    opened(v0 + 6 + m, 1)
                    for b, src in enumerate(((onhi, onlo), (oshi, oslo))):
                        for k in range(4):
                            wt = [w[1][:, (4 * b + k) * P:(4 * b + k + 1) * P] for w in (wh, wl)]
                            o = three(bank[2 + b][:, :], wt, [src[0][:, k], src[1][:, k]], k == 0, k == 3)
                        o.then_inc(tile_done, 1)
                for i in range(4):
                    two_tiles(v0 + 14 + i // 2, i % 2, (yhi, ylo), (lambda k: pe.wait_ge(S.y_ready, 8 * l + k + 1)) if i == 0 else None)
                variance(4 * l + 1)
                variance(4 * l + 2)
                with pe.Fori(0, FH) as i:
                    pe.wait_ge(S.h_ready, KT * (2 * l + 2))
                    for s in range(2):
                        two_tiles(v0 + 16 + i, s)
                down(v0 + 27, 0, a1hi, a1lo, FT * (l + 1))
                variance(4 * l + 3)

            v2 = DEPTH * VL
            zero = lambda c: 0

            def ffn2_up(u0, n, m):
                variance(n)
                with pe.Fori(0, FH) as i:
                    pe.wait_ge(S.h_ready, KT * (m + 1))
                    for q in range(2):
                        two_tiles(v2 + i + (u0 + q) // 2, (u0 + q) % 2)

            ffn2_up(0, 8, 4)
            down(v2 + 11, 0, a2hi, a2lo, FT * (DEPTH + 1))
            variance(9)
            variance(10)
            for c in range(2):
                for s in range(2):
                    two_tiles(v2 + 19 + c, s, H, h_tiles(5) if c == 0 and s == 0 else None)
            for s in range(2):
                v_tiles(v2 + 21, s)
            pe.wait_ge(S.aqk_act, 6)
            pe.wait_ge(S.aqk_dve, 6)

            def na_scores(n):
                rows, t = slice((n % 2) * HD, (n % 2 + 1) * HD), n // 2
                scores(na, n, zero, lambda i: aqT[rows, t, i * P:(i + 1) * P], lambda a, b: akT[rows, t, a:b], False)

            na_scores(0)
            for n in range(8):
                if n + 1 < 8:
                    na_scores(n + 1)
                transposes(na, n, zero)
                t, hf = n // 2, n % 2
                if hf == 0 and t >= 2:
                    pe.wait_ge(na.o_free, t - 1)
                times_v(na, n, zero, lambda j: avp[:, t // 2, 2 * j + t % 2, hf * HD:hf * HD + P], 6 + t % 2, hf == 0, hf == 1)

            for g, st in enumerate(DIL):
                if g == 0:
                    pe.wait_ge(na.o_free, 4)
                else:
                    pe.wait_ge(S.ob_copied, 2 * g)
                    pe.wait_ge(DIL[g - 1].bias_done, 16)
                dil = ORDER[g]

                def place(t, k, i):
                    if dil == 1:
                        return t[:, k, i * P:(i + 1) * P]
                    by = t[:, k].rearrange("p (l r) -> p r l", r=dil)
                    return by[:, i * dil // TT:(i + 1) * dil // TT, :]

                for c in range(3):
                    u = 44 + 3 * g + c
                    v, s = v2 + u // 2, u % 2
                    if c < 2:
                        two_tiles(v, s)
                    else:
                        v_tiles(v, s, place)
                pe.wait_ge(S.bqk_act, 3 * g + 3)
                pe.wait_ge(S.bqk_dve, 3 * g + 3)

                def dil_scores(n):
                    rows, t = slice((n % 2) * HD, (n % 2 + 1) * HD), n // 2
                    scores(st, n, zero, lambda i: bqT[rows, t, i * P:(i + 1) * P], lambda a, b: bkT[rows, t, a:b], False)

                dil_scores(0)
                for n in range(4):
                    if n + 1 < 4:
                        dil_scores(n + 1)
                    transposes(st, n, zero)
                    t, hf = n // 2, n % 2
                    if hf == 0:
                        add_zeros(6 + t, True)
                    times_v(st, n, zero, lambda j: bvp[:, 2 * j + t, hf * HD:hf * HD + P], 6 + t)
                    if hf == 1:
                        add_zeros(6 + t, False).then_inc(S.ob_done, 1)
            pe.wait_ge(S.lse_ready, 1)
            for g in range(3):
                for i in range(TT):
                    o = pe.transpose(bank[g][0:4, i * P:(i + 1) * P],
                                     lse[:, 16 * g:16 * g + 16].rearrange("p (h i) -> p i h", i=TT)[:, i], ident)
            o.then_inc(S.lseT_done, 1)
            pe.wait_ge(S.alpha_ready, 1)
            for t in range(6):
                if t >= 2:
                    pe.wait_ge(S.alpha_used, t - 1)
                pe.matmul(bank[t % 2][:, :], C2("sel")[0:4, (t % 2) * P:(t % 2 + 1) * P], alp[:, t // 2], start=True, stop=True).then_inc(S.alpha_b, 1)
            with pe.Fori(0, KT) as m:
                pe.wait_ge(S.ob_ready, 6)
                two_tiles(v2 + 26 + m, 1)
                opened(v2 + 27 + m, 0)
                at = 0
                for b, (src, nk) in enumerate((((oahi, oalo), 4), ((obhi, oblo), 6))):
                    for k in range(nk):
                        wt = [w[0][:, (at + k) * P:(at + k + 1) * P] for w in (wh, wl)]
                        o = three(bank[b][:, :], wt, [src[0][:, k], src[1][:, k]], k == 0, k == nk - 1)
                    at += nk
                    o.then_inc(tile_done, 1)
            for i in range(4):
                two_tiles(v2 + 34 + (1 + i) // 2, (1 + i) % 2, (y2hi, y2lo), (lambda k: pe.wait_ge(S.y_ready, 8 * DEPTH + k + 1)) if i == 0 else None)
            variance(11)
            ffn2_up(73, 12, 6)
            down(v2 + 47, 1, a2hi, a2lo, FT * (DEPTH + 2))
            variance(13)
            for i in range(TT):
                for b in range(2):
                    if i >= 2:
                        pe.wait_ge((S.out_ca, S.out_cd)[b], i - 1)
                    for k in range(4):
                        kk = 4 * b + k
                        if i == 0:
                            pe.wait_ge(S.x_ready, KT * 7 + kk + 1)
                        o = pe.transpose(bank[(2 * i + b) % 4][:, k * P:(k + 1) * P], x[:, kk, i * P:(i + 1) * P], ident)
                    o.then_inc(S.out_t, 1)


def kernel(**inputs):
    import concourse.bacc as bacc
    from concourse.bass_utils import run_bass_kernel_spmd

    nc = bacc.Bacc("TRN2", target_bir_lowering=False, num_devices=1)
    arrays, args = {}, {}
    for name, a in inputs.items():
        arrays[f"in_{name}"] = np.ascontiguousarray(a)
        args[name] = nc.dram_tensor(f"in_{name}", arrays[f"in_{name}"].shape, mybir.dt.from_np(arrays[f"in_{name}"].dtype), kind="ExternalInput").ap()
    arrays["shape_consts"], arrays["shape_consts2"] = shape_constants()
    consts = [nc.dram_tensor(n, arrays[n].shape, mybir.dt.float32, kind="ExternalInput").ap() for n in ("shape_consts", "shape_consts2")]
    toep = nc.dram_tensor("toeplitz_tables", (120 * TOEP + TOEP_PAD,), mybir.dt.float32, kind="Internal").ap()
    out = nc.dram_tensor("out_0", (1, T, D), mybir.dt.float32, kind="ExternalOutput").ap()
    build(nc, args, *consts, toep, out)
    return run_bass_kernel_spmd(nc, [arrays], core_ids=[0]).results[0]["out_0"]
```

```python
import concourse.bass as bass
from concourse import mybir
from contextlib import ExitStack
import numpy as np

P = 128
T = 512
D = 1024
KT = D // P
TT = T // P
HD = 64
FF = 2816
FT = FF // P
FH = FT // 2
DEPTH = 2
NCMP = 31
CMPL = 32
EPS = 1e-6
NEG = -1e30
FAR = 1e32
QSCALE = HD ** -0.5
NBH = 12
SLOPES = [float(np.exp2(np.float32(-8.0 * (h + 1.0) / NBH))) for h in range(NBH)]
UL = 70
VL = UL // 2
UNITS = DEPTH * UL + 111
def _columns(parts):
    cols, at = {}, 0
    for name, n in parts:
        cols[name] = (at, n)
        at += n
    return cols, at


CONST_COLS, CONST_N = _columns((("ident", P), ("negtri", P), ("causal", P), ("strictneg", P), ("strict01", P),
                                ("cmpadd", TT * NCMP), ("cmpmul", TT * NCMP), ("invfreq", 1), ("sinsign", 1)))
CONST2_COLS, CONST2_N = _columns((("dist0", 3 * P), ("dist1", P), ("dist2", P), ("colmask", HD), ("sel", 2 * P)))
ORDER = (1, 4, 4)
TOEP = 65 * 64
TOEP_AT, TOEP_PAD = 16, 64
GAINS = 14
CONVN = DEPTH * 4 * 2 * FT
TABLE_DMAS = DEPTH * (4 + 2 * 3)
TWO_PI = 2 * np.pi
TURN_PARTS = (6.28125, 0.0019340515136718750, 2 * np.pi - 6.28125 - 0.0019340515136718750)
ROUND = 1.5 * 2.0 ** 23
PI_IN = 3.1415925


def shape_constants():
    c, c2 = np.zeros((P, CONST_N), np.float32), np.zeros((P, CONST2_N), np.float32)

    def put(name, a):
        to, (at, n) = (c, CONST_COLS[name]) if name in CONST_COLS else (c2, CONST2_COLS[name])
        to[:a.shape[0], at:at + n] = a

    r = np.arange(P)
    put("ident", np.eye(P))
    put("negtri", np.where(r[:, None] >= r[None, :], -1.0, 0.0))
    put("causal", np.where(r[None, :] <= r[:, None], 0.0, NEG))
    put("strictneg", np.where(r[:, None] < r[None, :], 0.0, NEG))
    put("strict01", np.where(r[:, None] < r[None, :], 1.0, 0.0))
    rel = np.abs(np.arange(3 * P)[None, :] - P - r[:, None])
    put("dist0", np.where(rel <= 64, rel, FAR))
    rel = np.abs(r[None, :] - r[:, None])
    put("dist1", np.where(rel <= 64, 4 * rel, FAR))
    put("dist2", np.where(rel % 4 == 0, 4 * rel, FAR))
    tok = (np.arange(TT) * P)[None, :, None] + r[:, None, None]
    ok = (np.arange(NCMP) * 16 + CMPL - 1)[None, None, :] <= tok
    put("cmpadd", np.where(ok, 0.0, NEG).reshape(P, -1))
    put("cmpmul", ok.astype(np.float32).reshape(P, -1))
    col = r % 64
    first = np.clip(col - 8, 0, 48)
    cw = np.arange(64)[None, :]
    put("colmask", np.where((cw >= first[:, None]) & (cw < first[:, None] + 16), 0.0, NEG))
    half = np.arange(32, dtype=np.float32) / np.float32(32)
    put("invfreq", np.power(np.float32(10000.0), -half).astype(np.float32)[r % 32][:, None])
    put("sinsign", np.where(r % 64 < 32, -1.0, 1.0)[:, None])
    sel = np.zeros((4, 2, P), np.float32)
    for h in range(4):
        sel[h, h // 2, (h % 2) * 64:(h % 2) * 64 + 64] = 1.0
    put("sel", sel.reshape(4, 2 * P))
    return c, c2


SB_STEPS = {3: 6, 9: 7}


def build(nc, A, consts, consts2, toep, out):
    f32, f32r, bf16, i32 = mybir.dt.float32, mybir.dt.float32r, mybir.dt.bfloat16, mybir.dt.int32
    ALU = mybir.AluOpType
    ACT = mybir.ActivationFunctionType
    AX = mybir.AxisListType
    ctx = ExitStack()
    with ctx:
        def sem(name):
            return ctx.enter_context(nc.semaphore(name))

        def keep(name, shape, dt=f32):
            return ctx.enter_context(nc.sbuf_tensor(name, shape, dt))

        x = keep("x", [P, KT, T])
        raw = keep("raw", [P, 2, 2048])
        whi = keep("whi", [P, 2, 2048], f32r)
        wlo = keep("wlo", [P, 2, 2048], f32r)
        cst = keep("cst", [P, CONST_N])
        gains = keep("gains", [P, GAINS * KT])
        negones = keep("negones", [P, P])
        ident_bf = keep("ident_bf", [P, P], bf16)
        causal_bf = keep("causal_bf", [P, P], bf16)
        strict_bf = keep("strict_bf", [P, P], bf16)
        sq = keep("sq", [P, 2, T])
        acc = keep("acc", [P, T])
        diag = keep("diag", [P, TT, P])
        roots = keep("roots", [P, 2, TT])
        eps = keep("eps", [P, 1])
        tmp = keep("tmp", [P, 2, T])
        warm = keep("warm", [P, 4])
        rs, tg, tu = sq, sq, tmp
        pcT = sq[0:NCMP, :, :]

        def C(name):
            at, n = CONST_COLS[name]
            return cst[:, at:at + n]

        ident = C("ident")

        class Region:

            def __enter__(self):
                self.stack = ExitStack()
                self.stack.__enter__()
                return self

            def get(self, name, shape, dt=f32):
                return self.stack.enter_context(nc.sbuf_tensor(name, shape, dt))

            def __exit__(self, *a):
                self.stack.__exit__(*a)

        with Region() as r:
            branch = r.get("branch", [P, KT, T])
        hh = keep("hh", [P, KT, T], f32r)
        hl = keep("hl", [P, KT, T], f32r)
        with Region() as r:
            cosT = r.get("cosT", [P, T])
            sinT = r.get("sinT", [P, T])
            convc = r.get("convc", [P, CONVN])
            peT = r.get("peT", [P, DEPTH * 2, CMPL])
            cb1 = r.get("cb1", [HD, DEPTH * 2])
            with Region() as q:
                a1hi = q.get("a1hi", [P, FT, T], f32r)
                a1lo = q.get("a1lo", [P, FT, T], f32r)
            with Region() as q:
                posi = q.get("posi", [P, T], i32)
                ang = q.get("ang", [P, T])
                trn = q.get("trn", [P, T])
                trr = q.get("trr", [P, T])
                crows = q.get("crows", [88, 4, P])
                perows = q.get("perows", [CMPL, DEPTH * 2, P])
                xin = q.get("xin", [P, TT, D])
                grows = q.get("grows", [GAINS * KT, P])
            with Region() as q:
                onhi = q.get("onhi", [P, 4, T], f32r)
                onlo = q.get("onlo", [P, 4, T], f32r)
                with Region() as n:
                    nqT = n.get("nqT", [P, 4, T])
                    kT = n.get("kT", [P, 4, T])
                    kcT = n.get("kcT", [P, 2, NCMP])
                    vcpad = n.get("vcpad", [NCMP, 2, 3 * HD])
                    vpad = n.get("vpad", [P, 2, TT * 2, 3 * HD])
                    gate = n.get("gate", [P, TT, 24])
                    cs = n.get("cs", [P, 32, NCMP])
                    cstat = n.get("cstat", [P, 3, 32])
                    nstat = n.get("nstat", [P, 4, 64])
                    with Region() as m:
                        kvA = m.get("kvA", [P, 2, T])
                        kvB = m.get("kvB", [P, 2, T])
                        w1 = m.get("w1", [P, 2, CMPL, HD])
                        w2 = m.get("w2", [HD, 2, HD])
                        w2pad = m.get("w2pad", [HD, 3 * HD])
                        hid = m.get("hid", [HD, 2, 2 * NCMP])
                    with Region() as m:
                        nP = m.get("nP", [P, 2, 1280])
                        nPT = m.get("nPT", [P, 2, 1280])
                with Region() as n:
                    n.get("behind_nsa", [P, 2 * FT * T - 16 * T])
                    skT = n.get("skT", [P, 4, T])
                    sqT = n.get("sqT", [P, 4, T])
                oshi = q.get("oshi", [P, 4, T], f32r)
                oslo = q.get("oslo", [P, 4, T], f32r)
                with Region() as n:
                    svp = n.get("svp", [P, 2, TT * 2, 3 * HD])
                    sE = n.get("sE", [P, 1280])
                    sL = n.get("sL", [P, 2, 1280])
                    sW = n.get("sW", [P, 2, 1280])
                with Region() as n:
                    yhi = n.get("yhi", [P, KT, T], f32r)
                    ylo = n.get("ylo", [P, KT, T], f32r)
                    ga = n.get("ga", [P, T])
                    gb = n.get("gb", [P, T])
        with Region() as r:
            with Region() as q:
                a2hi = q.get("a2hi", [P, FT, T], f32r)
                a2lo = q.get("a2lo", [P, FT, T], f32r)
            with Region() as q:
                cst2 = q.get("cst2", [P, CONST2_N])
                zeros_bf = q.get("zeros_bf", [P, T], bf16)
                oahi = q.get("oahi", [P, 4, T], f32r)
                oalo = q.get("oalo", [P, 4, T], f32r)
                with Region() as n:
                    aqT = n.get("aqT", [P, 4, T])
                    akT = n.get("akT", [P, 4, T])
                    avp = n.get("avp", [P, 2, TT * 2, 3 * HD])
                    tab = n.get("tab", [P, 2, 14 * HD])
                    aP = n.get("aP", [P, 2, 2048])
                    aPT = n.get("aPT", [P, 2, 2048])
                    astat = n.get("astat", [P, 3, 32])
                obhi = q.get("obhi", [P, 6, T], f32r)
                oblo = q.get("oblo", [P, 6, T], f32r)
                with Region() as n:
                    bqT = n.get("bqT", [P, 2, T])
                    bkT = n.get("bkT", [P, 2, T])
                    bvp = n.get("bvp", [P, TT * 2, 3 * HD])
                    ob = n.get("ob", [P, 6, T])
                    bstat = n.get("bstat", [P, 3, 48])
                    lse = n.get("lse", [P, 48])
                    with Region() as m:
                        bP = m.get("bP", [P, 2, 1280])
                        bPT = m.get("bPT", [P, 2, 1280])
                    with Region() as m:
                        lseT = m.get("lseT", [4, 3, T])
                        alp = m.get("alp", [4, 3, T])
                        mz = m.get("mz", [4, 2, T])
                with Region() as n:
                    y2hi = n.get("y2hi", [P, KT, T], f32r)
                    y2lo = n.get("y2lo", [P, KT, T], f32r)
                    ga2 = n.get("ga2", [P, T])
                    gb2 = n.get("gb2", [P, T])
        with Region() as r:
            ostage = r.get("ostage", [P, TT, D])

        def C2(name):
            at, n = CONST2_COLS[name]
            return cst2[:, at:at + n]

        bank = [ctx.enter_context(nc.psum_tensor(f"bank{i}", [P, 512], f32)) for i in range(8)]
        RSTD = bank[4]
        SUMS = [bank[5], bank[6], bank[7], bank[4]]
        XSUMS = [bank[5], bank[6], bank[7], bank[3]]

        w_loaded = [sem("w_loaded0"), sem("w_loaded1")]
        hi_ready = sem("hi_ready")
        lo_ready = sem("lo_ready")
        tile_done = sem("tile_done")
        dve_read = sem("dve_read")
        SEMS = {}
        for name in """const_in const2_in start_in table_in pos_in gains_in zeros_set toep_zero toep_filled
            start_x gains_t gains_set tables_t tables_copied ang_ready sin_done tables_ready negones_set
            x_ready sq_done sq_used var_done diag_done sd_done rstd_done h_set hh_ready h_ready
            rs_ready rope_done k_exchanged cmp_in w2_staged kvAB_ready pads_zeroed v_ready v_ready_dve gateT_set gate_t gate_ready
            cmp_hid cmp_act cmp_out cmp_ready cs_done cs_masked cs_exp cs_probs cmp_pv
            sqk_act sqk_dve svp_zeroed z_done l_done L_ready arg_done w_ready spv_done so_hi so_lo
            gates_set y_set y2_hi y_ready
            aff_done conv_done gelu_done act_mul act_hi_done act_ready
            aqk_act aqk_dve avp_zeroed tab_in0 tab_in1 tab_used
            bqk_act bqk_dve bvp_zeroed ob_done ob_copied ln_done lse_ready lseT_done lseT_ready mx_ready aexp_done
            alpha_ready alpha_b alpha_used ob_hi ob_ready out_t out_ca out_cd out_st""".split():
            SEMS[name] = sem(name)
        S = type("Named", (), SEMS)

        class Rows:

            def __init__(self, name, items, keys, width, Pb, PTb, stat, lead=0, group=1, item0=0):
                self.items, self.keys, self.P, self.PT, self.stat = items, keys, Pb, PTb, stat
                self.lead, self.group, self.item0 = lead, group, item0
                self.s_done, self.max_done, self.exp_done, self.p_ready = (
                    sem(name + "_scores"), sem(name + "_max"), sem(name + "_exp"), sem(name + "_scaled"))
                self.t_done = sem(name + "_transposed")
                self.copied = [sem(name + "_copied_act"), sem(name + "_copied_dve")]
                self.pv_done, self.o_hi, self.o_free = sem(name + "_pv"), sem(name + "_ohi"), sem(name + "_ofree")
                self.off, at = [], 0
                for i in range(TT):
                    self.off.append(at)
                    at += (keys(i)[1] - keys(i)[0]) * P
                self.ptoff, at = [], 0
                for j in range(TT):
                    self.ptoff.append(at)
                    at += len(self.queries(j)) * P
                assert at <= width
                self.bias_done = sem(name + "_biased")
                self.fills = lead * (len(items) // group) + TT * len(items)
                self.scores = TT * len(items)

            def queries(self, j):
                return [i for i in range(TT) if self.keys(i)[0] <= j < self.keys(i)[1]]

            def fill(self, n, j):
                return (n // self.group + 1) * self.lead + TT * n + j

        nsa_items = [dict(h=2 * (n // 4) + (n // 2) % 2, b=n % 2) for n in range(16)]
        nsa = Rows("nsa", nsa_items, lambda i: (0, i + 1), 1280, nP, nPT, nstat, lead=2, group=4)
        na = Rows("na", [dict(h=h) for h in range(8)], lambda i: (0, TT), 2048, aP, aPT, astat)
        DIL = [Rows(f"dil{g}", [dict(h=h) for h in range(4)],
                    (lambda i: (max(0, i - 1), min(TT, i + 2))) if g == 0 else (lambda i: (i, i + 1)),
                    1280, bP, bPT, bstat, item0=4 * g) for g in range(3)]

        block = ctx.enter_context(nc.Block())
        w_in, w_in2 = A["w_in"], A["w_in_2"]

        @block.sync
        def _(sp):
            def unit(v, s, parts):
                sp.wait_ge(lo_ready, 2 * v + s + 1)
                for dst, src in parts:
                    sp.dma_start(dst, src).then_inc(w_loaded[s], 16)

            def wide(W, c0, s):
                src = W.rearrange("(k p) c -> p k c", p=P)[:, :, bass.ds(c0, 256)]
                dst = raw[:, s, :].rearrange("p (k c) -> p k c", k=8)
                return [(dst[:, 0:4], src[:, 0:4]), (dst[:, 4:8], src[:, 4:8])]

            def twin(Wa, ca, Wb, cb, s):
                dst = raw[:, s, :].rearrange("p (k t c) -> p k t c", k=8, t=2)
                return [(dst[:, :, i], W.rearrange("(k p) c -> p k c", p=P)[:, :, bass.ds(c, P)])
                        for i, (W, c) in enumerate(((Wa, ca), (Wb, cb)))]

            def half_rows(W, m, half, s):
                src = W[half * FH * P:(half + 1) * FH * P, bass.ds(m * P, P)].rearrange("(k p) c -> p k c", p=P)
                dst = raw[:, s, 0:FH * P].rearrange("p (k c) -> p k c", k=FH)
                return [(dst[:, 0:6], src[:, 0:6]), (dst[:, 6:FH], src[:, 6:FH])]

            def stacked(Wa, ka, Wb, kb, m, s):
                dst = raw[:, s, 0:(ka + kb) * P].rearrange("p (k c) -> p k c", k=ka + kb)
                return [(dst[:, k0:k1], W.rearrange("(k p) c -> p k c", p=P)[:, :, bass.ds(m * P, P)])
                        for W, k0, k1 in ((Wa, 0, ka), (Wb, ka, ka + kb))]

            sp.dma_start(cst[:, :], consts).then_inc(S.const_in, 16)
            for i in range(TT):
                sp.dma_start(xin[:, i, :], A["x"][0, i * P:(i + 1) * P, :]).then_inc(S.start_in, 16)
            sp.dma_start(posi[:, :], A["positions"].broadcast_to([P, T])).then_inc(S.pos_in, 16)
            norms = [("g_pre_mix", 0), ("g_post_mix", 0), ("g_pre_ffn", 0), ("g_post_ffn", 0),
                     ("g_pre_mix", 1), ("g_post_mix", 1), ("g_pre_ffn", 1), ("g_post_ffn", 1),
                     ("ffn1_pre_g_2", 0), ("ffn1_post_g_2", 0), ("mix_pre_g_2", 0), ("mix_post_g_2", 0),
                     ("ffn2_pre_g_2", 0), ("ffn2_post_g_2", 0)]
            for n, (name, l) in enumerate(norms):
                sp.dma_start(grows[n * KT:(n + 1) * KT, :], A[name][l].rearrange("(k p) -> k p", p=P)).then_inc(S.gains_in, 16)

            with sp.Fori(0, DEPTH) as l:
                v0 = l * VL
                W = w_in[l]
                for i in range(2):
                    unit(v0, i, wide(W, 256 * i, i))
                unit(v0 + 1, 0, wide(W, 512, 0))
                unit(v0 + 1, 1, twin(W, 768, W, 1024, 1))
                unit(v0 + 2, 0, twin(W, 896, W, 1152, 0))
                sp.wait_ge(S.x_ready, KT * (2 * l + 1))
                sp.wait_ge(S.tables_ready, 1)
                for kv, name in enumerate(("ck", "cv")):
                    for d in range(2):
                        sp.dma_start(w1[d * HD:(d + 1) * HD, kv], A[name + "_w1"][l].rearrange("(p d) h -> d p h", d=HD)).then_inc(S.cmp_in, 16)
                    sp.dma_start(w2[:, kv, :], A[name + "_w2"][l]).then_inc(S.cmp_in, 16)
                dst = raw[:, 1, :].rearrange("p (k c) -> p k c", k=8)[:, :, 0:24]
                src = W[:, 1280:1304].rearrange("(k p) c -> p k c", p=P)
                unit(v0 + 2, 1, [(dst[:, 0:4], src[:, 0:4]), (dst[:, 4:8], src[:, 4:8])])
                with sp.Fori(0, 3) as i:
                    for s in range(2):
                        unit(v0 + 3 + i, s, wide(W, 1304 + 512 * i + 256 * s, s))
                with sp.Fori(0, KT) as m:
                    unit(v0 + 6 + m, 0, twin(W, 2840 + P * m, W, 2840 + D + P * m, 0))
                    unit(v0 + 6 + m, 1, stacked(A["w_proj_nsa"][l], 4, A["w_proj_sb"][l], 4, m, 1))
                with sp.Fori(0, 2) as i:
                    for s in range(2):
                        unit(v0 + 14 + i, s, wide(A["w_out"][l], 512 * i + 256 * s, s))
                with sp.Fori(0, FH) as i:
                    for s in range(2):
                        unit(v0 + 16 + i, s, twin(A["w_up"][l], (2 * i + s) * P, A["w_up"][l], (2 * i + s) * P + FF, s))
                with sp.Fori(0, KT) as m:
                    for s in range(2):
                        unit(v0 + 27 + m, s, half_rows(A["w_down"][l], m, s, s))

            v2 = DEPTH * VL

            def ffn(v, pre):
                with sp.Fori(0, FH) as i:
                    for s in range(2):
                        unit(v + i, s, twin(A[pre + "_w_gate_2"][0], (2 * i + s) * P, A[pre + "_w_up_2"][0], (2 * i + s) * P, s))
                with sp.Fori(0, KT) as m:
                    for s in range(2):
                        unit(v + FH + m, s, half_rows(A[pre + "_w_down_2"][0], m, s, s))

            ffn(v2, "ffn1")
            sp.wait_ge(tile_done, 2 * (DEPTH * UL + 38))
            sp.dma_start(cst2[:, :], consts2).then_inc(S.const2_in, 16)
            W = w_in2[0]
            with sp.Fori(0, 3) as i:
                for s in range(2):
                    unit(v2 + 19 + i, s, wide(W, 512 * i + 256 * s, s))
            for g in range(3):
                for c in range(3):
                    u = 44 + 3 * g + c
                    unit(v2 + u // 2, u % 2, wide(W, 1536 + 768 * c + 256 * g, u % 2))
            with sp.Fori(0, KT) as m:
                unit(v2 + 26 + m, 1, twin(W, (m + 30) * P, W, (m + 38) * P, 1))
                unit(v2 + 27 + m, 0, stacked(A["w_branch_a_2"][0], 4, A["w_branch_b_2"][0], 6, m, 0))
            unit(v2 + 34, 1, wide(A["w_out_2"][0], 0, 1))
            unit(v2 + 35, 0, wide(A["w_out_2"][0], 256, 0))
            unit(v2 + 35, 1, wide(A["w_out_2"][0], 512, 1))
            unit(v2 + 36, 0, wide(A["w_out_2"][0], 768, 0))
            with sp.Fori(0, FH) as i:
                for s in range(2):
                    unit(v2 + 36 + i + (1 + s) // 2, (1 + s) % 2, twin(A["ffn2_w_gate_2"][0], (2 * i + s) * P, A["ffn2_w_up_2"][0], (2 * i + s) * P, (1 + s) % 2))
            with sp.Fori(0, KT) as m:
                for s in range(2):
                    unit(v2 + 47 + m + (1 + s) // 2, (1 + s) % 2, half_rows(A["ffn2_w_down_2"][0], m, s, (1 + s) % 2))
            for i in range(TT):
                sp.wait_ge(S.out_ca, i + 1)
                sp.wait_ge(S.out_cd, i + 1)
                sp.dma_start(out[0, i * P:(i + 1) * P, :], ostage[:, i, :]).then_inc(S.out_st, 16)
            sp.wait_ge(S.out_st, 16 * TT)

        @block.gpsimd
        def _(pool):
            pool.memset(warm[:, 0:1], 0.0).then_inc(lo_ready, 2)

            def rest(v, s):
                pool.wait_ge(hi_ready, 2 * v + s + 1)
                pool.tensor_tensor(wlo[:, s, :], raw[:, s, :], whi[:, s, :].bitcast(f32), ALU.subtract).then_inc(lo_ready, 1)

            with pool.Fori(0, UNITS // 2) as v:
                for s in range(2):
                    rest(v, s)
            rest(UNITS // 2, 0)

        @block.scalar
        def _(act):
            def upper(v, s, first=False):
                act.wait_ge(w_loaded[s], 32 * (v + 1))
                if not first:
                    act.wait_ge(tile_done, 4 * v + 2 * s - 2)
                act.activation(whi[:, s, :], raw[:, s, :], ACT.Copy).then_inc(hi_ready, 1)

            def tile(v, s, mt):
                act.wait_ge(tile_done, 4 * v + 2 * s + mt + 1)

            def root(n, pre=False):
                if pre:
                    act.wait_ge(S.sq_used, KT * n + KT)
                else:
                    act.wait_ge(S.var_done, n + 1)
                for i in range(TT):
                    o = act.activation(roots[:, 0, i:i + 1], (XSUMS if pre else SUMS)[i][:, 0:1], ACT.Sqrt, bias=eps[:, :], scale=-1.0 / D)
                o.then_inc(S.sd_done, 1)

            def pre_squares(n, m):
                for k in range(KT):
                    act.wait_ge(S.x_ready, KT * m + k + 1)
                    if k >= 2:
                        act.wait_ge(S.sq_used, KT * n + k - 1)
                    act.activation(sq[:, k % 2], x[:, k], ACT.Square).then_inc(S.sq_done, 1)
                root(n, True)

            def pre_upper(m, between=None):
                for k in range(KT):
                    if k == KT // 2 and between is not None:
                        between()
                    act.wait_ge(S.h_set, KT * m + k + 1)
                    act.activation(hh[:, k], tmp[:, k % 2], ACT.Copy).then_inc(S.hh_ready, 1)

            def pre_norm(n, m):
                pre_squares(n, m)
                pre_upper(m)

            def exp_tile(st, n, i, base, from_bank):
                lo, hi = st.keys(i)
                w = (hi - lo) * P
                a = TT * n + i
                col = TT * (n + st.item0) + i
                act.wait_ge(st.max_done, base(st.scores) + a + 1)
                if i == 0 and n >= 2:
                    act.wait_ge(st.t_done, base(st.fills) + st.fill(n - 2, TT - 1) + 1)
                pr = st.P[:, n % 2, st.off[i]:st.off[i] + w]
                act.activation(pr, bank[a % 3][:, 0:w] if from_bank else pr, ACT.Exp,
                               bias=st.stat[:, 0, col:col + 1], accum_out=st.stat[:, 1, col:col + 1]).then_inc(st.exp_done, 1)

            def copy_tile(st, n, j, base):
                f = st.fill(n, j)
                if f % 2:
                    return
                qs = st.queries(j)
                act.wait_ge(st.t_done, base(st.fills) + f + 1)
                if n >= 2:
                    act.wait_ge(st.pv_done, base(len(st.items)) + n - 1)
                act.activation(st.PT[:, n % 2, st.ptoff[j]:st.ptoff[j] + len(qs) * P],
                               bank[4 + f % 2][:, qs[0] * P:(qs[-1] + 1) * P], ACT.Copy).then_inc(st.copied[0], 1)

            def first_exp(st, base, from_bank):
                for i in range(TT):
                    exp_tile(st, 0, i, base, from_bank)

            def steps(st, base, from_bank, output, before=None, after=None):
                N = len(st.items)
                for n in range(-1, N):
                    if before is not None:
                        before(n)
                    for i in range(TT):
                        if n + 2 < N:
                            exp_tile(st, n + 2, i, base, from_bank)
                        if n + 1 < N:
                            copy_tile(st, n + 1, i, base)
                        if i == 0 and n >= 1:
                            output(n - 1)
                    if after is not None:
                        after(n)
                output(N - 1)

            def down(v, s0, n):
                with act.Fori(0, KT // 2) as i:
                    for q in range(2):
                        for half in range(2):
                            vv, s = v + 2 * i + (s0 + 2 * q + half) // 2, (s0 + half) % 2
                            tile(vv, s, 1)
                            if half == 1:
                                act.wait_ge(S.sq_used, KT * n + 2 * i + q - 1)
                                act.activation(sq[:, q], bank[2 * q][:, :], ACT.Square).then_inc(S.sq_done, 1)
                            upper(vv + 1, s)
                root(n)

            def out_proj(v, s0, n):
                for i in range(4):
                    vv, s = v + (s0 + i) // 2, (s0 + i) % 2
                    for mt in range(2):
                        k = 2 * i + mt
                        tile(vv, s, mt)
                        act.wait_ge(S.sq_used, KT * n + k - 1)
                        act.activation(sq[:, k % 2], bank[2 * s + mt][:, :], ACT.Square).then_inc(S.sq_done, 1)
                    upper(vv + 1, s)
                root(n)

            def merge(v, s, yb, gab, yn):
                act.wait_ge(S.y_set, yn + 1)
                tile(v, s, 0)
                act.activation(gab[0][:, :], bank[2 * s][:, :], ACT.Sigmoid)
                tile(v, s, 1)
                upper(v + 1, s)
                act.activation(gab[1][:, :], bank[2 * s + 1][:, :], ACT.Sigmoid).then_inc(S.gates_set, 1)
                upper(v + 1 + s, 1 - s)
                act.wait_ge(S.y_set, yn + 2)
                act.activation(yb, tmp[:, 0], ACT.Copy).then_inc(S.y2_hi, 1)

            for l in range(DEPTH):
                for c, name, k in ((2 * l, "conv_w", 0), (2 * l, "conv_w", 1), (2 * l + 1, "conv_w", 2), (2 * l + 1, "conv_b", None)):
                    src = A[name][l] if k is None else A[name][l, k]
                    r0 = 0 if (k == 0 or k == 2) else 44
                    act.dma_start(crows[r0:r0 + 44, c, :], src.rearrange("(k p) -> k p", p=P)).then_inc(S.table_in, 16)
                for kv, name in enumerate(("ck", "cv")):
                    for d in range(2):
                        act.dma_start(perows[:, 2 * l + kv, d * HD:(d + 1) * HD], A[name + "_pe"][l]).then_inc(S.table_in, 16)
                    act.dma_start(cb1[:, 2 * l + kv:2 * l + kv + 1], A[name + "_b1"][l].rearrange("(p o) -> p o", o=1)).then_inc(S.table_in, 16)
            act.wait_ge(S.zeros_set, 1)
            pre_squares(0, 0)
            upper(0, 0, True)
            pre_upper(0, lambda: upper(0, 1, True))
            act.wait_ge(S.ang_ready, 1)
            act.activation(sinT[:, :], trr[:, :], ACT.Sin).then_inc(S.sin_done, 1)
            act.wait_ge(S.ang_ready, 2)
            act.activation(cosT[:, :], ang[:, :], ACT.Sin).then_inc(S.sin_done, 1)
            act.wait_ge(S.tables_t, 1)
            act.activation(peT[:, :, :], bank[6][:, 0:4 * CMPL].rearrange("p (a c) -> p a c", a=4), ACT.Copy)
            act.activation(convc[:, :], bank[7][:, 0:CONVN], ACT.Copy).then_inc(S.tables_copied, 1)
            act.dma_start(bass.AP(tensor=toep.tensor, offset=0, ap=[[TOEP, 120], [416, 10], [1, 416]]),
                          acc[0:120, 0:416].rearrange("p (o c) -> p o c", o=1).broadcast_to([120, 10, 416])).then_inc(S.toep_zero, 16)
            act.dma_start(bass.AP(tensor=toep.tensor, offset=120 * TOEP, ap=[[TOEP_PAD, 1], [1, TOEP_PAD]]), acc[0:1, 0:TOEP_PAD]).then_inc(S.toep_zero, 16)

            with act.Fori(0, DEPTH) as l:
                v0 = l * VL
                base = lambda c, l=l: l * c
                rope = []

                def turned(v, s, mt, scale):
                    r = len(rope)
                    tile(v, s, mt)
                    if r >= 2:
                        act.wait_ge(S.rope_done, 7 * l + r - 1)
                    for qd in range(4):
                        to = 32 * (qd ^ 1)
                        o = act.activation(rs[to:to + 32, r % 2], bank[2 * s + mt][32 * qd:32 * qd + 32, :], ACT.Copy, scale=scale)
                    o.then_inc(S.rs_ready, 1)
                    rope.append(r)

                for i in range(2):
                    for mt in range(2):
                        turned(v0, i, mt, QSCALE)
                        if mt == 0:
                            upper(v0 + 1, i)
                turned(v0 + 1, 0, 0, 1.0)
                upper(v0 + 2, 0)
                for mt in range(2):
                    turned(v0 + 1, 1, mt, 1.0)
                upper(v0 + 2, 1)

                def v_half(bk, half, copy):
                    for b in range(2):
                        o = copy(vpad[:, b, 4 * half:4 * half + 4, HD:2 * HD].rearrange("p (i g) c -> p i g c", g=2),
                                 bank[bk][:, :].rearrange("p (i b g c) -> p b i g c", i=2, b=2, g=2)[:, b])
                    return o

                tile(v0 + 2, 0, 0)
                act.wait_ge(S.pads_zeroed, l + 1)
                v_half(0, 0, lambda d, s_: act.activation(d, s_, ACT.Copy)).then_inc(S.v_ready, 1)
                upper(v0 + 3, 0)
                tile(v0 + 2, 1, 1)
                act.wait_ge(S.toep_zero, 32)
                act.activation(acc[0:24, :], bank[2][0:24, :], ACT.Sigmoid).then_inc(S.gateT_set, 1)
                upper(v0 + 3, 1)

                def sb_tile(k):
                    c, s = k // 4, (k // 2) % 2
                    if k % 2 == 0:
                        tile(v0 + 3 + c, s, 0)
                        act.activation((sqT, skT)[c][:, 2 * s], bank[3][:, :], ACT.Copy, scale=QSCALE if c == 0 else 1.0).then_inc(S.sqk_act, 1)
                    else:
                        upper(v0 + 4 + c, s)

                act.wait_ge(S.gate_t, l + 1)
                act.activation(gate[:, :, :], bank[2][:, :].rearrange("p (a c) -> p a c", a=TT)[:, :, 0:24], ACT.Copy).then_inc(S.gate_ready, 1)
                sb_tile(0)
                act.wait_ge(S.rope_done, 7 * l + 7)
                for b in range(2):
                    for g in range(2):
                        o = act.activation(kT[(1 - g) * HD:(2 - g) * HD, 2 + b], kT[g * HD:(g + 1) * HD, b], ACT.Copy)
                o.then_inc(S.k_exchanged, 1)
                for kv in range(2):
                    act.wait_ge(S.cmp_hid, 2 * l + 2)
                    for g in range(2):
                        o = act.activation(hid[:, kv, g * NCMP:(g + 1) * NCMP], bank[6 + g][0:HD, kv * 64:kv * 64 + NCMP],
                                           ACT.Gelu_apprx_tanh, bias=cb1[:, bass.ds(2 * l + kv, 1)])
                    o.then_inc(S.cmp_act, 1)
                sb_tile(1)
                act.wait_ge(S.cmp_out, l + 1)
                act.activation(kcT[:, 0], bank[4][:, 0:NCMP], ACT.Copy)
                for g in range(2):
                    act.activation(kcT[(1 - g) * HD:(2 - g) * HD, 1], bank[4][g * HD:(g + 1) * HD, 0:NCMP], ACT.Copy)
                act.wait_ge(S.pads_zeroed, l + 1)
                act.activation(vcpad[:, :, HD:2 * HD], bank[4][0:NCMP, 64:192].rearrange("p (a c) -> p a c", a=2), ACT.Copy).then_inc(S.cmp_ready, 1)
                sb_tile(2)
                sb_tile(3)
                act.wait_ge(S.cs_masked, l + 1)
                act.activation(cs[:, :, :], cs[:, :, :], ACT.Exp).then_inc(S.cs_exp, 1)

                first_exp(nsa, base, True)
                sb_tile(4)
                sb_tile(5)

                def lead_copy(n):
                    t = (n + 1) // 4
                    if (n + 1) % 4 == 0 and t < 4:
                        act.wait_ge(nsa.t_done, nsa.fills * l + 18 * t + 1)
                        if t >= 1:
                            act.wait_ge(S.cmp_pv, 4 * l + t)
                        act.activation(pcT[:, 0], bank[4][0:NCMP, :], ACT.Copy).then_inc(nsa.copied[0], 1)

                def nsa_output(n):
                    if n % 4 == 3:
                        t = n // 4
                        act.wait_ge(nsa.pv_done, 16 * l + n + 1)
                        act.activation(onhi[:, t], bank[6 + t % 2][:, :], ACT.Copy).then_inc(nsa.o_hi, 1)

                steps(nsa, base, True, nsa_output, lead_copy, lambda n: sb_tile(SB_STEPS[n]) if n in SB_STEPS else None)

                for s in range(2):
                    tile(v0 + 5, s, 0)
                    act.wait_ge(S.svp_zeroed, l + 1)
                    for hf in range(2):
                        o = act.activation(svp[:, s, 0:4, 2 * HD * hf:2 * HD * hf + HD],
                                           bank[2 * s][:, :].rearrange("p (a h c) -> p a h c", a=4, h=2)[:, :, hf], ACT.Copy)
                    o.then_inc(S.sqk_act, 1)
                    upper(v0 + 6, s)

                act.preload_act_table_set("natural_log_exp_and_others")

                def sb_soft(h):
                    act.wait_ge(S.z_done, 8 * l + h + 1)
                    if h >= 1:
                        act.wait_ge(S.L_ready, 8 * l + h)
                    for b, (c0, w) in enumerate(((0, 512), (512, 512), (1024, 256))):
                        act.activation(sE[:, c0:c0 + w], bank[3 * (h % 2) + b][:, 0:w], ACT.Abs)
                    act.drain()
                    act.activation(sE[:, :], sE[:, :], ACT.Exp, scale=-1.0)
                    act.drain()
                    act.activation(sE[:, :], sE[:, :], ACT.Ln, bias=1.0).then_inc(S.l_done, 1)

                sb_soft(0)
                for h in range(8):
                    if h + 1 < 8:
                        sb_soft(h + 1)
                    act.wait_ge(S.arg_done, 8 * l + h + 1)
                    if h >= 2:
                        act.wait_ge(S.spv_done, 8 * l + h - 1)
                    for b, (c0, w) in enumerate(((0, 512), (512, 512), (1024, 256))):
                        o = act.activation(sW[:, h % 2, c0:c0 + w], bank[3 * (h % 2) + b][:, 0:w], ACT.Exp)
                    o.then_inc(S.w_ready, 1)
                    if (h % 2 == 0 and h > 0) or h == 7:
                        t = h // 2 - (h < 7)
                        act.wait_ge(S.spv_done, 8 * l + 2 * t + 2)
                        act.activation(oshi[:, t], bank[6 + t % 2][:, :], ACT.Copy).then_inc(S.so_hi, 1)

                with act.Fori(0, KT) as m:
                    merge(v0 + 6 + m, 0, yhi[:, bass.ds(m, 1)].rearrange("p o t -> p (o t)"), (ga, gb), 8 * l + m)

                out_proj(v0 + 14, 0, 4 * l + 1)
                pre_norm(4 * l + 2, 2 * l + 1)

                with act.Fori(0, FH) as i:
                    for s in range(2):
                        v = v0 + 16 + i
                        f = 2 * i + s
                        for mt, dst in ((0, tg), (1, tu)):
                            tile(v, s, mt)
                            if mt == 1:
                                upper(v + 1, s)
                            act.wait_ge(S.act_ready, FT * l + f + 1)
                            at = 176 * l + f + FT * mt
                            act.activation(dst[:, 0], bank[2 * s + mt][:, :], ACT.Identity,
                                           bias=convc[:, bass.ds(at + 132, 1)], scale=convc[:, bass.ds(at + 88, 1)]).then_inc(S.aff_done, 1)
                        act.wait_ge(S.conv_done, 2 * FT * l + 2 * f + 1)
                        act.activation(tg[:, 1], tg[:, 0], ACT.Gelu_apprx_tanh).then_inc(S.gelu_done, 1)
                        act.wait_ge(S.act_mul, FT * l + f + 1)
                        act.activation(a1hi[:, bass.ds(f, 1)].rearrange("p o t -> p (o t)"), tu[:, 1], ACT.Copy).then_inc(S.act_hi_done, 1)
                down(v0 + 27, 0, 4 * l + 3)
                pre_norm(4 * l + 4, 2 * l + 2)

            act.wait_ge(S.toep_zero, 32)
            act.dma_start(bass.AP(tensor=toep.tensor, offset=TOEP_AT - 15, ap=[[TOEP, 120], [65, HD], [1, 31]]),
                          bass.AP(tensor=A["na_rpb_2"].tensor, offset=0, ap=[[31, 120], [0, HD], [1, 31]])).then_inc(S.toep_filled, 16)
            v2 = DEPTH * VL
            zero = lambda c: 0

            def ffn2(u0, n, m, f0):
                if n > 4 * DEPTH:
                    pre_norm(n, m)
                with act.Fori(0, FH) as i:
                    for q in range(2):
                        v, s = v2 + i + (u0 + q) // 2, (u0 + q) % 2
                        f = f0 + 2 * i + q
                        tile(v, s, 0)
                        act.wait_ge(S.act_ready, f + 1)
                        act.activation(tg[:, 0], bank[2 * s][:, :], ACT.Silu).then_inc(S.gelu_done, 1)
                        upper(v + 1, s)
                        act.wait_ge(S.act_mul, f + 1)
                        act.activation(a2hi[:, bass.ds(2 * i + q, 1)].rearrange("p o t -> p (o t)"), tu[:, 1], ACT.Copy).then_inc(S.act_hi_done, 1)

            ffn2(0, 8, 4, DEPTH * FT)
            down(v2 + 11, 0, 9)
            pre_norm(10, 5)
            for c in range(2):
                for s in range(2):
                    tile(v2 + 19 + c, s, 0)
                    act.activation((aqT, akT)[c][:, 2 * s], bank[2 * s][:, :], ACT.Copy, scale=QSCALE if c == 0 else 1.0).then_inc(S.aqk_act, 1)
                    upper(v2 + 20 + c, s)
            for s in range(2):
                tile(v2 + 21, s, 0)
                act.wait_ge(S.avp_zeroed, 1)
                for hf in range(2):
                    o = act.activation(avp[:, s, 0:4, 2 * HD * hf:2 * HD * hf + HD],
                                       bank[2 * s][:, :].rearrange("p (a h c) -> p a h c", a=4, h=2)[:, :, hf], ACT.Copy)
                o.then_inc(S.aqk_act, 1)
                upper(v2 + 22, s)

            def load_table(h):
                for r2 in range(2):
                    src = bass.AP(tensor=toep.tensor, offset=TOEP_AT + (h * 15 + 1 - r2) * TOEP, ap=[[HD, HD], [TOEP, 14], [1, HD]])
                    act.dma_start(tab[r2 * HD:(r2 + 1) * HD, h % 2, :].rearrange("p (u c) -> p u c", u=14), src).then_inc((S.tab_in0, S.tab_in1)[h % 2], 16)

            act.wait_ge(S.toep_filled, 16)
            load_table(0)
            load_table(1)
            first_exp(na, zero, False)

            def next_table(n):
                if n + 3 < 8:
                    act.wait_ge(S.tab_used, n + 2)
                    load_table(n + 3)

            def na_output(n):
                if n % 2 == 1:
                    t = n // 2
                    act.wait_ge(na.pv_done, n + 1)
                    act.activation(oahi[:, t], bank[6 + t % 2][:, :], ACT.Copy).then_inc(na.o_hi, 1)

            steps(na, zero, False, na_output, next_table)

            for g, st in enumerate(DIL):
                dil = ORDER[g]
                for c in range(3):
                    u = 44 + 3 * g + c
                    v, s = v2 + u // 2, u % 2
                    tile(v, s, 0)
                    if c < 2:
                        if g > 0 and c == 0:
                            act.wait_ge(DIL[g - 1].pv_done, 4)
                        act.activation((bqT, bkT)[c][:, 0].rearrange("p (r l) -> p r l", r=dil),
                                       bank[2 * s][:, :].rearrange("p (l r) -> p r l", r=dil), ACT.Copy,
                                       scale=QSCALE if c == 0 else 1.0).then_inc(S.bqk_act, 1)
                    else:
                        act.wait_ge(S.bvp_zeroed, 1)
                        for hf in range(2):
                            o = act.activation(bvp[:, 0:4, 2 * HD * hf:2 * HD * hf + HD],
                                               bank[2 * s][:, :].rearrange("p (a h c) -> p a h c", a=4, h=2)[:, :, hf], ACT.Copy)
                        o.then_inc(S.bqk_act, 1)
                    upper(v + 1, s)
                first_exp(st, zero, False)

                def back_in_order(n, g=g, dil=dil):
                    if n % 2 == 1:
                        act.wait_ge(S.ob_done, 2 * g + n // 2 + 1)
                        act.activation(ob[:, 2 * g + n // 2].rearrange("p (l r) -> p r l", r=dil),
                                       bank[6 + n // 2][:, :].rearrange("p (r l) -> p r l", r=dil), ACT.Copy).then_inc(S.ob_copied, 1)

                steps(st, zero, False, back_in_order)
            act.wait_ge(DIL[2].p_ready, 16)
            act.activation(lse[:, :], bstat[:, 1, :], ACT.Ln).then_inc(S.ln_done, 1)
            act.wait_ge(S.lseT_done, 1)
            for g in range(3):
                dil = ORDER[g]
                o = act.activation(lseT[:, g].rearrange("p (l r) -> p r l", r=dil),
                                   bank[g][0:4, :].rearrange("p (r l) -> p r l", r=dil), ACT.Copy)
            o.then_inc(S.lseT_ready, 1)
            act.wait_ge(S.mx_ready, 1)
            act.activation(alp[:, :, :], alp[:, :, :], ACT.Exp).then_inc(S.aexp_done, 1)
            for t in range(6):
                act.wait_ge(S.alpha_used, t + 1)
                act.activation(obhi[:, t], ob[:, t], ACT.Copy).then_inc(S.ob_hi, 1)

            with act.Fori(0, KT) as m:
                merge(v2 + 26 + m, 1, y2hi[:, bass.ds(m, 1)].rearrange("p o t -> p (o t)"), (ga2, gb2), 8 * DEPTH + m)
            out_proj(v2 + 34, 1, 11)
            ffn2(73, 12, 6, DEPTH * FT + FT)

            last = KT // 2 - 1
            with act.Fori(0, last) as i:
                for q in range(2):
                    for half in range(2):
                        vv, s = v2 + 47 + 2 * i + (1 + 2 * q + half) // 2, (1 + half) % 2
                        tile(vv, s, 1)
                        if half == 1:
                            act.wait_ge(S.sq_used, KT * 13 + 2 * i + q - 1)
                            act.activation(sq[:, q], bank[2 - 2 * q][:, :], ACT.Square).then_inc(S.sq_done, 1)
                        upper(vv + 1, s)
            for q in range(2):
                for half in range(2):
                    vv, s = v2 + 47 + 2 * last + (1 + 2 * q + half) // 2, (1 + half) % 2
                    tile(vv, s, 1)
                    if half == 1:
                        act.wait_ge(S.sq_used, KT * 13 + 2 * last + q - 1)
                        act.activation(sq[:, q], bank[2 - 2 * q][:, :], ACT.Square).then_inc(S.sq_done, 1)
                    if q == 0:
                        upper(vv + 1, s)
            root(13)
            for i in range(TT):
                act.wait_ge(S.out_t, 2 * i + 1)
                act.activation(ostage[:, i, 0:512], bank[(2 * i) % 4][:, :], ACT.Copy).then_inc(S.out_ca, 1)

        @block.vector
        def _(dve):
            def tile(v, s, mt):
                dve.drain()
                dve.wait_ge(tile_done, 4 * v + 2 * s + mt + 1)

            def pre_norm(n, m):
                inverse_root(n)

                def lower(k):
                    dve.wait_ge(S.hh_ready, KT * m + k + 1)
                    dve.tensor_tensor(hl[:, k], tmp[:, k % 2], hh[:, k].bitcast(f32), ALU.subtract).then_inc(S.h_ready, 1)

                for k in range(KT):
                    if k > 0:
                        dve.drain()
                    dve.scalar_tensor_tensor(tmp[:, k % 2], x[:, k], gains[:, bass.ds(KT * n + k, 1)], RSTD[:, :],
                                             ALU.mult, ALU.mult).then_inc(S.h_set, 1)
                    if k >= 1:
                        lower(k - 1)
                lower(KT - 1)

            def inverse_root(n):
                dve.drain()
                dve.wait_ge(S.sd_done, n + 1)
                dve.reciprocal(roots[:, 1], roots[:, 0])
                dve.drain()
                for i in range(TT):
                    dve.tensor_scalar(diag[:, i], ident, roots[:, 1, i:i + 1], -1.0, ALU.mult, ALU.mult).then_inc(S.diag_done, 1)
                dve.wait_ge(S.rstd_done, n + 1)

            def add_square(n, k, slot, first):
                dve.wait_ge(S.sq_done, KT * n + k + 1)
                if first:
                    dve.tensor_copy(acc[:, :], sq[:, slot]).then_inc(S.sq_used, 1)
                else:
                    dve.tensor_tensor(acc[:, :], acc[:, :], sq[:, slot], ALU.add).then_inc(S.sq_used, 1)

            def post_norm(n, scale):
                inverse_root(n)
                for k0 in range(0, KT, 2):
                    for k in (k0, k0 + 1):
                        dve.scalar_tensor_tensor(tmp[:, k % 2], branch[:, k], gains[:, bass.ds(KT * n + k, 1)], RSTD[:, :],
                                                 ALU.mult, ALU.mult)
                    dve.drain()
                    for k in (k0, k0 + 1):
                        dve.scalar_tensor_tensor(x[:, k], tmp[:, k % 2], scale, x[:, k], ALU.mult, ALU.add).then_inc(S.x_ready, 1)
                    dve.drain()

            def down(v, s0, n):
                with dve.Fori(0, KT // 2) as i:
                    for q in range(2):
                        dve.drain().then_inc(dve_read, 1)
                        vv, s = v + 2 * i + (s0 + 2 * q + 1) // 2, (s0 + 1) % 2
                        tile(vv, s, 1)
                        k = 2 * i + q
                        dve.wait_ge(S.sq_done, KT * n + k + 1)
                        dve.tensor_copy(branch[:, bass.ds(k, 1)].rearrange("p o t -> p (o t)"), bank[(2 * s0 + 2 * q) % 4][:, :])
                        dve.tensor_tensor(acc[:, :], acc[:, :], sq[:, q], ALU.add).then_inc(S.sq_used, 1)
                        dve.drain().then_inc(dve_read, 1)

            def out_proj(v, s0, n):
                for i in range(4):
                    vv, s = v + (s0 + i) // 2, (s0 + i) % 2
                    for mt in range(2):
                        k = 2 * i + mt
                        tile(vv, s, mt)
                        add_square(n, k, k % 2, k == 0)
                        o = dve.tensor_copy(branch[:, k], bank[2 * s + mt][:, :])
                        if mt == 1:
                            o.then_inc(dve_read, 1)

            def max_tile(st, n, i, base, table=None, slopes=None):
                lo, hi = st.keys(i)
                w = (hi - lo) * P
                a = TT * n + i
                col = TT * (n + st.item0) + i
                dve.wait_ge(st.s_done, base(st.scores) + a + 1)
                src = bank[a % 3][:, 0:w]
                if table is not None or slopes is not None:
                    if i == 0 and n >= 2:
                        dve.wait_ge(st.t_done, base(st.fills) + st.fill(n - 2, TT - 1) + 1)
                    pr = st.P[:, n % 2, st.off[i]:st.off[i] + w]
                    if table is not None:
                        dve.tensor_tensor(pr, src, table[:, (6 - 2 * i) * HD:(14 - 2 * i) * HD], ALU.add).then_inc(st.bias_done, 1)
                    else:
                        dist = slopes[0][:, (lo - i + 1) * P:(hi - i + 1) * P] if slopes[2] else slopes[0]
                        dve.scalar_tensor_tensor(pr, dist, -slopes[1], src, ALU.mult, ALU.add).then_inc(st.bias_done, 1)
                    dve.drain()
                    src = pr
                dve.tensor_reduce(st.stat[:, 0, col:col + 1], src, AX.X, ALU.max, negate=True).then_inc(st.max_done, 1)

            def row_scale(st, n, base, gates=None):
                dve.drain()
                dve.wait_ge(st.exp_done, base(st.scores) + TT * n + TT)
                c0 = TT * (n + st.item0)
                dve.reciprocal(st.stat[:, 2, c0:c0 + TT], st.stat[:, 1, c0:c0 + TT])
                dve.drain()
                if gates is not None:
                    dve.tensor_tensor(st.stat[:, 2, c0:c0 + TT], st.stat[:, 2, c0:c0 + TT], gates, ALU.mult)
                    dve.drain()
                for i in range(TT):
                    lo, hi = st.keys(i)
                    pr = st.P[:, n % 2, st.off[i]:st.off[i] + (hi - lo) * P]
                    dve.tensor_scalar(pr, pr, st.stat[:, 2, c0 + i:c0 + i + 1], None, ALU.mult).then_inc(st.p_ready, 1)

            def copy_tile(st, n, j, base):
                f = st.fill(n, j)
                if f % 2 == 0:
                    return
                qs = st.queries(j)
                dve.wait_ge(st.t_done, base(st.fills) + f + 1)
                if n >= 2:
                    dve.wait_ge(st.pv_done, base(len(st.items)) + n - 1)
                dve.tensor_copy(st.PT[:, n % 2, st.ptoff[j]:st.ptoff[j] + len(qs) * P],
                                bank[4 + f % 2][:, qs[0] * P:(qs[-1] + 1) * P]).then_inc(st.copied[1], 1)

            def first_max(tile_max):
                for i in range(TT):
                    tile_max(0, i)

            def steps(st, base, tile_max, output=None, gates=lambda n: None, lead=None, after=None):
                N = len(st.items)
                for n in range(-1, N):
                    if n + 1 < N:
                        row_scale(st, n + 1, base, gates(n + 1))
                    if lead is not None:
                        lead(n)
                    for i in range(TT):
                        if n + 2 < N:
                            tile_max(n + 2, i)
                        if n + 1 < N:
                            copy_tile(st, n + 1, i, base)
                        if i == 0 and n >= 1 and output is not None:
                            output(n - 1)
                    if after is not None:
                        after(n)
                if output is not None:
                    output(N - 1)

            def merged(v, s, yn, lo_t):
                gab = (ga, gb) if lo_t is ylo else (ga2, gb2)
                v, s = v + s, 1 - s
                tile(v, s, 0)
                dve.wait_ge(S.gates_set, yn + 1)
                dve.tensor_tensor(tmp[:, 0], bank[2 * s][:, :], gab[0][:, :], ALU.mult).then_inc(dve_read, 1)
                tile(v, s, 1)
                dve.tensor_tensor(tmp[:, 1], bank[2 * s + 1][:, :], gab[1][:, :], ALU.mult).then_inc(dve_read, 1)
                dve.drain()
                dve.tensor_tensor(tmp[:, 0], tmp[:, 0], tmp[:, 1], ALU.add).then_inc(S.y_set, 1)
                dve.wait_ge(S.y2_hi, yn + 1)

            dve.memset(eps[:, :], EPS)
            dve.memset(acc[:, :], 0.0).then_inc(S.zeros_set, 1)
            dve.memset(warm[:, 1:2], 0.0).then_inc(dve_read, 2)
            dve.memset(warm[:, 2:3], 0.0).then_inc(S.y_set, 1)
            dve.memset(warm[:, 3:4], 0.0).then_inc(S.act_ready, 1)
            dve.memset(negones[:, :], -1.0).then_inc(S.negones_set, 1)
            dve.wait_ge(S.const_in, 16)
            dve.tensor_copy(ident_bf[:, :], ident)
            dve.tensor_copy(causal_bf[:, :], C("causal"))
            dve.tensor_copy(strict_bf[:, :], C("strictneg"))
            for k in range(KT):
                dve.wait_ge(S.start_x, k + 1)
                dve.tensor_copy(x[:, k], bank[k % 4][:, :]).then_inc(S.x_ready, 1)
            dve.wait_ge(S.gains_t, 1)
            dve.tensor_copy(gains[:, :], bank[6][:, 0:GAINS * KT]).then_inc(S.gains_set, 1)
            dve.wait_ge(S.pos_in, 16)
            dve.tensor_copy(trr[:, :], posi[:, :])
            dve.drain()
            dve.tensor_scalar(ang[:, :], trr[:, :], C("invfreq"), None, ALU.mult)
            dve.drain()

            def reduced(dst, turn, add):
                dve.tensor_scalar(trn[:, :], ang[:, :], 1.0 / TWO_PI, turn, ALU.mult, ALU.add)
                dve.drain()
                dve.tensor_scalar(trn[:, :], trn[:, :], ROUND, None, ALU.add)
                dve.drain()
                dve.tensor_scalar(trn[:, :], trn[:, :], ROUND, None, ALU.subtract)
                src = ang
                for part in TURN_PARTS:
                    dve.drain()
                    dve.scalar_tensor_tensor(dst[:, :], trn[:, :], -part, src[:, :], ALU.mult, ALU.add)
                    src = dst
                dve.drain()
                if add:
                    dve.tensor_scalar(dst[:, :], dst[:, :], add, None, ALU.add)
                    dve.drain()
                dve.tensor_scalar(dst[:, :], dst[:, :], PI_IN, -PI_IN, ALU.min, ALU.max).then_inc(S.ang_ready, 1)

            reduced(trr, 0.0, 0.0)
            reduced(ang, 0.25, TWO_PI / 4)

            pre_norm(0, 0)
            dve.wait_ge(S.sin_done, 2)
            dve.tensor_scalar(sinT[:, :], sinT[:, :], C("sinsign"), None, ALU.mult)
            dve.wait_ge(S.tables_copied, 1)
            dve.drain().then_inc(S.tables_ready, 1)

            with dve.Fori(0, DEPTH) as l:
                v0 = l * VL
                base = lambda c, l=l: l * c
                dve.memset(vpad[:, :, :, 0:HD], 0.0)
                dve.memset(vpad[:, :, :, 2 * HD:3 * HD], 0.0)
                dve.memset(vcpad[:, :, 0:HD], 0.0)
                dve.memset(vcpad[:, :, 2 * HD:3 * HD], 0.0).then_inc(S.pads_zeroed, 1)
                rope = []

                def roped(v, s, mt, scale, out, last_read):
                    r = len(rope)
                    tile(v, s, mt)
                    dve.wait_ge(S.rs_ready, 7 * l + r + 1)
                    o = dve.scalar_tensor_tensor(tmp[:, 0], bank[2 * s + mt][:, :], scale, cosT[:, :], ALU.mult, ALU.mult)
                    if last_read:
                        o.then_inc(dve_read, 1)
                    dve.tensor_tensor(tmp[:, 1], rs[:, r % 2], sinT[:, :], ALU.mult)
                    dve.drain()
                    dve.tensor_tensor(out, tmp[:, 0], tmp[:, 1], ALU.add).then_inc(S.rope_done, 1)
                    rope.append(r)

                for i in range(2):
                    for mt in range(2):
                        roped(v0, i, mt, QSCALE, nqT[:, 2 * i + mt], mt == 1)
                roped(v0 + 1, 0, 0, 1.0, kvB[:, 0], False)
                dve.drain()
                tile(v0 + 1, 0, 1)

                def with_pe(dst, src, kv, first):
                    pe_row = peT[:, bass.ds(2 * l + kv, 1), first:first + 16].broadcast_to([P, CMPL, 16])
                    return dve.tensor_tensor(dst.rearrange("p (n c) -> p n c", c=16), src.rearrange("p (n c) -> p n c", c=16), pe_row, ALU.add)

                with_pe(kvA[:, 0], kvB[:, 0], 0, 0)
                dve.drain()
                with_pe(kvB[:, 0], kvB[:, 0], 0, 16)
                with_pe(kvA[:, 1], bank[1][:, :], 1, 0)
                with_pe(kvB[:, 1], bank[1][:, :], 1, 16).then_inc(dve_read, 1)
                for mt in range(2):
                    roped(v0 + 1, 1, mt, 1.0, kT[:, mt], mt == 1)
                tile(v0 + 2, 0, 1)
                for b in range(2):
                    o = dve.tensor_copy(vpad[:, b, 4:8, HD:2 * HD].rearrange("p (i g) c -> p i g c", g=2),
                                        bank[1][:, :].rearrange("p (i b g c) -> p b i g c", i=2, b=2, g=2)[:, b])
                o.then_inc(S.v_ready_dve, 1)
                dve.drain().then_inc(dve_read, 1)
                dve.drain().then_inc(dve_read, 1)
                dve.wait_ge(S.cmp_in, 96 * (l + 1))
                dve.memset(w2pad[:, HD:2 * HD], 0.0)
                dve.tensor_copy(w2pad[:, 0:HD], w2[:, 0])
                dve.tensor_copy(w2pad[:, 2 * HD:3 * HD], w2[:, 0])
                dve.drain().then_inc(S.kvAB_ready, 1)

                def sb_tile(k):
                    c, s = k // 4, (k // 2) % 2
                    if k % 2 == 1:
                        tile(v0 + 3 + c, s, 1)
                        dve.tensor_scalar((sqT, skT)[c][:, 2 * s + 1], bank[3][:, :], QSCALE if c == 0 else 1.0, None, ALU.mult).then_inc(S.sqk_dve, 1)
                        dve.drain().then_inc(dve_read, 1)

                sb_tile(1)
                dve.wait_ge(S.cs_done, l + 1)
                madd = C("cmpadd").rearrange("p (o i c) -> p o i c", o=1, i=TT).broadcast_to([P, 4, TT, NCMP])
                mmul = C("cmpmul").rearrange("p (o i c) -> p o i c", o=1, i=TT).broadcast_to([P, 8, TT, NCMP])
                for b in range(2):
                    dve.tensor_tensor(cs[:, :].rearrange("p (t g i) c -> p g t i c", g=2, i=TT)[:, b],
                                      bank[b][:, :].rearrange("p (h i c) -> p h i c", h=4, i=TT)[:, :, :, 0:NCMP], madd, ALU.add)
                dve.drain()
                dve.tensor_reduce(cstat[:, 0], cs[:, :, :], AX.X, ALU.max)
                dve.drain()

                def over(k):
                    return cstat[:, k].rearrange("p (s o) -> p s o", o=1).broadcast_to([P, 32, NCMP])

                dve.tensor_tensor(cs[:, :, :], cs[:, :, :], over(0), ALU.subtract)
                dve.drain().then_inc(S.cs_masked, 1)
                sb_tile(3)

                def nsa_max(n, i):
                    max_tile(nsa, n, i, base)

                first_max(nsa_max)
                dve.wait_ge(S.cs_exp, l + 1)
                dve.tensor_reduce(cstat[:, 1], cs[:, :, :], AX.X, ALU.add)
                dve.drain()
                dve.reciprocal(cstat[:, 2], cstat[:, 1])
                dve.tensor_tensor(cs[:, :, :].rearrange("p (h i) c -> p h i c", i=TT), cs[:, :, :].rearrange("p (h i) c -> p h i c", i=TT), mmul, ALU.mult)
                dve.drain()
                dve.wait_ge(S.gate_ready, l + 1)
                dve.tensor_tensor(cstat[:, 2].rearrange("p (h i) -> p h i", i=TT), cstat[:, 2].rearrange("p (h i) -> p h i", i=TT),
                                  gate[:, :, :].rearrange("p i (h b) -> p h i b", b=3)[:, :, :, 0], ALU.mult)
                dve.drain()
                dve.tensor_tensor(cs[:, :, :], cs[:, :, :], over(2), ALU.mult)
                dve.drain().then_inc(S.cs_probs, 1)
                sb_tile(5)

                def nsa_gate(n):
                    it = nsa.items[n]
                    return gate[:, :, 3 * it["h"] + 1 + it["b"]]

                def lead_copy(n):
                    t = (n + 1) // 4
                    if (n + 1) % 4 == 0 and t < 4:
                        dve.wait_ge(nsa.t_done, nsa.fills * l + 18 * t + 2)
                        if t >= 1:
                            dve.wait_ge(S.cmp_pv, 4 * l + t)
                        dve.tensor_copy(pcT[:, 1], bank[5][0:NCMP, :]).then_inc(nsa.copied[1], 1)

                def nsa_output(n):
                    if n % 4 == 3:
                        t = n // 4
                        dve.wait_ge(nsa.o_hi, 4 * l + t + 1)
                        dve.tensor_tensor(onlo[:, t], bank[6 + t % 2][:, :], onhi[:, t].bitcast(f32), ALU.subtract).then_inc(nsa.o_free, 1)

                steps(nsa, base, nsa_max, nsa_output, nsa_gate, lead_copy, lambda n: sb_tile(SB_STEPS[n]) if n in SB_STEPS else None)

                dve.memset(svp[:, :, :, HD:2 * HD], 0.0).then_inc(S.svp_zeroed, 1)
                for s in range(2):
                    tile(v0 + 5, s, 1)
                    for hf in range(2):
                        o = dve.tensor_copy(svp[:, s, 4:8, 2 * HD * hf:2 * HD * hf + HD],
                                            bank[2 * s + 1][:, :].rearrange("p (a h c) -> p a h c", a=4, h=2)[:, :, hf])
                    o.then_inc(S.sqk_dve, 1)
                    dve.drain().then_inc(dve_read, 1)

                Z = ((0, 512), (512, 512), (1024, 256))

                def sb_softplus(h):
                    dve.drain()
                    dve.wait_ge(S.l_done, 8 * l + h + 1)
                    if h >= 2:
                        dve.wait_ge(S.arg_done, 8 * l + h - 1)
                    for b, (c0, w) in enumerate(Z):
                        dve.scalar_tensor_tensor(sL[:, h % 2, c0:c0 + w], bank[3 * (h % 2) + b][:, 0:w], 0.0, sE[:, c0:c0 + w], ALU.max, ALU.add)
                    dve.drain()
                    for at in (0, 512, 896, 1024):
                        o = dve.tensor_tensor(sL[:, h % 2, at:at + P], sL[:, h % 2, at:at + P], C("strict01"), ALU.mult)
                    o.then_inc(S.L_ready, 1)

                for h in range(8):
                    sb_softplus(h)
                    if h % 2 == 1 and h >= 3:
                        t = h // 2 - 1
                        dve.wait_ge(S.so_hi, 4 * l + t + 1)
                        dve.tensor_tensor(oslo[:, t], bank[6 + t % 2][:, :], oshi[:, t].bitcast(f32), ALU.subtract).then_inc(S.so_lo, 1)
                dve.wait_ge(S.so_hi, 4 * l + 4)
                dve.tensor_tensor(oslo[:, 3], bank[7][:, :], oshi[:, 3].bitcast(f32), ALU.subtract).then_inc(S.so_lo, 1)

                with dve.Fori(0, KT) as m:
                    merged(v0 + 6 + m, 0, 8 * l + m, ylo)
                    dve.tensor_tensor(ylo[:, bass.ds(m, 1)].rearrange("p o t -> p (o t)"), tmp[:, 0],
                                      yhi[:, bass.ds(m, 1)].rearrange("p o t -> p (o t)").bitcast(f32), ALU.subtract).then_inc(S.y_ready, 1)
                dve.wait_ge(S.toep_zero, 32)
                out_proj(v0 + 14, 0, 4 * l + 1)
                post_norm(4 * l + 1, 1.0)
                pre_norm(4 * l + 2, 2 * l + 1)

                with dve.Fori(0, FH) as i:
                    for s in range(2):
                        v = v0 + 16 + i
                        f = 2 * i + s
                        for mt, dst in ((0, tg), (1, tu)):
                            tile(v, s, mt)
                            at = 176 * l + f + FT * mt
                            dve.wait_ge(S.aff_done, 2 * FT * l + 2 * f + mt + 1)
                            ps = bank[2 * s + mt]
                            dve.scalar_tensor_tensor(dst[:, 0, 1:T], ps[:, 0:T - 1], convc[:, bass.ds(at + 44, 1)], dst[:, 0, 1:T], ALU.mult, ALU.add)
                            dve.drain()
                            o = dve.scalar_tensor_tensor(dst[:, 0, 2:T], ps[:, 0:T - 2], convc[:, bass.ds(at, 1)], dst[:, 0, 2:T], ALU.mult, ALU.add)
                            o.then_inc(S.conv_done, 1)
                        dve.drain().then_inc(dve_read, 1)
                        dve.wait_ge(S.gelu_done, FT * l + f + 1)
                        dve.tensor_tensor(tu[:, 1], tg[:, 1], tu[:, 0], ALU.mult).then_inc(S.act_mul, 1)
                        dve.wait_ge(S.act_hi_done, FT * l + f + 1)
                        dve.tensor_tensor(a1lo[:, bass.ds(f, 1)].rearrange("p o t -> p (o t)"), tu[:, 1],
                                          a1hi[:, bass.ds(f, 1)].rearrange("p o t -> p (o t)").bitcast(f32), ALU.subtract).then_inc(S.act_ready, 1)
                dve.memset(acc[:, :], 0.0)
                down(v0 + 27, 0, 4 * l + 3)
                post_norm(4 * l + 3, 1.0)
                pre_norm(4 * l + 4, 2 * l + 2)

            v2 = DEPTH * VL
            zero = lambda c: 0

            def ffn2(u0, n, m, f0):
                if n > 4 * DEPTH:
                    pre_norm(n, m)
                with dve.Fori(0, FH) as i:
                    for q in range(2):
                        v, s = v2 + i + (u0 + q) // 2, (u0 + q) % 2
                        f = f0 + 2 * i + q
                        tile(v, s, 1)
                        dve.wait_ge(S.gelu_done, f + 1)
                        dve.tensor_tensor(tu[:, 1], bank[2 * s + 1][:, :], tg[:, 0], ALU.mult).then_inc(S.act_mul, 1)
                        dve.drain().then_inc(dve_read, 1)
                        dve.wait_ge(S.act_hi_done, f + 1)
                        dve.tensor_tensor(a2lo[:, bass.ds(2 * i + q, 1)].rearrange("p o t -> p (o t)"), tu[:, 1],
                                          a2hi[:, bass.ds(2 * i + q, 1)].rearrange("p o t -> p (o t)").bitcast(f32), ALU.subtract).then_inc(S.act_ready, 1)
                dve.memset(acc[:, :], 0.0)

            ffn2(0, 8, 4, DEPTH * FT)
            down(v2 + 11, 0, 9)
            post_norm(9, 0.5)
            pre_norm(10, 5)

            dve.memset(avp[:, :, :, HD:2 * HD], 0.0).then_inc(S.avp_zeroed, 1)
            for c in range(2):
                for s in range(2):
                    tile(v2 + 19 + c, s, 1)
                    dve.tensor_scalar((aqT, akT)[c][:, 2 * s + 1], bank[2 * s + 1][:, :], QSCALE if c == 0 else 1.0, None, ALU.mult).then_inc(S.aqk_dve, 1)
                    dve.drain().then_inc(dve_read, 1)
            for s in range(2):
                tile(v2 + 21, s, 1)
                for hf in range(2):
                    o = dve.tensor_copy(avp[:, s, 4:8, 2 * HD * hf:2 * HD * hf + HD],
                                        bank[2 * s + 1][:, :].rearrange("p (a h c) -> p a h c", a=4, h=2)[:, :, hf])
                o.then_inc(S.aqk_dve, 1)
                dve.drain().then_inc(dve_read, 1)
            dve.wait_ge(S.const2_in, 16)

            def na_max(n, i):
                tb = tab[:, n % 2]
                if i == 0:
                    dve.wait_ge((S.tab_in0, S.tab_in1)[n % 2], 32 * (n // 2 + 1))
                    tv = tb.rearrange("p (u c) -> p u c", u=14)
                    dve.tensor_tensor(tv, tv, C2("colmask").rearrange("p (o c) -> p o c", o=1).broadcast_to([P, 14, HD]), ALU.add)
                    dve.drain()
                max_tile(na, n, i, zero, table=tb)
                if i == TT - 1:
                    dve.drain().then_inc(S.tab_used, 1)

            def na_output(n):
                if n % 2 == 1:
                    t = n // 2
                    dve.wait_ge(na.o_hi, t + 1)
                    dve.tensor_tensor(oalo[:, t], bank[6 + t % 2][:, :], oahi[:, t].bitcast(f32), ALU.subtract).then_inc(na.o_free, 1)

            first_max(na_max)
            steps(na, zero, na_max, na_output)

            dve.memset(zeros_bf[:, :], 0.0)
            dve.memset(bvp[:, :, HD:2 * HD], 0.0).then_inc(S.bvp_zeroed, 1)
            for g, st in enumerate(DIL):
                dil = ORDER[g]
                for c in range(3):
                    u = 44 + 3 * g + c
                    v, s = v2 + u // 2, u % 2
                    tile(v, s, 1)
                    if c < 2:
                        dve.tensor_scalar((bqT, bkT)[c][:, 1].rearrange("p (r l) -> p r l", r=dil),
                                          bank[2 * s + 1][:, :].rearrange("p (l r) -> p r l", r=dil),
                                          QSCALE if c == 0 else 1.0, None, ALU.mult).then_inc(S.bqk_dve, 1)
                    else:
                        for hf in range(2):
                            o = dve.tensor_copy(bvp[:, 4:8, 2 * HD * hf:2 * HD * hf + HD],
                                                bank[2 * s + 1][:, :].rearrange("p (a h c) -> p a h c", a=4, h=2)[:, :, hf])
                        o.then_inc(S.bqk_dve, 1)
                    dve.drain().then_inc(dve_read, 1)
                dist = C2(f"dist{g}")

                def dil_max(n, i, st=st, g=g, dist=dist):
                    max_tile(st, n, i, zero, slopes=(dist, SLOPES[4 * g + n], g == 0))

                first_max(dil_max)
                steps(st, zero, dil_max)
            dve.wait_ge(S.ln_done, 1)
            dve.tensor_tensor(lse[:, :], lse[:, :], bstat[:, 0, :], ALU.subtract).then_inc(S.lse_ready, 1)
            dve.wait_ge(S.lseT_ready, 1)
            dve.tensor_tensor(mz[:, 0], lseT[:, 0], lseT[:, 1], ALU.max)
            dve.drain()
            dve.tensor_tensor(mz[:, 0], mz[:, 0], lseT[:, 2], ALU.max)
            dve.drain()
            for g in range(3):
                o = dve.tensor_tensor(alp[:, g], lseT[:, g], mz[:, 0], ALU.subtract)
            o.then_inc(S.mx_ready, 1)
            dve.wait_ge(S.aexp_done, 1)
            dve.tensor_tensor(mz[:, 1], alp[:, 0], alp[:, 1], ALU.add)
            dve.drain()
            dve.tensor_tensor(mz[:, 1], mz[:, 1], alp[:, 2], ALU.add)
            dve.drain()
            dve.reciprocal(mz[:, 0], mz[:, 1])
            dve.drain()
            for g in range(3):
                o = dve.tensor_tensor(alp[:, g], alp[:, g], mz[:, 0], ALU.mult)
            o.then_inc(S.alpha_ready, 1)
            dve.wait_ge(S.ob_copied, 6)
            for t in range(6):
                dve.wait_ge(S.alpha_b, t + 1)
                dve.tensor_tensor(ob[:, t], ob[:, t], bank[t % 2][:, :], ALU.mult).then_inc(S.alpha_used, 1)
                dve.wait_ge(S.ob_hi, t + 1)
                dve.tensor_tensor(oblo[:, t], ob[:, t], obhi[:, t].bitcast(f32), ALU.subtract).then_inc(S.ob_ready, 1)

            with dve.Fori(0, KT) as m:
                merged(v2 + 26 + m, 1, 8 * DEPTH + m, y2lo)
                dve.tensor_tensor(y2lo[:, bass.ds(m, 1)].rearrange("p o t -> p (o t)"), tmp[:, 0],
                                  y2hi[:, bass.ds(m, 1)].rearrange("p o t -> p (o t)").bitcast(f32), ALU.subtract).then_inc(S.y_ready, 1)
            out_proj(v2 + 34, 1, 11)
            post_norm(11, 1.0)
            ffn2(73, 12, 6, DEPTH * FT + FT)
            down(v2 + 47, 1, 13)
            post_norm(13, 0.5)
            for i in range(TT):
                dve.wait_ge(S.out_t, 2 * i + 2)
                dve.tensor_copy(ostage[:, i, 512:1024], bank[(2 * i + 1) % 4][:, :]).then_inc(S.out_cd, 1)

        @block.tensor
        def _(pe):
            wh = [whi[:, s, :] for s in range(2)]
            wl = [wlo[:, s, :] for s in range(2)]

            def opened(v, s):
                pe.wait_ge(lo_ready, 2 * v + s + 3)
                pe.wait_ge(dve_read, 2 * v + s + 1)

            def three(out, wt, inp, start, stop, swap=False):
                for a, b, first, last in ((0, 0, True, False), (0, 1, False, False), (1, 0, False, True)):
                    l, r = (inp[a], wt[b]) if swap else (wt[a], inp[b])
                    o = pe.matmul(out, l, r, start=start and first, stop=stop and last)
                return o

            def cols(s, pattern, k, c0, n, **sizes):
                return [w[s].rearrange("p (k c) -> p k c", k=pattern)[:, k, c0:c0 + n] for w in (wh, wl)]

            def dense(v, s, inp, nk, width, tiles, ready=None):
                opened(v, s)
                if ready is not None:
                    for j, (k, ki) in enumerate(tiles[0][1]):
                        ready(ki)
                        for b, _, c0 in tiles:
                            wt = [w[s][:, k * width + c0:k * width + c0 + P] for w in (wh, wl)]
                            o = three(bank[b][:, :], wt, [inp[0][:, ki], inp[1][:, ki]], j == 0, j == nk - 1)
                            if j == nk - 1:
                                o.then_inc(tile_done, 1)
                    return
                for b, ks, c0 in tiles:
                    for j, (k, ki) in enumerate(ks):
                        wt = [w[s][:, k * width + c0:k * width + c0 + P] for w in (wh, wl)]
                        o = three(bank[b][:, :], wt, [inp[0][:, ki], inp[1][:, ki]], j == 0, j == len(ks) - 1)
                    o.then_inc(tile_done, 1)

            H = (hh, hl)

            def two_tiles(v, s, inp=H, ready=None):
                ks = [(k, k) for k in range(KT)]
                dense(v, s, inp, KT, 256, [(2 * s, ks, 0), (2 * s + 1, ks, P)], ready)

            def tokens_major(v, s, n, c0, outs, order=None):
                for i in range(TT):
                    b, at = outs(i)
                    for k in range(KT):
                        inp = [(t[:, k, i * P:(i + 1) * P] if order is None else order(t, k, i)) for t in H]
                        wt = [w[s][:, k * 256 + c0:k * 256 + c0 + n] for w in (wh, wl)]
                        o = three(bank[b][:, at:at + n], wt, inp, k == 0, k == KT - 1, swap=True)
                    yield i, o

            def v_tiles(v, s, order=None):
                opened(v, s)
                for i, o in tokens_major(v, s, 256, 0, lambda i: (2 * s + i // 2, (i % 2) * 256), order):
                    if i % 2 == 1:
                        o.then_inc(tile_done, 1)

            def spread(n):
                for i in range(TT):
                    pe.wait_ge(S.diag_done, TT * n + i + 1)
                    o = pe.matmul(RSTD[:, i * P:(i + 1) * P], negones[:, :], diag[:, i], start=True, stop=True)
                o.then_inc(S.rstd_done, 1)

            def variance(n):
                pe.wait_ge(S.sq_used, KT * n + KT)
                for i in range(TT):
                    o = pe.matmul(SUMS[i][:, 0:1], acc[:, i * P:(i + 1) * P], negones[:, 0:1], start=True, stop=True)
                o.then_inc(S.var_done, 2)
                spread(n)

            def variance_of_x(n):
                for k in range(KT):
                    pe.wait_ge(S.sq_done, KT * n + k + 1)
                    for i in range(TT):
                        o = pe.matmul(XSUMS[i][:, 0:1], sq[:, k % 2, i * P:(i + 1) * P], negones[:, 0:1], start=k == 0, stop=k == KT - 1)
                    o.then_inc(S.sq_used, 1)
                spread(n)

            def h_tiles(m):
                return lambda k: pe.wait_ge(S.h_ready, KT * m + k + 1)

            def down(v, s0, hi_t, lo_t, hidden):
                with pe.Fori(0, KT // 2) as i:
                    for q in range(2):
                        for half in range(2):
                            pe.wait_ge(S.act_ready, hidden + 1 - (1 - half) * FH)
                            vv, s = v + 2 * i + (s0 + 2 * q + half) // 2, (s0 + half) % 2
                            opened(vv, s)
                            b = (2 * s0 + 2 * q) % 4
                            for j in range(FH):
                                wt = [w[s][:, j * P:(j + 1) * P] for w in (wh, wl)]
                                kk = half * FH + j
                                o = three(bank[b][:, :], wt, [hi_t[:, kk], lo_t[:, kk]], kk == 0, kk == FT - 1)
                                if j >= FH - 2:
                                    o.then_inc(tile_done, 1)

            def score_tile(st, n, i, base, q, k, causal):
                lo, hi = st.keys(i)
                w = (hi - lo) * P
                a = TT * n + i
                if a >= 3:
                    pe.wait_ge(st.exp_done if causal else st.bias_done, base(st.scores) + a - 2)
                if not causal:
                    o = pe.matmul(bank[a % 3][:, 0:w], q(i), k(lo * P, hi * P), start=True, stop=True)
                else:
                    if i > 0:
                        pe.matmul(bank[a % 3][:, 0:i * P], q(i), k(0, i * P), start=True, stop=True)
                    pe.matmul(bank[a % 3][:, i * P:w], q(i), k(i * P, w), start=True, stop=False)
                    o = pe.matmul(bank[a % 3][:, i * P:w], ident_bf[:, :], causal_bf[:, :], start=False, stop=True)
                o.then_inc(st.s_done, 1)

            def free_fill(st, base, f):
                if f >= 2:
                    pe.wait_ge(st.copied[f % 2], base(st.fills // 2) + f // 2)

            def transpose_tile(st, n, j, base):
                f = st.fill(n, j)
                free_fill(st, base, f)
                qs = st.queries(j)
                pe.wait_ge(st.p_ready, base(st.scores) + TT * n + qs[-1] + 1)
                for i in qs:
                    at = st.off[i] + (j - st.keys(i)[0]) * P
                    o = pe.transpose(bank[4 + f % 2][:, i * P:(i + 1) * P], st.P[:, n % 2, at:at + P], ident)
                o.then_inc(st.t_done, 1)

            def v_tile(st, n, j, base, vt, obank, start, stop):
                f = st.fill(n, j)
                qs = st.queries(j)
                pe.wait_ge(st.copied[f % 2], base(st.fills // 2) + f // 2 + 1)
                w = len(qs) * P
                return pe.matmul(bank[obank][:, qs[0] * P:qs[0] * P + w], vt(j), st.PT[:, n % 2, st.ptoff[j]:st.ptoff[j] + w],
                                 start=start, stop=stop)

            def steps(st, base, score, v_of, obank, opens, closes, before=None, after=None):
                N = len(st.items)
                for n in range(-1, N):
                    if before is not None:
                        before(n)
                    shut = n >= 0 and closes(n)
                    for i in range(TT):
                        if n + 2 < N:
                            score(n + 2, i)
                        if n >= 0:
                            j = (i + 1) % TT if shut else i
                            o = v_tile(st, n, j, base, v_of(n), obank(n), opens(n) and i == 0, shut and i == TT - 1)
                            if i == TT - 1:
                                o.then_inc(st.pv_done, 1)
                        if n + 1 < N:
                            transpose_tile(st, n + 1, i, base)
                    if after is not None:
                        after(n)

            def add_zeros(b, start):
                return pe.matmul(bank[b][:, :], zeros_bf[:, 0:P], zeros_bf[:, :], start=start, stop=not start)

            pe.wait_ge(S.const_in, 16)
            pe.wait_ge(S.start_in, 16 * TT)
            for k in range(KT):
                if k >= 4:
                    pe.wait_ge(S.x_ready, k - 3)
                for i in range(TT):
                    o = pe.transpose(bank[k % 4][:, i * P:(i + 1) * P], xin[:, i, k * P:(k + 1) * P], ident)
                o.then_inc(S.start_x, 1)
            pe.wait_ge(S.gains_in, 16 * GAINS)
            pe.transpose(bank[6][:, 0:GAINS * KT], grows[:, :], ident[0:GAINS * KT, 0:GAINS * KT]).then_inc(S.gains_t, 1)
            pe.wait_ge(S.gains_set, 1)
            pe.wait_ge(S.negones_set, 1)
            variance_of_x(0)
            pe.wait_ge(S.table_in, 16 * TABLE_DMAS)
            for a in range(2 * DEPTH):
                pe.transpose(bank[6][:, a * CMPL:(a + 1) * CMPL], perows[:, a, :], ident[0:CMPL, 0:CMPL])
            for c in range(4):
                o = pe.transpose(bank[7][:, 88 * c:88 * (c + 1)], crows[:, c, :], ident[0:88, 0:88])
            o.then_inc(S.tables_t, 1)
            with pe.Fori(0, DEPTH) as l:
                v0 = l * VL
                base = lambda c, l=l: l * c
                for i in range(2):
                    two_tiles(v0, i, H, h_tiles(2 * l) if i == 0 else None)
                two_tiles(v0 + 1, 0)
                two_tiles(v0 + 1, 1)
                v_tiles(v0 + 2, 0)
                opened(v0 + 2, 1)
                for k in range(KT):
                    wt = [w[1][:, k * 256:k * 256 + 24] for w in (wh, wl)]
                    o = three(bank[2][0:24, :], wt, [hh[:, k], hl[:, k]], k == 0, k == KT - 1)
                o.then_inc(tile_done, 2)

                def sb_tile(k):
                    c, s, mt = k // 4, (k // 2) % 2, k % 2
                    if mt == 1:

                        pe.wait_ge(S.sqk_act, 6 * l + k // 2 + 1)
                    elif k > 0:
                        pe.wait_ge(S.sqk_dve, 6 * l + k // 2)
                    if mt == 0:
                        opened(v0 + 3 + c, s)
                    for j in range(KT):
                        wt = [w[s][:, j * 256 + mt * P:j * 256 + (mt + 1) * P] for w in (wh, wl)]
                        o = three(bank[3][:, :], wt, [hh[:, j], hl[:, j]], j == 0, j == KT - 1)
                    o.then_inc(tile_done, 1)

                pe.wait_ge(S.kvAB_ready, l + 1)
                sb_tile(0)
                pe.wait_ge(S.gateT_set, l + 1)
                for i in range(TT):
                    o = pe.transpose(bank[2][:, i * P:(i + 1) * P], acc[:, i * P:(i + 1) * P], ident)
                o.then_inc(S.gate_t, 1)
                for kv in range(2):
                    for g in range(2):
                        rows = slice(g * HD, (g + 1) * HD)
                        for p in range(CMPL):
                            src = (kvA if p < 16 else kvB)[rows, kv].rearrange("p (n c) -> p n c", c=16)
                            src = src[:, 0:NCMP, p] if p < 16 else src[:, 1:NCMP + 1, p - 16]
                            o = pe.matmul(bank[6 + g][0:HD, kv * 64:kv * 64 + NCMP], w1[rows, kv, p, :], src,
                                          start=p == 0, stop=p == CMPL - 1)
                    o.then_inc(S.cmp_hid, 1)
                sb_tile(1)
                pe.wait_ge(S.cmp_act, 2 * l + 2)
                for g in range(2):
                    pe.matmul(bank[4][:, 0:NCMP], w2pad[:, g * HD:g * HD + P], hid[:, 0, g * NCMP:(g + 1) * NCMP], start=g == 0, stop=g == 1)
                for g in range(2):
                    o = pe.matmul(bank[4][0:NCMP, 64 + g * HD:128 + g * HD], hid[:, 1, g * NCMP:(g + 1) * NCMP], w2[:, 1, :], start=True, stop=True)
                o.then_inc(S.cmp_out, 1)

                def nsa_q(h, i):
                    return nqT[(h % 2) * HD:(h % 2 + 1) * HD, h // 2, i * P:(i + 1) * P]

                sb_tile(2)
                pe.wait_ge(S.cmp_ready, l + 1)
                pe.wait_ge(dve_read, UL * l + 8)
                pe.wait_ge(S.k_exchanged, l + 1)
                for h in range(8):
                    rows = slice((h % 2) * HD, (h % 2 + 1) * HD)
                    for i in range(TT):
                        at = ((h // 2) * TT + i) * 32
                        o = pe.matmul(bank[h % 2][:, at:at + NCMP], nsa_q(h, i), kcT[rows, int(h % 2 != h // 4)], start=True, stop=True)
                o.then_inc(S.cs_done, 1)
                sb_tile(3)
                pe.wait_ge(S.cs_masked, l + 1)

                def nsa_score(n, i):
                    it = nsa.items[n]
                    g = it["h"] // 4
                    hf = it["h"] % 2
                    keys = kT[hf * HD:(hf + 1) * HD, it["b"] + (2 if hf != g else 0)]
                    score_tile(nsa, n, i, base, lambda i: nsa_q(it["h"], i), lambda a, b: keys[:, a:b], True)

                def nsa_v(n):
                    it = nsa.items[n]
                    hf, g = it["h"] % 2, it["h"] // 4
                    return lambda j: vpad[:, it["b"], 2 * j + g, (1 - hf) * HD:(1 - hf) * HD + P]

                def compressed(n):
                    t = (n + 1) // 4
                    if (n + 1) % 4 == 0 and t < 4:
                        for hf in range(2):
                            f = 18 * t + hf
                            free_fill(nsa, base, f)
                            for i in range(TT):
                                o = pe.transpose(bank[4 + f % 2][0:NCMP, i * P:(i + 1) * P], cs[:, (2 * t + hf) * TT + i, :], ident)
                            o.then_inc(nsa.t_done, 1)
                    if n % 4 == 0:
                        t = n // 4
                        if t >= 2:
                            pe.wait_ge(nsa.o_free, 4 * l + t - 1)
                        for hf in range(2):
                            f = 18 * t + hf
                            pe.wait_ge(nsa.copied[hf], 36 * l + f // 2 + 1)
                            o = pe.matmul(bank[6 + t % 2][:, :], vcpad[:, t // 2, (1 - hf) * HD:(1 - hf) * HD + P], pcT[:, hf], start=hf == 0, stop=False)
                        o.then_inc(S.cmp_pv, 1)

                for i in range(TT):
                    nsa_score(0, i)
                sb_tile(4)
                sb_tile(5)
                pe.wait_ge(S.cs_probs, l + 1)
                pe.wait_ge(S.v_ready, l + 1)
                pe.wait_ge(S.v_ready_dve, l + 1)
                steps(nsa, base, nsa_score, nsa_v, lambda n: 6 + (n // 4) % 2, lambda n: False, lambda n: n % 4 == 3,
                      compressed, lambda n: sb_tile(SB_STEPS[n]) if n in SB_STEPS else None)

                for s in range(2):
                    v_tiles(v0 + 5, s)
                pe.wait_ge(S.sqk_act, 6 * l + 6)
                pe.wait_ge(S.sqk_dve, 6 * l + 6)
                pe.wait_ge(nsa.o_free, 4 * l + 4)
                ZAT = {0: (0, 0, 0), 1: (1, 0, 512), 3: (1, 384, 896), 2: (2, 0, 1024)}

                def z_tile(h, j, stop):
                    rows, t = slice((h % 2) * HD, (h % 2 + 1) * HD), h // 2
                    b, c0, _ = ZAT[j]
                    return pe.matmul(bank[3 * (h % 2) + b][:, c0:c0 + T - j * P], skT[rows, t, j * P:(j + 1) * P],
                                     sqT[rows, t, j * P:T], start=True, stop=stop)

                def z_scores(h):
                    if h >= 2:
                        pe.wait_ge(S.w_ready, 8 * l + h - 1)
                    for j in (0, 1, 3, 2):
                        o = z_tile(h, j, True)
                    o.then_inc(S.z_done, 1)

                def z_minus_sums(h):
                    pe.wait_ge(S.L_ready, 8 * l + h + 1)
                    L = sL[:, h % 2]
                    for j in (0, 1, 3, 2):
                        b, c0, a0 = ZAT[j]
                        zb = bank[3 * (h % 2) + b]
                        w = T - j * P
                        z_tile(h, j, False)
                        pe.matmul(zb[:, c0:c0 + P], ident_bf[:, :], strict_bf[:, :], start=False, stop=False)
                        for j2 in range(j + 1, TT):
                            _, _, a2 = ZAT[j2]
                            w2_ = T - j2 * P
                            pe.matmul(zb[:, c0 + w - w2_:c0 + w], negones[:, :], L[:, a2:a2 + w2_], start=False, stop=False)
                        o = pe.matmul(zb[:, c0:c0 + w], C("negtri"), L[:, a0:a0 + w], start=False, stop=True)
                    o.then_inc(S.arg_done, 1)

                z_scores(0)
                for step in range(9):
                    if step + 1 < 8:
                        z_scores(step + 1)
                    if step < 8:
                        z_minus_sums(step)
                    if step == 0:
                        continue
                    h = step - 1
                    t, hf = h // 2, h % 2
                    if hf == 0 and t >= 2:
                        pe.wait_ge(S.so_lo, 4 * l + t - 1)
                    pe.wait_ge(S.w_ready, 8 * l + h + 1)
                    for j in (1, 2, 3, 0) if hf else (0, 1, 2, 3):
                        a0 = ZAT[j][2]
                        o = pe.matmul(bank[6 + t % 2][:, j * P:T], svp[:, t // 2, 2 * j + t % 2, hf * HD:hf * HD + P],
                                      sW[:, hf, a0:a0 + T - j * P], start=hf == 0 and j == 0, stop=hf == 1 and j == 0)
                    o.then_inc(S.spv_done, 1)

                with pe.Fori(0, KT) as m:
                    pe.wait_ge(S.w_ready, 8 * l + 8)
                    two_tiles(v0 + 6 + m, 0)
                    pe.wait_ge(S.so_lo, 4 * l + 4)
                    opened(v0 + 6 + m, 1)
                    for b, src in enumerate(((onhi, onlo), (oshi, oslo))):
                        for k in range(4):
                            wt = [w[1][:, (4 * b + k) * P:(4 * b + k + 1) * P] for w in (wh, wl)]
                            o = three(bank[2 + b][:, :], wt, [src[0][:, k], src[1][:, k]], k == 0, k == 3)
                        o.then_inc(tile_done, 1)
                for i in range(4):
                    two_tiles(v0 + 14 + i // 2, i % 2, (yhi, ylo), (lambda k: pe.wait_ge(S.y_ready, 8 * l + k + 1)) if i == 0 else None)
                variance(4 * l + 1)
                variance_of_x(4 * l + 2)
                with pe.Fori(0, FH) as i:
                    for s in range(2):
                        two_tiles(v0 + 16 + i, s, H, h_tiles(2 * l + 1) if s == 0 else None)
                down(v0 + 27, 0, a1hi, a1lo, FT * (l + 1))
                variance(4 * l + 3)
                variance_of_x(4 * l + 4)

            v2 = DEPTH * VL
            zero = lambda c: 0

            def ffn2_up(u0, n, m):
                if n > 4 * DEPTH:
                    variance_of_x(n)
                with pe.Fori(0, FH) as i:
                    for q in range(2):
                        two_tiles(v2 + i + (u0 + q) // 2, (u0 + q) % 2, H, h_tiles(m) if q == 0 else None)

            ffn2_up(0, 8, 4)
            down(v2 + 11, 0, a2hi, a2lo, FT * (DEPTH + 1))
            variance(9)
            variance_of_x(10)
            for c in range(2):
                for s in range(2):
                    two_tiles(v2 + 19 + c, s, H, h_tiles(5) if c == 0 and s == 0 else None)
            for s in range(2):
                v_tiles(v2 + 21, s)
            pe.wait_ge(S.aqk_act, 6)
            pe.wait_ge(S.aqk_dve, 6)

            def na_score(n, i):
                rows, t = slice((n % 2) * HD, (n % 2 + 1) * HD), n // 2
                score_tile(na, n, i, zero, lambda i: aqT[rows, t, i * P:(i + 1) * P], lambda a, b: akT[rows, t, a:b], False)

            def na_v(n):
                t, hf = n // 2, n % 2
                return lambda j: avp[:, t // 2, 2 * j + t % 2, hf * HD:hf * HD + P]

            def na_bank(n):
                if n >= 4 and n % 2 == 0:
                    pe.wait_ge(na.o_free, n // 2 - 1)

            for i in range(TT):
                na_score(0, i)
            steps(na, zero, na_score, na_v, lambda n: 6 + (n // 2) % 2, lambda n: n % 2 == 0, lambda n: n % 2 == 1, na_bank)

            for g, st in enumerate(DIL):
                if g == 0:
                    pe.wait_ge(na.o_free, 4)
                else:
                    pe.wait_ge(S.ob_copied, 2 * g)
                    pe.wait_ge(DIL[g - 1].bias_done, 16)
                dil = ORDER[g]

                def place(t, k, i):
                    if dil == 1:
                        return t[:, k, i * P:(i + 1) * P]
                    by = t[:, k].rearrange("p (l r) -> p r l", r=dil)
                    return by[:, i * dil // TT:(i + 1) * dil // TT, :]

                for c in range(3):
                    u = 44 + 3 * g + c
                    v, s = v2 + u // 2, u % 2
                    if c < 2:
                        two_tiles(v, s)
                    else:
                        v_tiles(v, s, place)
                pe.wait_ge(S.bqk_act, 3 * g + 3)
                pe.wait_ge(S.bqk_dve, 3 * g + 3)

                def dil_score(n, i, st=st):
                    rows, t = slice((n % 2) * HD, (n % 2 + 1) * HD), n // 2
                    score_tile(st, n, i, zero, lambda i: bqT[rows, t, i * P:(i + 1) * P], lambda a, b: bkT[rows, t, a:b], False)

                def dil_v(n):
                    t, hf = n // 2, n % 2
                    return lambda j: bvp[:, 2 * j + t, hf * HD:hf * HD + P]

                def dil_open(n):
                    if n >= 0 and n % 2 == 0:
                        add_zeros(6 + n // 2, True)

                def dil_close(n):
                    if n >= 0 and n % 2 == 1:
                        add_zeros(6 + n // 2, False).then_inc(S.ob_done, 1)

                for i in range(TT):
                    dil_score(0, i)
                steps(st, zero, dil_score, dil_v, lambda n: 6 + n // 2, lambda n: False, lambda n: False, dil_open, dil_close)
            pe.wait_ge(S.lse_ready, 1)
            for g in range(3):
                for i in range(TT):
                    o = pe.transpose(bank[g][0:4, i * P:(i + 1) * P],
                                     lse[:, 16 * g:16 * g + 16].rearrange("p (h i) -> p i h", i=TT)[:, i], ident)
            o.then_inc(S.lseT_done, 1)
            pe.wait_ge(S.lseT_ready, 1)
            two_tiles(v2 + 26, 1)
            pe.wait_ge(S.alpha_ready, 1)
            for t in range(6):
                if t >= 2:
                    pe.wait_ge(S.alpha_used, t - 1)
                pe.matmul(bank[t % 2][:, :], C2("sel")[0:4, (t % 2) * P:(t % 2 + 1) * P], alp[:, t // 2], start=True, stop=True).then_inc(S.alpha_b, 1)
            pe.wait_ge(S.ob_ready, 6)

            def branches(v):
                opened(v, 0)
                at = 0
                for b, (src, nk) in enumerate((((oahi, oalo), 4), ((obhi, oblo), 6))):
                    for k in range(nk):
                        wt = [w[0][:, (at + k) * P:(at + k + 1) * P] for w in (wh, wl)]
                        o = three(bank[b][:, :], wt, [src[0][:, k], src[1][:, k]], k == 0, k == nk - 1)
                    at += nk
                    o.then_inc(tile_done, 1)

            with pe.Fori(0, KT - 1) as m:
                branches(v2 + 27 + m)
                two_tiles(v2 + 27 + m, 1)
            branches(v2 + 34)
            for i in range(4):
                two_tiles(v2 + 34 + (1 + i) // 2, (1 + i) % 2, (y2hi, y2lo), (lambda k: pe.wait_ge(S.y_ready, 8 * DEPTH + k + 1)) if i == 0 else None)
            variance(11)
            ffn2_up(73, 12, 6)
            down(v2 + 47, 1, a2hi, a2lo, FT * (DEPTH + 2))
            variance(13)
            for i in range(TT):
                for b in range(2):
                    if i >= 2:
                        pe.wait_ge((S.out_ca, S.out_cd)[b], i - 1)
                    for k in range(4):
                        kk = 4 * b + k
                        if i == 0:
                            pe.wait_ge(S.x_ready, KT * 7 + kk + 1)
                        o = pe.transpose(bank[(2 * i + b) % 4][:, k * P:(k + 1) * P], x[:, kk, i * P:(i + 1) * P], ident)
                    o.then_inc(S.out_t, 1)


def kernel(**inputs):
    import concourse.bacc as bacc
    from concourse.bass_utils import run_bass_kernel_spmd

    nc = bacc.Bacc("TRN2", target_bir_lowering=False, num_devices=1)
    arrays, args = {}, {}
    for name, a in inputs.items():
        arrays[f"in_{name}"] = np.ascontiguousarray(a)
        args[name] = nc.dram_tensor(f"in_{name}", arrays[f"in_{name}"].shape, mybir.dt.from_np(arrays[f"in_{name}"].dtype), kind="ExternalInput").ap()
    arrays["shape_consts"], arrays["shape_consts2"] = shape_constants()
    consts = [nc.dram_tensor(n, arrays[n].shape, mybir.dt.float32, kind="ExternalInput").ap() for n in ("shape_consts", "shape_consts2")]
    toep = nc.dram_tensor("toeplitz_tables", (120 * TOEP + TOEP_PAD,), mybir.dt.float32, kind="Internal").ap()
    out = nc.dram_tensor("out_0", (1, T, D), mybir.dt.float32, kind="ExternalOutput").ap()
    build(nc, args, *consts, toep, out)
    return run_bass_kernel_spmd(nc, [arrays], core_ids=[0]).results[0]["out_0"]
```
